# Optimizing a Trainium2 kernel written in Bass

```python
import jax, jax.numpy as jnp
from jax import lax
import numpy as np

D_MODEL = 1024
BATCH = 1
SEQ = 1024
DEPTH = 2

N_MIXERS = 2
N_HEADS = 16
HEAD_DIM = D_MODEL // N_HEADS
RMS_EPS = 1e-6
NEG = -1e30
BIG = 1e30
NSA_KV_GROUPS = 4
NSA_HPG = N_HEADS // NSA_KV_GROUPS
KV_W = NSA_KV_GROUPS * HEAD_DIM
CMP_BLOCK = 32
CMP_STRIDE = 16
CMP_HIDDEN = 4 * HEAD_DIM
SLC_BLOCK = 64
N_SLC_BLOCKS = 8
WINDOW = 512
NSA_QBLOCK = 32
N_BRANCH = 3
NSA_IN_W = D_MODEL + 6 * KV_W + N_BRANCH * N_HEADS
SB_QBLOCK = 128
D_FF = ((8 * D_MODEL // 3 + 255) // 256) * 256
N_NSA_LAYERS = (DEPTH + 1) // 2
N_SB_LAYERS = DEPTH // 2

kernel_name = "nsa_stickbreaking_interleaved_trunk"

def _alibi_slopes(n):
    return jnp.asarray(2.0 ** (-8.0 * (np.arange(n) + 1) / n), dtype=jnp.float32)

def _rmsnorm(x, g):
    xf = x.astype(jnp.float32)
    y = xf * lax.rsqrt(jnp.mean(xf * xf, axis=-1, keepdims=True) + RMS_EPS)
    return (y * g.astype(jnp.float32)).astype(x.dtype)

def _swiglu(h, w1, w3, w2):
    return (jax.nn.silu(h @ w1) * (h @ w3)) @ w2

def _compress(kv, pe, w1, w2):
    b, s, g, dh = kv.shape
    r = CMP_BLOCK // CMP_STRIDE
    nch = s // CMP_STRIDE
    nc = nch - r + 1
    ch = kv.reshape(b, nch, CMP_STRIDE, g, dh)
    blk = jnp.concatenate([ch[:, i:i + nc] for i in range(r)], axis=2)
    blk = blk + pe[None, None, :, None, :]
    flat = jnp.moveaxis(blk, 3, 2).reshape(b, nc, g, CMP_BLOCK * dh)
    return jax.nn.gelu(flat @ w1) @ w2

def _cmp_to_slc_matrix(n_cmp, n_slc):
    cs = np.arange(n_cmp) * CMP_STRIDE
    ce = cs + CMP_BLOCK
    ss = np.arange(n_slc) * SLC_BLOCK
    se = ss + SLC_BLOCK
    ov = np.clip(np.minimum(ce[:, None], se[None]) - np.maximum(cs[:, None], ss[None]), 0, None)
    return jnp.asarray(ov / CMP_STRIDE, dtype=jnp.float32)

def _gather_blocks(blk, idx):
    return jax.vmap(jax.vmap(lambda kb, ib: kb[ib]))(blk, idx)

def _nsa_mixer(h, w_in, gate_b, cmp_pe, cmp_w1, cmp_w2, w_out, slopes):
    b, s, d = h.shape
    g_, hpg, dh = NSA_KV_GROUPS, NSA_HPG, HEAD_DIM
    proj = h @ w_in
    cuts = np.cumsum([d, KV_W, KV_W, KV_W, KV_W, KV_W, KV_W]).tolist()
    q, kc, vc, ksl, vsl, kw, vw, gt = jnp.split(proj, cuts, axis=-1)
    q = q.reshape(b, s, g_, hpg, dh) * (dh ** -0.5)
    gates = jax.nn.sigmoid(gt + gate_b).reshape(b, s, N_BRANCH, g_, hpg)
    kc = _compress(kc.reshape(b, s, g_, dh), cmp_pe[0], cmp_w1[0], cmp_w2[0])
    vc = _compress(vc.reshape(b, s, g_, dh), cmp_pe[1], cmp_w1[1], cmp_w2[1])
    n_cmp = kc.shape[1]
    n_slcb = s // SLC_BLOCK
    n_sel = min(N_SLC_BLOCKS, n_slcb)
    cmap = _cmp_to_slc_matrix(n_cmp, n_slcb)
    c_end = jnp.arange(n_cmp) * CMP_STRIDE + CMP_BLOCK - 1
    ks_blk = jnp.transpose(ksl.reshape(b, n_slcb, SLC_BLOCK, g_, dh), (0, 3, 1, 2, 4))
    vs_blk = jnp.transpose(vsl.reshape(b, n_slcb, SLC_BLOCK, g_, dh), (0, 3, 1, 2, 4))
    pad = ((0, 0), (WINDOW, 0), (0, 0), (0, 0))
    kw_pad = jnp.pad(kw.reshape(b, s, g_, dh), pad)
    vw_pad = jnp.pad(vw.reshape(b, s, g_, dh), pad)
    sl = slopes.reshape(g_, hpg)
    qb = NSA_QBLOCK

    def step(c):
        qs = c * qb
        qc = lax.dynamic_slice_in_dim(q, qs, qb, axis=1)
        gc = lax.dynamic_slice_in_dim(gates, qs, qb, axis=1)
        t = qs + jnp.arange(qb)
        dist_c = t[:, None] - c_end[None]
        valid_c = dist_c >= 0
        s_c = jnp.einsum('bqghd,bngd->bghqn', qc, kc, preferred_element_type=jnp.float32)
        s_c = s_c - sl[None, :, :, None, None] * dist_c.astype(jnp.float32)
        p_c = jax.nn.softmax(jnp.where(valid_c, s_c, NEG), axis=-1) * valid_c
        o_c = jnp.einsum('bghqn,bngd->bqghd', p_c.astype(vc.dtype), vc)
        imp = jnp.einsum('bghqn,nj->bgqj', p_c, cmap)
        cur = t // SLC_BLOCK
        jb = jnp.arange(n_slcb)
        causal_j = jb[None] <= cur[:, None]
        forced = (jb[None] == 0) | (jb[None] == cur[:, None]) | (jb[None] == cur[:, None] - 1)
        imp = jnp.where(causal_j & forced, BIG, jnp.where(causal_j, imp, -BIG))
        _, idx = lax.top_k(imp, n_sel)
        blk_ok = idx <= cur[None, None, :, None]
        k_sel = _gather_blocks(ks_blk, idx)
        v_sel = _gather_blocks(vs_blk, idx)
        pos_s = idx[..., None] * SLC_BLOCK + jnp.arange(SLC_BLOCK)
        dist_s = t[None, None, :, None, None] - pos_s
        valid_s = ((dist_s >= 0) & blk_ok[..., None])[:, :, None]
        s_s = jnp.einsum('bqghd,bgqnkd->bghqnk', qc, k_sel, preferred_element_type=jnp.float32)
        s_s = s_s - sl[None, :, :, None, None, None] * dist_s[:, :, None].astype(jnp.float32)
        s_s = jnp.where(valid_s, s_s, NEG)
        p_s = jax.nn.softmax(s_s.reshape(b, g_, hpg, qb, n_sel * SLC_BLOCK), axis=-1)
        p_s = p_s.reshape(s_s.shape) * valid_s
        o_s = jnp.einsum('bghqnk,bgqnkd->bqghd', p_s.astype(v_sel.dtype), v_sel)
        kwc = lax.dynamic_slice_in_dim(kw_pad, qs, WINDOW + qb, axis=1)
        vwc = lax.dynamic_slice_in_dim(vw_pad, qs, WINDOW + qb, axis=1)
        pos_w = qs - WINDOW + jnp.arange(WINDOW + qb)
        dist_w = t[:, None] - pos_w[None]
        valid_w = (dist_w >= 0) & (dist_w < WINDOW) & (pos_w[None] >= 0)
        s_w = jnp.einsum('bqghd,bkgd->bghqk', qc, kwc, preferred_element_type=jnp.float32)
        s_w = s_w - sl[None, :, :, None, None] * dist_w.astype(jnp.float32)
        p_w = jax.nn.softmax(jnp.where(valid_w, s_w, NEG), axis=-1)
        o_w = jnp.einsum('bghqk,bkgd->bqghd', p_w.astype(vwc.dtype), vwc)
        return (gc[:, :, 0, :, :, None] * o_c + gc[:, :, 1, :, :, None] * o_s
                + gc[:, :, 2, :, :, None] * o_w)

    outs = lax.map(step, jnp.arange(s // qb))
    o = jnp.moveaxis(outs, 0, 1).reshape(b, s, d)
    return o @ w_out

def _stick_breaking_mixer(h, w_in, w_out):
    b, s, d = h.shape
    q, k, v = jnp.split(h @ w_in, 3, axis=-1)
    q = jnp.transpose(q.reshape(b, s, N_HEADS, HEAD_DIM), (0, 2, 1, 3)) * (HEAD_DIM ** -0.5)
    k = jnp.transpose(k.reshape(b, s, N_HEADS, HEAD_DIM), (0, 2, 1, 3))
    v = jnp.transpose(v.reshape(b, s, N_HEADS, HEAD_DIM), (0, 2, 1, 3))
    qb = SB_QBLOCK
    kpos = jnp.arange(s)

    def step(c):
        qs = c * qb
        qc = lax.dynamic_slice_in_dim(q, qs, qb, axis=2)
        t = qs + jnp.arange(qb)
        before = kpos[None] < t[:, None]
        z = jnp.einsum('bhqd,bhkd->bhqk', qc, k, preferred_element_type=jnp.float32)
        log_1m_beta = jnp.where(before, -jax.nn.softplus(z), 0.0)
        suffix = lax.cumsum(log_1m_beta, axis=3, reverse=True) - log_1m_beta
        log_a = -jax.nn.softplus(-z) + suffix
        a = jnp.where(before, jnp.exp(log_a), 0.0)
        return jnp.einsum('bhqk,bhkd->bqhd', a.astype(v.dtype), v)

    outs = lax.map(step, jnp.arange(s // qb))
    o = jnp.moveaxis(outs, 0, 1).reshape(b, s, d)
    return o @ w_out

def setup_inputs(seed: int = 0) -> dict:
    key = jax.random.key(seed)
    ks = jax.random.split(key, 16)

    def nrm(k, shape, scale):
        return jax.random.normal(k, shape, jnp.float32) * scale

    na, nb = N_NSA_LAYERS, N_SB_LAYERS
    return {
        "x": nrm(ks[0], (BATCH, SEQ, D_MODEL), 1.0),
        "mix_norm_g": 1.0 + nrm(ks[1], (DEPTH, D_MODEL), 0.05),
        "ffn_norm_g": 1.0 + nrm(ks[2], (DEPTH, D_MODEL), 0.05),
        "final_norm_g": 1.0 + nrm(ks[3], (D_MODEL,), 0.05),
        "nsa_w_in": nrm(ks[4], (na, D_MODEL, NSA_IN_W), D_MODEL ** -0.5),
        "nsa_gate_b": nrm(ks[5], (na, N_BRANCH * N_HEADS), 0.1),
        "nsa_cmp_pe": nrm(ks[6], (na, 2, CMP_BLOCK, HEAD_DIM), 0.1),
        "nsa_cmp_w1": nrm(ks[7], (na, 2, CMP_BLOCK * HEAD_DIM, CMP_HIDDEN), (CMP_BLOCK * HEAD_DIM) ** -0.5),
        "nsa_cmp_w2": nrm(ks[8], (na, 2, CMP_HIDDEN, HEAD_DIM), CMP_HIDDEN ** -0.5),
        "nsa_w_out": nrm(ks[9], (na, D_MODEL, D_MODEL), D_MODEL ** -0.5),
        "sb_w_in": nrm(ks[10], (nb, D_MODEL, 3 * D_MODEL), D_MODEL ** -0.5),
        "sb_w_out": nrm(ks[11], (nb, D_MODEL, D_MODEL), D_MODEL ** -0.5),
        "ffn_w1": nrm(ks[12], (DEPTH, D_MODEL, D_FF), D_MODEL ** -0.5),
        "ffn_w3": nrm(ks[13], (DEPTH, D_MODEL, D_FF), D_MODEL ** -0.5),
        "ffn_w2": nrm(ks[14], (DEPTH, D_FF, D_MODEL), D_FF ** -0.5),
    }

def reference(x, mix_norm_g, ffn_norm_g, final_norm_g, nsa_w_in, nsa_gate_b, nsa_cmp_pe,
              nsa_cmp_w1, nsa_cmp_w2, nsa_w_out, sb_w_in, sb_w_out, ffn_w1, ffn_w3, ffn_w2):
    slopes = _alibi_slopes(N_HEADS)
    h = x
    for i in range(DEPTH):
        a = _rmsnorm(h, mix_norm_g[i])
        j = i // N_MIXERS
        if i % N_MIXERS == 0:
            mix = _nsa_mixer(a, nsa_w_in[j], nsa_gate_b[j], nsa_cmp_pe[j], nsa_cmp_w1[j],
                             nsa_cmp_w2[j], nsa_w_out[j], slopes)
        else:
            mix = _stick_breaking_mixer(a, sb_w_in[j], sb_w_out[j])
        h = h + mix
        h = h + _swiglu(_rmsnorm(h, ffn_norm_g[i]), ffn_w1[i], ffn_w3[i], ffn_w2[i])
    return _rmsnorm(h, final_norm_g)


_drawn_inputs = setup_inputs


def setup_inputs(seed=0):
    import zlib

    import numpy as np

    out = dict(_drawn_inputs(seed))
    spreads = {}
    factors = {'nsa_gate_b': 2.909}
    for name, (base, spread) in spreads.items():
        noise = np.random.default_rng([zlib.crc32(name.encode()), seed]).standard_normal(out[name].shape)
        drawn = base * np.exp(spread * noise) if base else spread * noise
        out[name] = __import__('jax').numpy.asarray(drawn.astype(out[name].dtype))
    for name, factor in factors.items():
        out[name] = (out[name] * factor).astype(out[name].dtype)
    return out
```

```python
import concourse.bass as bass
from concourse import mybir
import numpy as np

F32 = mybir.dt.float32
F32R = mybir.dt.float32r
ACT = mybir.ActivationFunctionType
ALU = mybir.AluOpType
AX = mybir.AxisListType

P = 128
SEQ = 1024
D = 1024
HALF = 512
KT = D // P
QT = SEQ // P
HEADS = 16
HD = D // HEADS
GROUPS = 4
HPG = HEADS // GROUPS
KVW = GROUPS * HD
BRANCHES = 3
CMP_LEN, CMP_STEP = 32, 16
NCP = SEQ // CMP_STEP
NC = NCP - 1
HID = 4 * HD
BLK = 64
NBLK = SEQ // BLK
N_SEL = 8
WIN = 512
WT = WIN // P
D_FF = 2816
FT = D_FF // P
EPS = 1e-6
BIG = 1e30
QSCALE = HD ** -0.5
NSA_TILES = (D + 6 * KVW) // P
FFN_CHUNKS = (8, 8, 6)
assert sum(FFN_CHUNKS) == FT


class Memory:

    def __init__(self, nc):
        self.nc = nc
        tile = SEQ * 4
        self.base = 16512
        self.xr = self.base + KT * tile
        self.st = self.xr + 2 * KT * tile
        self.big = self.st + 6 * tile
        self.small = self.big + NSA_TILES * tile
        at = self.at
        self.H = at("H", self.base, [P, KT, SEQ])
        self.XH = at("XH", self.xr, [P, KT, SEQ], F32R)
        self.XL = at("XL", self.xr + KT * tile, [P, KT, SEQ], F32R)
        self.W32 = at("W32", self.st, [P, 2, KT, P])
        self.WHI = at("WHI", self.st + 2 * tile, [P, 2, KT, P], F32R)
        self.WLO = at("WLO", self.st + 4 * tile, [P, 2, KT, P], F32R)
        o = self.small
        self.ident = at("ident", o, [P, P]); o += P * 4
        self.ones = at("ones", o, [P, P], F32R); o += P * 4
        self.slopes = at("slopes", o, [P, HEADS]); o += HEADS * 4
        self.gains = at("gains", o, [P, 5, KT]); o += 5 * KT * 4
        self.eps = at("eps", o, [P, 8]); o += 32
        self.gates = at("gates", o, [P, QT, BRANCHES * HEADS]); o += QT * BRANCHES * HEADS * 4
        self.gate_bias = at("gate_bias", o, [P, BRANCHES * HEADS]); o += BRANCHES * HEADS * 4
        self.proj = at("proj", self.big, [P, NSA_TILES, SEQ])
        self.small_end = o
        self.PS = nc.alloc_psum_tensor("PS", [P, 8, HALF], F32)

    def at(self, name, offset, shape, dt=F32):
        return self.nc.alloc_sbuf_tensor_at(name, shape, dt, offset=offset)


def sems(nc, prefix, *names):
    return [nc.alloc_semaphore(f"{prefix}_{n}") for n in names]


def strip_products(nc, out, whi, wlo, xh, xl, n):
    for k in range(n):
        for w, x in ((whi, xh), (whi, xl), (wlo, xh)):
            for half in range(2):
                cols = slice(half * HALF, half * HALF + HALF)
                last = nc.tensor.matmul(out[:, cols], w[:, k, :], x[:, k, cols],
                                        start=(k == 0 and w is whi and x is xh),
                                        stop=(k == n - 1 and w is wlo))
    return last


def strip_psum(m, slot):
    return m.PS[:, 2 * slot:2 * slot + 2, :].rearrange("p a n -> p (a n)")


def load_input(nc, m, x, gains):
    ones32 = m.at("ones32", m.big, [P, P])
    loaded, made, rounded = sems(nc, "in", "loaded", "made", "rounded")
    with nc.Block() as block:
        @block.sync
        def _(sp):
            sp.dma_start(m.gains[:], gains).then_inc(loaded, 16)
            for k in range(0, KT, 2):
                sp.dma_start(m.H[:, k:k + 2, :], x[:, k:k + 2, :]).then_inc(loaded, 16)
            sp.wait_ge(loaded, 16 * (1 + KT // 2))

        @block.gpsimd
        def _(pool):
            nc.gpsimd.memset(m.ident[:], 0.0).then_inc(made, 1)
            pool.wait_ge(made, 1)
            nc.gpsimd.affine_select(out=m.ident[:], in_=m.ident[:], compare_op=ALU.not_equal, fill=1.0,
                                    base=0, pattern=[[-1, P]], channel_multiplier=1).then_inc(made, 1)
            nc.gpsimd.memset(ones32[:], 1.0).then_inc(made, 1)
            nc.gpsimd.memset(m.eps[:], EPS).then_inc(made, 1)
            for h in range(HEADS):
                slope = float(np.float32(2.0 ** (-8.0 * (h + 1) / HEADS)))
                nc.gpsimd.memset(m.slopes[:, h:h + 1], slope).then_inc(made, 1)
            pool.wait_ge(made, 4 + HEADS)

        @block.vector
        def _(dve):
            dve.wait_ge(made, 3)
            nc.vector.tensor_copy(m.ones[:], ones32[:]).then_inc(rounded, 1)
            dve.wait_ge(rounded, 1)


def rmsnorm(nc, m, n, out=None):
    t = SEQ * 4
    sq = m.at(f"sq{n}", m.big, [P, 2, SEQ])
    sqh = m.at(f"sqh{n}", m.big + 2 * t, [P, 2, SEQ], F32R)
    sql = m.at(f"sql{n}", m.big + 4 * t, [P, 2, SEQ], F32R)
    lnv = m.at(f"lnv{n}", m.big + 6 * t, [P, SEQ])
    rstd = m.at(f"rstd{n}", m.big + 7 * t, [P, SEQ])
    y = m.at(f"y{n}", m.big + 8 * t, [P, 2, SEQ])
    squared, hi, lo, summed, rs, yv, yh, yl, stored = sems(
        nc, f"n{n}", "squared", "hi", "lo", "summed", "rstd", "y", "yh", "yl", "stored")
    with nc.Block() as block:
        @block.scalar
        def _(act):
            for k in range(KT):
                if k >= 2:
                    act.wait_ge(lo, k - 1)
                nc.scalar.activation(sq[:, k % 2, :], m.H[:, k, :], ACT.Square).then_inc(squared, 1)
                if k >= 2:
                    act.wait_ge(summed, k - 1)
                act.wait_ge(squared, k + 1)
                nc.scalar.copy(sqh[:, k % 2, :], sq[:, k % 2, :]).then_inc(hi, 1)
            act.wait_ge(summed, KT)
            nc.scalar.activation(lnv[:], strip_psum(m, 0), ACT.Ln, bias=m.eps[:, 0:1], scale=1.0 / D).then_inc(rs, 1)
            act.wait_ge(rs, 1)
            nc.scalar.activation(rstd[:], lnv[:], ACT.Exp, scale=-0.5).then_inc(rs, 1)
            if out is None:
                for k in range(KT):
                    act.wait_ge(yv, k + 1)
                    nc.scalar.copy(m.XH[:, k, :], y[:, k % 2, :]).then_inc(yh, 1)

        @block.vector
        def _(dve):
            def low_part(k):
                dve.wait_ge(yh, k + 1)
                nc.vector.tensor_tensor(m.XL[:, k, :], y[:, k % 2, :], m.XH[:, k, :].bitcast(F32),
                                        ALU.subtract).then_inc(yl, 1)

            for k in range(KT):
                if k >= 2:
                    dve.wait_ge(summed, k - 1)
                dve.wait_ge(hi, k + 1)
                nc.vector.tensor_tensor(sql[:, k % 2, :], sq[:, k % 2, :], sqh[:, k % 2, :].bitcast(F32),
                                        ALU.subtract).then_inc(lo, 1)
            dve.wait_ge(rs, 2)
            for k in range(KT):
                dst = m.H[:, k, :] if out is not None else y[:, k % 2, :]
                if k >= 2 and out is None:
                    dve.wait_ge(yl, k - 1)
                nc.vector.scalar_tensor_tensor(out=dst, in0=m.H[:, k, :], scalar=m.gains[:, n, k:k + 1],
                                               in1=rstd[:], op0=ALU.mult, op1=ALU.mult).then_inc(yv, 1)
                if out is None and k >= 1:
                    low_part(k - 1)
            if out is None:
                low_part(KT - 1)

        @block.tensor
        def _(pe):
            for k in range(KT):
                pe.wait_ge(lo, k + 1)
                for part in (sqh, sql):
                    for half in range(2):
                        cols = slice(half * HALF, half * HALF + HALF)
                        last = nc.tensor.matmul(strip_psum(m, 0)[:, cols], m.ones[:], part[:, k % 2, cols],
                                                start=(k == 0 and part is sqh), stop=(k == KT - 1 and part is sql))
                last.then_inc(summed, 1)

        if out is not None:
            @block.sync
            def _(sp):
                for k in range(KT):
                    sp.wait_ge(yv, k + 1)
                    sp.dma_start(out[:, k, :], m.H[:, k, :]).then_inc(stored, 16)
                sp.wait_ge(stored, 16 * KT)


class Strips:

    def __init__(self, nc, m, tag):
        self.nc, self.m = nc, m
        self.loaded = sems(nc, tag, "loaded0", "loaded1")
        self.high, self.low, self.multiplied, self.drained = sems(nc, tag, "high", "low", "multiplied", "drained")

    def load(self, sp, s, slot, src, n=KT, cols=P):
        sp.wait_ge(self.low, s + 1)
        sp.dma_start(self.m.W32[:, slot, 0:n, 0:cols], src).then_inc(self.loaded[slot], 16)

    def split_high(self, act, s, slot, rounds, n=KT, cols=P):
        act.wait_ge(self.loaded[slot], rounds * 16)
        act.wait_ge(self.multiplied, s + 1)
        self.nc.scalar.copy(self.m.WHI[:, slot, 0:n, 0:cols], self.m.W32[:, slot, 0:n, 0:cols]).then_inc(self.high, 1)

    def split_low(self, dve, s, slot, n=KT, cols=P):
        dve.wait_ge(self.high, s + 1)
        self.nc.vector.tensor_tensor(self.m.WLO[:, slot, 0:n, 0:cols], self.m.W32[:, slot, 0:n, 0:cols],
                                     self.m.WHI[:, slot, 0:n, 0:cols].bitcast(F32), ALU.subtract).then_inc(self.low, 1)

    def multiply(self, pe, s, slot, xh, xl, n=KT):
        pe.wait_ge(self.low, s + 3)
        strip_products(self.nc, strip_psum(self.m, slot), self.m.WHI[:, slot], self.m.WLO[:, slot],
                       xh, xl, n).then_inc(self.multiplied, 1)


def strip_of(w, s, n=KT, k0=0):
    return w[bass.ds(s, 1), :, k0:k0 + n, :].rearrange("a p k c -> (a p) k c")


def row(t, i):
    return t[:, bass.ds(i, 1), :].rearrange("p a n -> p (a n)")


def nsa_projection(nc, m, w_in, w_gate, gate_b):
    st = Strips(nc, m, "ni")
    biased, gated, bias_loaded = sems(nc, "ni", "biased", "gated", "bias")
    GC = BRANCHES * HEADS
    N = NSA_TILES
    with nc.Block() as block:
        @block.sync
        def _(sp):
            sp.dma_start(m.gate_bias[:], gate_b.partition_broadcast(P)).then_inc(bias_loaded, 16)
            with sp.Fori(0, N // 2) as i:
                for slot in range(2):
                    st.load(sp, 2 * i + slot, slot, strip_of(w_in, 2 * i + slot))
            st.load(sp, N, 0, w_gate, cols=GC)

        @block.scalar
        def _(act):
            with act.Fori(0, N // 2) as i:
                for slot in range(2):
                    st.split_high(act, 2 * i + slot, slot, i + 1)
            st.split_high(act, N, 0, N // 2 + 1, cols=GC)
            act.wait_ge(biased, 1)
            nc.scalar.activation(m.gates[:], m.gates[:], ACT.Sigmoid).then_inc(gated, 1)

        @block.vector
        def _(dve):
            def drain(s, slot):
                dve.wait_ge(st.multiplied, s + 3)
                nc.vector.tensor_copy(row(m.proj, s), strip_psum(m, slot)).then_inc(st.drained, 1)

            dve.sem_inc(st.low, 2)
            dve.sem_inc(st.drained, 2)
            for slot in range(2):
                st.split_low(dve, slot, slot)
            with dve.Fori(0, N // 2 - 1) as i:
                for slot in range(2):
                    drain(2 * i + slot, slot)
                    st.split_low(dve, 2 * i + slot + 2, slot)
            drain(N - 2, 0)
            st.split_low(dve, N, 0, cols=GC)
            drain(N - 1, 1)
            dve.wait_ge(st.multiplied, N + 3)
            dve.wait_ge(bias_loaded, 16)
            for t in range(QT):
                last = nc.vector.tensor_tensor(m.gates[:, t, :], m.PS[:, 0, t * GC:(t + 1) * GC],
                                               m.gate_bias[:], ALU.add)
            last.then_inc(biased, 1)

        @block.tensor
        def _(pe):
            pe.sem_inc(st.multiplied, 2)
            with pe.Fori(0, N // 2) as i:
                for slot in range(2):
                    pe.wait_ge(st.drained, 2 * i + slot + 1)
                    st.multiply(pe, 2 * i + slot, slot, m.XH, m.XL)
            pe.wait_ge(st.low, N + 3)
            pe.wait_ge(st.drained, N + 1)
            for t in range(QT):
                rows = slice(t * P, (t + 1) * P)
                for k in range(KT):
                    for x, w in ((m.XH, m.WHI), (m.XL, m.WHI), (m.XH, m.WLO)):
                        last = nc.tensor.matmul(m.PS[:, 0, t * GC:(t + 1) * GC], x[:, k, rows], w[:, 0, k, 0:GC],
                                                start=(k == 0 and w is m.WHI and x is m.XH),
                                                stop=(k == KT - 1 and w is m.WLO))
            last.then_inc(st.multiplied, 1)


def add_residual(nc, m, st, dve, tile, slot, s):
    dve.wait_ge(st.multiplied, s + 3)
    nc.vector.tensor_tensor(row(m.H, tile), row(m.H, tile), strip_psum(m, slot), ALU.add).then_inc(st.drained, 1)


def residual_projection(nc, m, tag, w):
    st = Strips(nc, m, tag)
    oh, ol = sems(nc, tag, "oh", "ol")
    with nc.Block() as block:
        @block.sync
        def _(sp):
            with sp.Fori(0, KT // 2) as i:
                for slot in range(2):
                    st.load(sp, 2 * i + slot, slot, strip_of(w, 2 * i + slot))

        @block.scalar
        def _(act):
            for k in range(KT):
                nc.scalar.copy(m.XH[:, k, :], m.proj[:, k, :]).then_inc(oh, 1)
            with act.Fori(0, KT // 2) as i:
                for slot in range(2):
                    st.split_high(act, 2 * i + slot, slot, i + 1)

        @block.vector
        def _(dve):
            dve.sem_inc(st.low, 2)
            dve.sem_inc(st.drained, 2)
            for k in range(KT):
                dve.wait_ge(oh, k + 1)
                nc.vector.tensor_tensor(m.XL[:, k, :], m.proj[:, k, :], m.XH[:, k, :].bitcast(F32),
                                        ALU.subtract).then_inc(ol, 1)
            for slot in range(2):
                st.split_low(dve, slot, slot)
            with dve.Fori(0, KT // 2 - 1) as i:
                for slot in range(2):
                    add_residual(nc, m, st, dve, 2 * i + slot, slot, 2 * i + slot)
                    st.split_low(dve, 2 * i + slot + 2, slot)
            for slot in range(2):
                add_residual(nc, m, st, dve, KT - 2 + slot, slot, KT - 2 + slot)

        @block.tensor
        def _(pe):
            pe.sem_inc(st.multiplied, 2)
            pe.wait_ge(ol, KT)
            with pe.Fori(0, KT // 2) as i:
                for slot in range(2):
                    pe.wait_ge(st.drained, 2 * i + slot + 1)
                    st.multiply(pe, 2 * i + slot, slot, m.XH, m.XL)


def ffn_chunk(nc, m, tag, w1, w3, w2, f0, nf):
    t = SEQ * 4
    mh = m.at(f"mh{tag}", m.big, [P, 8, SEQ], F32R)
    ml = m.at(f"ml{tag}", m.big + 8 * t, [P, 8, SEQ], F32R)
    sil = m.at(f"sil{tag}", m.big + 16 * t, [P, SEQ])
    prod = m.at(f"prod{tag}", m.big + 17 * t, [P, SEQ])
    st = Strips(nc, m, tag)
    silu, mul, mhi, mlo = sems(nc, tag, "silu", "mul", "mhi", "mlo")
    N1 = 2 * nf
    with nc.Block() as block:
        @block.sync
        def _(sp):
            with sp.Fori(0, nf) as i:
                for slot, w in ((0, w1), (1, w3)):
                    st.load(sp, 2 * i + slot, slot, strip_of(w, i + f0))
            with sp.Fori(0, KT // 2) as i:
                for slot in range(2):
                    st.load(sp, 2 * i + slot + N1, slot, strip_of(w2, 2 * i + slot, nf, f0), nf)

        @block.scalar
        def _(act):
            def gate(i, between):
                act.wait_ge(st.multiplied, 2 * i + 3)
                act.wait_ge(mul, i)
                nc.scalar.activation(sil[:], strip_psum(m, 0), ACT.Silu).then_inc(silu, 1)
                between()
                act.wait_ge(mul, i + 1)
                nc.scalar.copy(row(mh, i), prod[:]).then_inc(mhi, 1)

            for slot in range(2):
                st.split_high(act, slot, slot, 1)
            with act.Fori(0, nf - 1) as i:
                gate(i, lambda: st.split_high(act, 2 * i + 2, 0, i + 2))
                st.split_high(act, 2 * i + 3, 1, i + 2)
            gate(nf - 1, lambda: st.split_high(act, N1, 0, nf + 1, nf))
            st.split_high(act, N1 + 1, 1, nf + 1, nf)
            with act.Fori(1, KT // 2) as i:
                for slot in range(2):
                    st.split_high(act, 2 * i + slot + N1, slot, i + nf + 1, nf)

        @block.vector
        def _(dve):
            def product(i):
                dve.wait_ge(st.multiplied, 2 * i + 4)
                dve.wait_ge(silu, i + 1)
                dve.wait_ge(mlo, i)
                nc.vector.tensor_tensor(prod[:], sil[:], strip_psum(m, 1), ALU.mult).then_inc(mul, 1)
                dve.wait_ge(mhi, i + 1)
                nc.vector.tensor_tensor(row(ml, i), prod[:], row(mh, i).bitcast(F32), ALU.subtract).then_inc(mlo, 1)

            dve.sem_inc(st.low, 2)
            for slot in range(2):
                st.split_low(dve, slot, slot)
            with dve.Fori(0, nf - 1) as i:
                st.split_low(dve, 2 * i + 2, 0)
                product(i)
                st.split_low(dve, 2 * i + 3, 1)
            st.split_low(dve, N1, 0, nf)
            product(nf - 1)
            st.split_low(dve, N1 + 1, 1, nf)
            with dve.Fori(0, KT // 2 - 1) as i:
                for slot in range(2):
                    add_residual(nc, m, st, dve, 2 * i + slot, slot, 2 * i + slot + N1)
                    st.split_low(dve, 2 * i + slot + 2 + N1, slot, nf)
            for slot in range(2):
                add_residual(nc, m, st, dve, KT - 2 + slot, slot, KT - 2 + slot + N1)

        @block.tensor
        def _(pe):
            pe.sem_inc(st.multiplied, 2)
            with pe.Fori(0, nf) as i:
                pe.wait_ge(silu, i)
                st.multiply(pe, 2 * i, 0, m.XH, m.XL)
                pe.wait_ge(mul, i)
                st.multiply(pe, 2 * i + 1, 1, m.XH, m.XL)
            pe.wait_ge(mlo, nf)
            for slot in range(2):
                st.multiply(pe, slot + N1, slot, mh, ml, nf)
            with pe.Fori(1, KT // 2) as i:
                for slot in range(2):
                    pe.wait_ge(st.drained, 2 * i + slot - 1)
                    st.multiply(pe, 2 * i + slot + N1, slot, mh, ml, nf)


def nsa_memory(m):
    t = SEQ * 4
    o = m.xr
    m.Q1 = m.at("Q1", o, [P, HPG, SEQ], F32R); o += HPG * t
    m.Q2 = m.at("Q2", o, [P, HPG, HALF], F32R); o += HPG * HALF * 4
    m.KS1 = m.at("KS1", o, [P, SEQ], F32R); o += t
    m.KS2 = m.at("KS2", o, [P, SEQ], F32R); o += t
    m.KW1 = m.at("KW1", o, [P, SEQ], F32R); o += t
    m.KW2 = m.at("KW2", o, [P, SEQ], F32R); o += t
    m.T = m.at("T", o, [P, 2, SEQ]); o += 2 * t
    m.BS = m.at("BS", o, [P, 2, SEQ]); o += 2 * t
    m.PT = m.at("PT", o, [P, 2, HALF]); o += 2 * HALF * 4
    assert o <= m.st
    o = m.st
    m.DIST = m.at("DIST", o, [P, SEQ]); o += t
    m.DISTW = m.at("DISTW", o, [P, WIN + P]); o += (WIN + P) * 4
    m.BW = m.at("BW", o, [P, 2, WIN + P]); o += 2 * (WIN + P) * 4
    m.DISTC = m.at("DISTC", o, [P, QT, NCP]); o += QT * NCP * 4
    m.LOWER = m.at("LOWER", o, [P, NBLK, NBLK]); o += NBLK * NBLK * 4
    m.FORCED = m.at("FORCED", o, [P, QT // 2, NBLK]); o += QT // 2 * NBLK * 4
    m.PG = m.at("PG", o, [P, QT, NCP]); o += QT * NCP * 4
    m.TO = m.at("TO", o, [P, QT, HD]); o += QT * HD * 4
    m.IMP = m.at("IMP", o, [P, QT // 2, NBLK]); o += QT // 2 * NBLK * 4
    m.RANK = m.at("RANK", o, [P, QT // 2, NBLK]); o += QT // 2 * NBLK * 4
    m.NM = m.at("NM", o, [P, 2, 2, QT]); o += 32 * 4
    m.SUM = m.at("SUM", o, [P, 2, 2, QT]); o += 32 * 4
    m.REC = m.at("REC", o, [P, 2, QT]); o += 16 * 4
    m.MX = m.at("MX", o, [P, 2, QT]); o += 16 * 4
    m.DEN = m.at("DEN", o, [P, 2, QT]); o += 16 * 4
    m.SOME = m.at("SOME", o, [P, 8]); o += 32
    m.VCG = m.at("VCG", o, [P, HD]); o += HD * 4
    m.IND = m.at("IND", o, [P, SEQ]); o += t
    assert o <= m.big
    m.VS = m.at("VS", m.big + 8 * t, [P, QT, KVW])
    m.VW = m.at("VW", m.big + 10 * t, [P, QT, KVW])
    m.OT = m.at("OT", m.big + 14 * t, [P, QT, HPG * HD])
    m.TMPQ = m.at("TMPQ", m.big + 18 * t, [P, 2, SEQ])
    o = m.small_end
    m.KC1 = m.at("KC1", o, [P, GROUPS, NCP], F32R); o += GROUPS * NCP * 4
    m.KC2 = m.at("KC2", o, [P, GROUPS, NCP], F32R); o += GROUPS * NCP * 4
    m.VC = m.at("VC", o, [P, GROUPS, HD]); o += GROUPS * HD * 4
    assert o <= 229368


def nsa_compress(nc, m, cmp_w1, cmp_w2, cmp_pe):
    t = SEQ * 4
    o = m.xr
    w1 = m.at("cw1", o, [P, 2, KT * 2, HID]); o += 2 * 2 * KT * HID * 4
    x2 = m.at("cx2", o, [P, 2, GROUPS, CMP_STEP // 2, NCP]); o += 2 * GROUPS * CMP_STEP // 2 * NCP * 4
    gel = m.at("cgel", o, [P, 2, 2, GROUPS, NCP]); o += 4 * GROUPS * NCP * 4
    w2 = m.at("cw2", o, [P, 2, 2, HD]); o += 4 * HD * 4
    pe_ = m.at("cpe", o, [P, 2, 2 * KT]); o += 4 * KT * 4
    hb = m.at("chb", o, [P, 4]); o += 16
    kc = m.at("ckc", o + 16, [P, GROUPS, NCP]); o += GROUPS * NCP * 4 + 16
    assert o <= m.st
    loaded, pairs_a, pairs_v, biased, bias_kept, hidden, gelu, zero, kready, vready, kc_kept, kc_hi, kc_done, \
        turned, vt_kept, made, vc_done = sems(nc, "c", "loaded", "pairsa", "pairsv", "biased", "biaskept", "hidden", "gelu",
                                     "zero", "kready", "vready", "kckept", "kchi", "kcdone", "turned", "vtkept",
                                     "made", "vcdone")
    MM = CMP_LEN // 2
    with nc.Block() as block:
        @block.sync
        def _(sp):
            sp.dma_start(w1[:], cmp_w1).then_inc(loaded, 16)
            sp.dma_start(w2[:], cmp_w2).then_inc(loaded, 16)
            sp.dma_start(pe_[:], cmp_pe).then_inc(loaded, 16)
            sp.wait_ge(loaded, 48)

        def pair_copies(which):
            for g in range(GROUPS):
                src = m.proj[HD * (g % 2):HD * (g % 2) + HD, 8 + 2 * which + g // 2, :].rearrange(
                    "p (n r a) -> p a r n", r=CMP_STEP // 2, a=2)
                for par in range(2):
                    yield x2[HD * par:HD * par + HD, which, g], src[:, par]

        @block.scalar
        def _(act):
            for dst, src in pair_copies(0):
                last = nc.scalar.copy(dst, src)
            last.then_inc(pairs_a, 1)
            act.wait_ge(zero, 1)
            act.wait_ge(bias_kept, 1)
            for n in range(4):
                act.wait_ge(hidden, n + 1)
                nc.scalar.activation(gel[:, n // 2, n % 2, :, 0:NC],
                                     m.PS[:, n % 2, 0:GROUPS * NC].rearrange("p (g n) -> p g n", g=GROUPS),
                                     ACT.Gelu_apprx_tanh, bias=hb[:, n:n + 1]).then_inc(gelu, 1)
            act.wait_ge(kc_kept, 1)
            nc.scalar.copy(m.KC1[0:HD], kc[0:HD]).then_inc(kc_hi, 1)
            for n in range(4):
                act.wait_ge(turned, n + 1)
                v = m.VS if n < 2 else m.VW
                nc.scalar.copy(v[:, :, (n % 2) * P:(n % 2) * P + P],
                               strip_psum(m, 2 + n % 2).rearrange("p (t c) -> p t c", c=P)).then_inc(vt_kept, 1)

        @block.vector
        def _(dve):
            nc.vector.memset(gel[:], 0.0).then_inc(zero, 1)
            for dst, src in pair_copies(1):
                last = nc.vector.tensor_copy(dst, src)
            last.then_inc(pairs_v, 1)
            dve.wait_ge(biased, 1)
            nc.vector.tensor_copy(hb[:], m.PS[:, 3, 0:4]).then_inc(bias_kept, 1)
            dve.wait_ge(kready, 1)
            nc.vector.tensor_copy(kc[0:HD], m.PS[0:HD, 2, 0:GROUPS * NCP].rearrange("p (g n) -> p g n", g=GROUPS)
                                  ).then_inc(kc_kept, 1)
            dve.wait_ge(kc_hi, 1)
            nc.vector.tensor_copy(m.KC1[HD:P], m.KC1[0:HD].bitcast(F32)).then_inc(kc_done, 1)
            nc.vector.tensor_tensor(m.KC2[0:HD], kc[0:HD], m.KC1[0:HD].bitcast(F32), ALU.subtract).then_inc(kc_done, 1)
            dve.wait_ge(vready, 1)
            for half in range(2):
                nc.vector.tensor_copy(m.VC[HD * half:HD * half + HD],
                                      m.PS[0:NCP, 3, 0:KVW].rearrange("p (g d) -> p g d", g=GROUPS)).then_inc(vc_done, 1)

        @block.tensor
        def _(pe):
            pe.wait_ge(loaded, 48)
            for n in range(4):
                for mm in range(MM):
                    last = nc.tensor.matmul(m.PS[:, 3, n:n + 1], w1[:, n // 2, mm, (n % 2) * P:(n % 2) * P + P],
                                            pe_[:, n // 2, mm:mm + 1], start=(mm == 0), stop=(mm == MM - 1))
            last.then_inc(biased, 1)
            pe.wait_ge(pairs_a, 1)
            for n in range(4):
                if n == 2:
                    pe.wait_ge(pairs_v, 1)
                if n >= 2:
                    pe.wait_ge(gelu, n - 1)
                for mm in range(MM):
                    r, first = mm % (CMP_STEP // 2), mm // (CMP_STEP // 2)
                    last = nc.tensor.matmul(m.PS[:, n % 2, 0:GROUPS * NC].rearrange("p (g n) -> p g n", g=GROUPS),
                                            w1[:, n // 2, mm, (n % 2) * P:(n % 2) * P + P],
                                            x2[:, n // 2, :, r, first:first + NC],
                                            start=(mm == 0), stop=(mm == MM - 1))
                last.then_inc(hidden, 1)
            pe.wait_ge(gelu, 4)
            pe.wait_ge(bias_kept, 1)
            for half in range(2):
                last = nc.tensor.matmul(m.PS[0:HD, 2, 0:GROUPS * NCP], w2[:, 0, half, :],
                                        gel[:, 0, half, :, :].rearrange("p g n -> p (g n)"), start=(half == 0), stop=(half == 1))
            last.then_inc(kready, 1)
            for g in range(GROUPS):
                for half in range(2):
                    last = nc.tensor.matmul(m.PS[0:NCP, 3, g * HD:(g + 1) * HD], gel[:, 1, half, g, :], w2[:, 1, half, :],
                                            start=(half == 0), stop=(half == 1))
            last.then_inc(vready, 1)
            for n in range(4):
                tile = (14, 15, 18, 19)[n]
                if n >= 2:
                    pe.wait_ge(vt_kept, n - 1)
                for kt in range(QT):
                    last = nc.tensor.transpose(strip_psum(m, 2 + n % 2)[:, kt * P:(kt + 1) * P],
                                               m.proj[:, tile, kt * P:(kt + 1) * P], m.ident[:])
                last.then_inc(turned, 1)

        @block.gpsimd
        def _(pool):
            count = 0

            def put(ins):
                nonlocal count
                count += 1
                ins.then_inc(made, 1)
                pool.wait_ge(made, count)

            def keep(out, op, base, pattern, mult, fill):
                put(nc.gpsimd.affine_select(out=out, in_=out, compare_op=op, fill=fill, base=base,
                                            pattern=pattern, channel_multiplier=mult))

            exact = dict(allow_small_or_imprecise_dtypes=True)
            put(nc.gpsimd.iota(m.DIST[:], pattern=[[1, SEQ]], base=P - SEQ, channel_multiplier=-1, **exact))
            keep(m.DIST[:], ALU.is_ge, SEQ - P, [[-1, SEQ]], 1, -BIG)
            put(nc.gpsimd.iota(m.DISTW[:], pattern=[[1, WIN + P]], base=-WIN, channel_multiplier=-1, **exact))
            keep(m.DISTW[:], ALU.is_ge, WIN, [[-1, WIN + P]], 1, -BIG)
            keep(m.DISTW[:], ALU.is_gt, 0, [[1, WIN + P]], -1, -BIG)
            put(nc.gpsimd.iota(m.DISTC[:], pattern=[[-P, QT], [CMP_STEP, NCP]], base=CMP_LEN - 1,
                               channel_multiplier=-1, **exact))
            keep(m.DISTC[:], ALU.is_ge, 1 - CMP_LEN, [[P, QT], [-CMP_STEP, NCP]], 1, -BIG)
            put(nc.gpsimd.memset(m.SOME[:], 1.0))
            keep(m.SOME[:], ALU.is_ge, 1 - CMP_LEN, [[0, 8]], 1, 0.0)
            put(nc.gpsimd.memset(m.LOWER[:], 1.0))
            keep(m.LOWER[:], ALU.is_gt, 0, [[1, NBLK], [-1, NBLK]], 0, 0.0)
            put(nc.gpsimd.memset(m.FORCED[:], 0.0))
            put(nc.gpsimd.memset(m.FORCED[:, :, 0:1], BIG))
            for q in range(QT // 2):
                for half in range(2):
                    cur = (q + QT // 2) * (P // BLK) + half
                    rows = m.FORCED[half * BLK:half * BLK + BLK, q]
                    put(nc.gpsimd.memset(rows[:, cur - 1:cur + 1], BIG))
                    if cur + 1 < NBLK:
                        put(nc.gpsimd.memset(rows[:, cur + 1:], -BIG))
            ind = m.IND[HD:HD + NBLK, :]
            put(nc.gpsimd.memset(ind, 1.0))
            keep(ind, ALU.is_ge, 0, [[1, SEQ]], -BLK, 0.0)
            keep(ind, ALU.is_ge, BLK - 1, [[-1, SEQ]], BLK, 0.0)


UNITS = [(h, q, b) for h in range(HPG) for q in range(QT) for b in range(2)]
UPH = 2 * QT


def unit_tiles(u):
    _, q, b = UNITS[u]
    return (q - min(q, WT), q + 1) if b else (0, q + 1)


def chunk_table():
    out = []
    for u in range(len(UNITS)):
        a, b = unit_tiles(u)
        n = b - a
        cut = b if n <= 4 else a + (3 if n == 5 else 4)
        out.append([(a, cut)] + ([(cut, b)] if cut < b else []))
    return out


CHUNKS = chunk_table()
FIRST_CHUNK = [HPG + sum(len(c) for c in CHUNKS[:u]) for u in range(len(UNITS) + 1)]
NCH = FIRST_CHUNK[-1]
NU = len(UNITS)
ORDER = [("c", h) for h in range(HPG)]
for _u in range(NU):
    ORDER.append(("u", _u))
    if _u == 2 * UPH + 2:
        ORDER.append(("o", 0))
ORDER.append(("o", 1))
SEQ_OF = {e: n for n, e in enumerate(ORDER)}
NS = len(ORDER)
assert NS % 2 == 0 and NCH % 2 == 0


def on_dve(c):
    return c >= HPG and c % 3 == 1


NCH_D = sum(on_dve(c) for c in range(NCH))
NCH_A = NCH - NCH_D


def done_before(c):
    return sum(on_dve(k) == on_dve(c) for k in range(c + 1))


def nsa_attention(nc, m):
    st_t, st_h, st_l, s_ready, s_free, c_sub, c_exp, c_p, pt_t, ev_a, ev_d, pv, o_free, mk, mk_t, q2m, \
        b_r, p_r, ch, ind_r, begun = sems(nc, "a", "shifted", "high", "low", "scores", "scorefree", "csub", "cexp", "cp",
                                   "turned", "evact", "evdve", "pv", "ofree", "mask", "maskturned",
                                   "maskkept", "bias", "probs", "chain", "ind", "begun")
    CHAIN = HPG * 5 + 9 + HPG * 5

    def ptslot(c):
        return m.PS[:, 4 + c % 2, :]

    with nc.Block() as block:
        @block.scalar
        def _(act):
            act.activation(m.KS2[HD:HD + NBLK, :], m.IND[HD:HD + NBLK, :], ACT.Copy).then_inc(ind_r, 1)
            with act.Fori(0, GROUPS // 2) as j:
                for gi in range(2):
                    g = 2 * j + gi
                    act.wait_ge(s_free, NS * g + 2)

                    def bias(h):
                        nc.scalar.activation(m.BS[:, h % 2, :], m.DIST[:], ACT.Copy,
                                             scale=m.slopes[:, bass.ds(HPG * g + h, 1)])
                        nc.scalar.activation(m.BW[:, h % 2, :], m.DISTW[:], ACT.Copy,
                                             scale=m.slopes[:, bass.ds(HPG * g + h, 1)]).then_inc(b_r, 1)

                    def evacuate(c):
                        act.wait_ge(pt_t, NCH * g + c + 1)
                        act.wait_ge(pv, NCH * g + max(c - 1, 0))
                        nc.scalar.copy(m.PT[:, c % 2, :], ptslot(c)).then_inc(ev_a, 1)

                    for n in range(2 + HPG):
                        if n < 2:
                            src = m.proj[HD * gi:HD * gi + HD, bass.ds((12, 16)[n] + j, 1), :]
                            hi = (m.KS1, m.KW1)[n][0:HD, :]
                        else:
                            h = n - 2
                            src = m.proj[HD * (h % 2):HD * (h % 2) + HD, bass.ds(2 * g + h // 2, 1), :]
                            hi = m.Q1[0:HD, h, :]
                        if n >= 2:
                            act.wait_ge(st_l, (2 + HPG) * g + n - 1)
                        nc.scalar.activation(m.TMPQ[0:HD, n % 2, :], src.rearrange("p a n -> p (a n)"), ACT.Copy,
                                             scale=1.0 if n < 2 else QSCALE).then_inc(st_t, 1)
                        act.wait_ge(st_t, (2 + HPG) * g + n + 1)
                        nc.scalar.copy(hi, m.TMPQ[0:HD, n % 2, :]).then_inc(st_h, 1)
                    bias(0)
                    for h in range(HPG + 1):
                        if h < HPG:
                            act.wait_ge(c_sub, HPG * g + h + 1)
                            nc.scalar.activation(m.T[:, h % 2, 0:HALF], m.T[:, h % 2, 0:HALF], ACT.Exp).then_inc(c_exp, 1)
                        if h >= 1:
                            evacuate(h - 1)
                    act.wait_ge(mk_t, g + 1)
                    for h in range(HPG):
                        nc.scalar.copy(m.Q2[HD:HD + NBLK, h, :], m.PS[0:NBLK, 7, :]).then_inc(q2m, 1)
                    for u in range(NU + 1):
                        if u < NU:
                            h, q, b = UNITS[u]
                            a, e = unit_tiles(u)
                            t = m.T[:, u % 2, 0:(e - a) * P]
                            act.wait_ge(s_free, NS * g + SEQ_OF["u", u] + 3)
                            nc.scalar.activation(t, t, ACT.Exp, bias=m.NM[:, h % 2, b, q:q + 1], scale=-1.0,
                                                 accum_out=m.SUM[:, h % 2, b, q:q + 1]).then_inc(p_r, 1)
                            if u % UPH == UPH // 2 and h + 1 < HPG:
                                bias(h + 1)
                        if u >= 1:
                            for c in range(FIRST_CHUNK[u - 1], FIRST_CHUNK[u]):
                                if not on_dve(c):
                                    evacuate(c)

        @block.vector
        def _(dve):
            dve.sem_inc(s_free, 2)
            with dve.Fori(0, GROUPS // 2) as j:
                for gi in range(2):
                    g = 2 * j + gi
                    links = 0

                    def link(ins):
                        nonlocal links
                        links += 1
                        ins.then_inc(ch, 1)
                        dve.wait_ge(ch, CHAIN * g + links)

                    dve.wait_ge(s_ready, NS * g)
                    nc.vector.tensor_copy(m.VCG[:], row(m.VC, g))
                    for n in range(2 + HPG):
                        dve.wait_ge(st_h, (2 + HPG) * g + n + 1)
                        if n < 2:
                            k1, k2 = ((m.KS1, m.KS2), (m.KW1, m.KW2))[n]
                            nc.vector.tensor_copy(k1[HD:P, :], k1[0:HD, :].bitcast(F32))
                            nc.vector.tensor_tensor(k2[0:HD, :], m.TMPQ[0:HD, n % 2, :], k1[0:HD, :].bitcast(F32),
                                                    ALU.subtract).then_inc(st_l, 1)
                        else:
                            q1 = m.Q1[:, n - 2, :]
                            nc.vector.tensor_copy(m.Q2[0:HD, n - 2, :], q1[0:HD, HALF:].bitcast(F32))
                            nc.vector.tensor_tensor(q1[HD:P, :], m.TMPQ[0:HD, n % 2, :], q1[0:HD, :].bitcast(F32),
                                                    ALU.subtract).then_inc(st_l, 1)

                    def over_heads(x):
                        return x.unsqueeze(2).broadcast_to([P, QT, NCP])

                    def comp_out(h):
                        dve.wait_ge(pv, NCH * g + h + 1)
                        for b in range(2):
                            ins = nc.vector.tensor_tensor(
                                m.OT[:, b::2, h * HD:(h + 1) * HD],
                                m.PS[:, 6 + b, 0:KVW].rearrange("p (t d) -> p t d", d=HD),
                                m.gates[:, b::2, bass.ds(HPG * g + h, 1)].broadcast_to([P, QT // 2, HD]), ALU.mult)
                        ins.then_inc(o_free, 1)

                    for h in range(HPG + 2):
                        if h < HPG:
                            t = m.T[:, h % 2, 0:HALF].rearrange("p (t n) -> p t n", n=NCP)
                            seq = NS * g + SEQ_OF["c", h]
                            dve.wait_ge(s_ready, seq + 1)
                            if h >= 2:
                                dve.wait_ge(pt_t, NCH * g + h - 1)
                            nc.vector.scalar_tensor_tensor(
                                out=m.T[:, h % 2, 0:HALF], in0=m.DISTC[:].rearrange("p t n -> p (t n)"),
                                scalar=m.slopes[:, bass.ds(HPG * g + h, 1)], in1=m.PS[:, 2 * (SEQ_OF["c", h] % 2), :],
                                op0=ALU.mult, op1=ALU.add).then_inc(s_free, 1)
                            dve.wait_ge(s_free, seq + 3)
                            link(nc.vector.tensor_reduce(m.MX[:, h % 2, :], t, AX.X, ALU.max))
                            nc.vector.tensor_tensor(t, t, over_heads(m.MX[:, h % 2, :]), ALU.subtract).then_inc(c_sub, 1)
                        if 1 <= h <= HPG:
                            k = h - 1
                            t = m.T[:, k % 2, 0:HALF].rearrange("p (t n) -> p t n", n=NCP)
                            den = m.DEN[:, k % 2, :]
                            dve.wait_ge(c_exp, HPG * g + k + 1)
                            link(nc.vector.tensor_reduce(den, t, AX.X, ALU.add))
                            link(nc.vector.reciprocal(den, den))
                            link(nc.vector.tensor_tensor(den[:, 0:1], den[:, 0:1], m.SOME[:, 0:1], ALU.mult))
                            nc.vector.tensor_tensor(t, t, over_heads(den), ALU.mult).then_inc(c_p, 1)
                            dve.wait_ge(c_p, HPG * g + k + 1)
                            if k == 0:
                                link(nc.vector.tensor_copy(m.PG[:], t))
                            else:
                                link(nc.vector.tensor_tensor(m.PG[:], m.PG[:], t, ALU.add))
                        if h >= 2:
                            comp_out(h - 2)

                    v = m.PG[:, QT // 2:QT, :].rearrange("p t (j r) -> p t j r", r=4)
                    imp = m.IMP[:]
                    link(nc.vector.tensor_tensor(imp, v[:, :, :, 0], v[:, :, :, 1], ALU.add))
                    link(nc.vector.tensor_tensor(imp, imp, v[:, :, :, 2], ALU.add))
                    link(nc.vector.scalar_tensor_tensor(out=imp, in0=imp, scalar=2.0, in1=v[:, :, :, 3],
                                                        op0=ALU.mult, op1=ALU.add))
                    link(nc.vector.tensor_tensor(imp[:, :, 1:], imp[:, :, 1:], v[:, :, 0:NBLK - 1, 3], ALU.add))
                    link(nc.vector.tensor_tensor(imp, imp, m.FORCED[:], ALU.add))
                    dve.wait_ge(pt_t, NCH * g + HPG)
                    QH = QT // 2
                    gt = m.T[:, 0, :].rearrange("p (t j i) -> p t j i", t=QH, j=NBLK)
                    eq = m.T[:, 1, :].rearrange("p (t j i) -> p t j i", t=QH, j=NBLK)
                    for q in range(QH):
                        ii = imp[:, q, :].unsqueeze(1).broadcast_to([P, NBLK, NBLK])
                        jj = imp[:, q, :].unsqueeze(2).broadcast_to([P, NBLK, NBLK])
                        nc.vector.tensor_tensor(gt[:, q], ii, jj, ALU.is_gt)
                        ins = nc.vector.tensor_tensor(eq[:, q], ii, jj, ALU.is_equal)
                    link(ins)
                    for q in range(QH):
                        ins = nc.vector.tensor_tensor(eq[:, q], eq[:, q], m.LOWER[:], ALU.mult)
                    link(ins)
                    link(nc.vector.tensor_tensor(m.T[:, 0, :], m.T[:, 0, :], m.T[:, 1, :], ALU.add))
                    link(nc.vector.tensor_reduce(m.RANK[:], gt, AX.X, ALU.add))
                    nc.vector.tensor_scalar(m.RANK[:], m.RANK[:], float(N_SEL), -BIG, ALU.is_ge, ALU.mult).then_inc(mk, 1)

                    def combine(h):
                        dve.wait_ge(pv, NCH * g + FIRST_CHUNK[UPH * (h + 1)])
                        dve.wait_ge(p_r, NU * g + UPH * (h + 1))
                        link(nc.vector.reciprocal(m.REC[:], m.SUM[:, h % 2, :, :]))
                        gate = m.gates[:].rearrange("p t (b h) -> p b t h", b=BRANCHES)[
                            :, 1:3, :, bass.ds(HPG * g + h, 1)].rearrange("p b t h -> p b (t h)")
                        link(nc.vector.tensor_tensor(m.REC[:], m.REC[:], gate, ALU.mult))
                        ot = m.OT[:, :, h * HD:(h + 1) * HD]
                        for b in range(2):
                            rec = m.REC[:, b, :].unsqueeze(2).broadcast_to([P, QT, HD])
                            link(nc.vector.tensor_tensor(m.TO[:], m.PS[:, 6 + b, :].rearrange("p (t d) -> p t d", d=HD),
                                                         rec, ALU.mult))
                            ins = nc.vector.tensor_tensor(ot, ot, m.TO[:], ALU.add)
                            if b == 0:
                                link(ins)
                        ins.then_inc(o_free, 1)

                    for u in range(NU + 1):
                        if u < NU:
                            h, q, b = UNITS[u]
                            a, e = unit_tiles(u)
                            n = (e - a) * P
                            s = SEQ_OF["u", u]
                            bias = m.BW[:, h % 2, WIN + P - n:] if b else m.BS[:, h % 2, SEQ - n:]
                            if u % UPH == 0:
                                dve.wait_ge(b_r, HPG * g + h + 1)
                            dve.wait_ge(s_ready, NS * g + s + 1)
                            if u >= 2:
                                dve.wait_ge(pt_t, NCH * g + FIRST_CHUNK[u - 1])
                            else:
                                dve.wait_ge(mk, g + 1)
                            dve.sem_inc(begun, 1)
                            nc.vector.tensor_tensor_reduce(m.T[:, u % 2, 0:n], strip_psum(m, s % 2)[:, 0:n], bias, -1.0,
                                                           3e38, ALU.add, ALU.min, m.NM[:, h % 2, b, q:q + 1]
                                                           ).then_inc(s_free, 1)
                        if u >= 1:
                            for c in range(FIRST_CHUNK[u - 1], FIRST_CHUNK[u]):
                                if on_dve(c):
                                    dve.wait_ge(pt_t, NCH * g + c + 1)
                                    dve.wait_ge(pv, NCH * g + c - 1)
                                    nc.vector.tensor_copy(m.PT[:, c % 2, :], ptslot(c)).then_inc(ev_d, 1)
                            if u % UPH == 0:
                                combine(u // UPH - 1)
                        if u in (2 * UPH + 2, NU):
                            pair = 1 if u == NU else 0
                            s = SEQ_OF["o", pair]
                            dve.wait_ge(s_ready, NS * g + s + 1)
                            nc.vector.tensor_copy(row(m.proj, 2 * g + pair), strip_psum(m, s % 2)).then_inc(s_free, 1)
                    assert links == CHAIN, links

        @block.tensor
        def _(pe):
            pe.wait_ge(ind_r, 1)
            with pe.Fori(0, GROUPS // 2) as j:
                for gi in range(2):
                    g = 2 * j + gi

                    def wait_bank(c):
                        if c >= 2:
                            pe.wait_ge(ev_d if on_dve(c - 2) else ev_a,
                                       (NCH_D if on_dve(c - 2) else NCH_A) * g + done_before(c - 2))
                        else:
                            pe.wait_ge(ev_a, NCH_A * g)
                            pe.wait_ge(ev_d, NCH_D * g)

                    def wait_kept(c):
                        pe.wait_ge(ev_d if on_dve(c) else ev_a, (NCH_D if on_dve(c) else NCH_A) * g + done_before(c))

                    def comp_scores(h):
                        s = SEQ_OF["c", h]
                        pe.wait_ge(st_l, (2 + HPG) * g + 3 + h)
                        pe.wait_ge(s_free, NS * g + s + 1)
                        for q in range(QT):
                            out = m.PS[:, 2 * (s % 2), q * NCP:(q + 1) * NCP]
                            nc.tensor.matmul(out, m.Q1[:, h, q * P:(q + 1) * P],
                                             m.KC1[:, bass.ds(g, 1), :].rearrange("p a n -> p (a n)"), start=True, stop=False)
                            last = nc.tensor.matmul(out, m.Q1[0:HD, h, q * P:(q + 1) * P],
                                                    m.KC2[0:HD, bass.ds(g, 1), :].rearrange("p a n -> p (a n)"),
                                                    start=False, stop=True)
                        last.then_inc(s_ready, 1)

                    def comp_values(h):
                        pe.wait_ge(c_p, HPG * g + h + 1)
                        wait_bank(h)
                        for k in range(4):
                            last = nc.tensor.transpose(ptslot(h)[:, k * P:(k + 1) * P], m.T[:, h % 2, k * P:(k + 1) * P],
                                                       m.ident[:])
                        last.then_inc(pt_t, 1)
                        wait_kept(h)
                        pe.wait_ge(o_free, 2 * HPG * g + h)
                        for q in range(QT):
                            r = slice(HD * (q % 2), HD * (q % 2) + HD)
                            last = nc.tensor.matmul(m.PS[:, 6 + q % 2, (q // 2) * HD:(q // 2) * HD + HD],
                                                    m.PT[r, h % 2, (q // 2) * P:(q // 2) * P + P],
                                                    m.VCG[r, :],
                                                    start=True, stop=True)
                        last.then_inc(pv, 1)

                    def scores(u):
                        h, q, b = UNITS[u]
                        a, e = unit_tiles(u)
                        s = SEQ_OF["u", u]
                        if u == 0:
                            pe.wait_ge(q2m, HPG * g + HPG)
                        pe.wait_ge(s_free, NS * g + s + 1)
                        k1, k2 = (m.KW1, m.KW2) if b else (m.KS1, m.KS2)
                        rows, q2 = (HD, m.Q1[0:HD, h, q * P:(q + 1) * P])
                        if not b and q >= QT // 2:
                            rows, q2 = HD + NBLK, m.Q2[0:HD + NBLK, h, (q - QT // 2) * P:(q - QT // 2 + 1) * P]
                        for n in range(a * P, e * P, HALF):
                            end = min(n + HALF, e * P)
                            out = strip_psum(m, s % 2)[:, n - a * P:end - a * P]
                            nc.tensor.matmul(out, m.Q1[:, h, q * P:(q + 1) * P], k1[:, n:end], start=True, stop=False)
                            last = nc.tensor.matmul(out, q2, k2[0:rows, n:end], start=False, stop=True)
                        last.then_inc(s_ready, 1)

                    def values(u, k):
                        h, q, b = UNITS[u]
                        a, e = unit_tiles(u)
                        c = FIRST_CHUNK[u] + k
                        t0, t1 = CHUNKS[u][k]
                        wait_kept(c)
                        if u % UPH == 0 and k == 0:
                            pe.wait_ge(o_free, 2 * HPG * g + HPG + h)
                        v = m.VW if b else m.VS
                        for t in range(t0, t1):
                            last = nc.tensor.matmul(m.PS[:, 6 + b, q * HD:(q + 1) * HD],
                                                    m.PT[:, c % 2, (t - t0) * P:(t - t0 + 1) * P],
                                                    v[:, t, bass.ds(HD * g, HD)], start=(t == a), stop=(t == e - 1))
                        last.then_inc(pv, 1)

                    def turn(u, k):
                        a, e = unit_tiles(u)
                        c = FIRST_CHUNK[u] + k
                        t0, t1 = CHUNKS[u][k]
                        wait_bank(c)
                        for t in range(t0, t1):
                            last = nc.tensor.transpose(ptslot(c)[:, (t - t0) * P:(t - t0 + 1) * P],
                                                       m.T[:, u % 2, (t - a) * P:(t - a + 1) * P], m.ident[:])
                        last.then_inc(pt_t, 1)

                    def turn_out(pair):
                        s = SEQ_OF["o", pair]
                        pe.wait_ge(o_free, 2 * HPG * g + HPG + 2 * pair + 2)
                        pe.wait_ge(s_free, NS * g + s + 1)
                        for q in range(QT):
                            last = nc.tensor.transpose(strip_psum(m, s % 2)[:, q * P:(q + 1) * P],
                                                       m.OT[:, q, pair * P:(pair + 1) * P], m.ident[:])
                        last.then_inc(s_ready, 1)

                    for h in range(HPG + 1):
                        if h < HPG:
                            comp_scores(h)
                        if h >= 1:
                            comp_values(h - 1)
                    pe.wait_ge(mk, g + 1)
                    for q in range(QT // 2):
                        last = nc.tensor.transpose(m.PS[0:NBLK, 7, q * P:(q + 1) * P], m.RANK[:, q, :], m.ident[:])
                    last.then_inc(mk_t, 1)
                    scores(0)
                    before = None
                    for u in range(NU):
                        if u + 1 < NU:
                            scores(u + 1)
                        if u == 2 * UPH + 1:
                            turn_out(0)
                        pe.wait_ge(p_r, NU * g + u + 1)
                        for k in range(len(CHUNKS[u])):
                            turn(u, k)
                            if before:
                                values(*before)
                            before = (u, k)
                    values(*before)
                    turn_out(1)


SB_UNITS = [(h, q) for h in range(2) for q in range(QT)]
SB_NU = len(SB_UNITS)
SB_CHUNKS = [[(k, min(k + 4, QT)) for k in range(QT - 1 - q, QT, 4)] for _, q in SB_UNITS]
SB_FIRST = [2 + sum(len(c) for c in SB_CHUNKS[:u]) for u in range(SB_NU + 1)]
SB_NV = SB_FIRST[-1] - 2
SB_NCH = SB_FIRST[-1] + 2
assert SB_NCH % 2 == 0


def sb_on_dve(c):
    return 2 <= c < SB_NCH - 2 and c % 4 == 1


SB_NCH_D = sum(sb_on_dve(c) for c in range(SB_NCH))
SB_NCH_A = SB_NCH - SB_NCH_D


def sb_done(c):
    return sum(sb_on_dve(k) == sb_on_dve(c) for k in range(c + 1))


def stick_breaking(nc, m, w_in):
    t = SEQ * 4
    o = m.big + 8 * t
    q1 = m.at("sq1", o, [P, 2, SEQ], F32R); o += 2 * t
    k1 = m.at("sk1", o, [P, 2, SEQ], F32R); o += 2 * t
    klo = m.at("sklo", o, [P, SEQ], F32R); o += t
    vtok = m.at("svtok", o, [P, QT, P]); o += t
    keep = m.at("skeep", o, [P, SEQ]); o += t
    beta = m.at("sbeta", o, [P, 2, SEQ]); o += 2 * t
    ot = m.at("sot", o, [P, QT, P]); o += t
    prod = m.at("sprod", o, [P, SEQ + 8]); o += t + 32
    assert o <= m.small
    pt = m.at("spt", m.small_end, [P, 2, HALF])
    assert m.small_end + 2 * HALF * 4 <= 229368
    st = Strips(nc, m, "s")
    hi, qkv, vst, z_r, z_free, sel, scn, a_r, pt_t, ev_a, ev_d, pv, o_c, one, begun = sems(
        nc, "s", "stackhigh", "stacklow", "vstaged", "zready", "zfree", "selected", "scanned", "aready", "turned",
        "evact", "evdve", "pv", "ocopied", "one", "begun")
    PAIRS = HEADS // 2
    pairs = KT

    def ptslot(c):
        return m.PS[:, 4 + c % 2, :]

    def own(h):
        return slice(HD * h, HD * h + HD)

    def other(h):
        return slice(HD - HD * h, 2 * HD - HD * h)

    with nc.Block() as block:
        @block.sync
        def _(sp):
            with sp.Fori(0, PAIRS) as j:
                for n, slot in enumerate((0, 1, 0)):
                    sp.wait_ge(st.low, 3 * j + (n == 2))
                    sp.dma_start(m.W32[:, slot], strip_of(w_in, j + n * pairs)).then_inc(st.loaded[slot], 16)

        @block.scalar
        def _(act):
            def split(j, n):
                slot = n % 2
                act.wait_ge(st.loaded[slot], 16 * (j + 1) if slot else 16 * (2 * j + n // 2 + 1))
                act.wait_ge(st.multiplied, 3 * j + (n == 2))
                nc.scalar.copy(m.WHI[:, slot], m.W32[:, slot]).then_inc(st.high, 1)

            def evacuate(j, c):
                act.wait_ge(pt_t, SB_NCH * j + c + 1)
                if c < 2:
                    dst = vtok[:, 4 * c:4 * c + 4, :].rearrange("p t d -> p (t d)")
                elif c >= SB_NCH - 2:
                    half = c - (SB_NCH - 2)
                    dst = row(m.proj, j)[:, half * HALF:half * HALF + HALF]
                else:
                    act.wait_ge(pv, SB_NV * j + max(c - 3, 0))
                    dst = pt[:, c % 2, :]
                nc.scalar.copy(dst, ptslot(c)).then_inc(ev_a, 1)

            def pair(j, last):
                for n in range(2):
                    act.wait_ge(st.multiplied, 3 * j + n + 1)
                    for h in range(2):
                        dst = q1 if n == 0 else k1
                        dst = dst[own(h), h, :] if n == 0 else dst[own(h), h, ::-1]
                        nc.scalar.activation(dst, strip_psum(m, n)[own(h)], ACT.Copy,
                                             scale=QSCALE if n == 0 else 1.0).then_inc(hi, 1)
                    if n == 0:
                        split(j, 2)
                act.wait_ge(hi, 4 * j + 4)
                for h in range(2):
                    ins = nc.scalar.copy(k1[other(h), h, :], k1[own(h), h, :].bitcast(F32))
                ins.then_inc(vst, 1)
                act.wait_ge(st.multiplied, 3 * j + 3)
                act.wait_ge(scn, SB_NU * j)
                nc.scalar.copy(keep[:, ::-1], strip_psum(m, 0)).then_inc(vst, 1)
                for c in range(2):
                    evacuate(j, c)
                for u in range(SB_NU + 1):
                    if u < SB_NU:
                        h, q = SB_UNITS[u]
                        n = (q + 1) * P
                        z = strip_psum(m, (u + 1) % 2)[:, 0:n]
                        act.wait_ge(z_r, SB_NU * j + u + 1)
                        act.wait_ge(scn, SB_NU * j + u)
                        nc.scalar.activation(keep[:, 0:n], z, ACT.Sigmoid, scale=-1.0)
                        act.wait_ge(pt_t, SB_NCH * j + SB_FIRST[max(u - 1, 0)])
                        nc.scalar.activation(beta[:, u % 2, 0:n], z, ACT.Sigmoid).then_inc(z_free, 1)
                    if u >= 1:
                        for c in range(SB_FIRST[u - 1], SB_FIRST[u]):
                            if not sb_on_dve(c):
                                evacuate(j, c)
                    if u == SB_NU - 4 and not last:
                        for n in range(2):
                            split(j + 1, n)
                for c in range(SB_NCH - 2, SB_NCH):
                    evacuate(j, c)

            for n in range(2):
                split(0, n)
            with act.Fori(0, PAIRS - 1) as j:
                pair(j, False)
            pair(PAIRS - 1, True)

        @block.gpsimd
        def _(pool):
            with pool.Fori(0, PAIRS) as j:
                for u in range(SB_NU):
                    pool.wait_ge(z_free, SB_NU * j + u + 1)
                    pool.sem_inc(begun, 1)
                    for x, fill in ((keep[:, 0:P], 1.0), (beta[:, u % 2, 0:P], 0.0)):
                        nc.gpsimd.affine_select(out=x, in_=x, compare_op=ALU.is_gt, fill=fill, base=1 - P,
                                                pattern=[[1, P]], channel_multiplier=1).then_inc(sel, 1)

        @block.vector
        def _(dve):
            def split(j, n):
                dve.wait_ge(st.high, 3 * j + n + 1)
                nc.vector.tensor_tensor(m.WLO[:, n % 2], m.W32[:, n % 2], m.WHI[:, n % 2].bitcast(F32),
                                        ALU.subtract).then_inc(st.low, 1)

            def pair(j, last):
                for n in range(2):
                    for h in range(2):
                        dve.wait_ge(hi, 4 * j + 2 * n + h + 1)
                        src = strip_psum(m, n)[own(h)]
                        if n == 0:
                            ins = nc.vector.scalar_tensor_tensor(
                                out=q1[other(h), h, :], in0=src, scalar=QSCALE, in1=q1[own(h), h, :].bitcast(F32),
                                op0=ALU.mult, op1=ALU.subtract)
                        else:
                            ins = nc.vector.tensor_tensor(klo[own(h), ::-1], src, k1[own(h), h, ::-1].bitcast(F32),
                                                          ALU.subtract)
                    ins.then_inc(qkv, 1)
                    if n == 0:
                        split(j, 2)
                for u in range(SB_NU + 1):
                    if u < SB_NU:
                        h, q = SB_UNITS[u]
                        n = (q + 1) * P
                        b = beta[:, u % 2, 0:n]
                        dve.wait_ge(sel, 2 * (SB_NU * j + u + 1))
                        dve.wait_ge(a_r, SB_NU * j + u)
                        nc.vector.tensor_tensor_scan(prod[:, 1:n + 1], keep[:, 0:n], keep[:, 0:n], 1.0,
                                                     ALU.mult, ALU.bypass).then_inc(scn, 1)
                        dve.wait_ge(scn, SB_NU * j + u + 1)
                        nc.vector.tensor_tensor(b, b, prod[:, 0:n], ALU.mult).then_inc(a_r, 1)
                    if u >= 1:
                        for c in range(SB_FIRST[u - 1], SB_FIRST[u]):
                            if sb_on_dve(c):
                                dve.wait_ge(pt_t, SB_NCH * j + c + 1)
                                dve.wait_ge(pv, SB_NV * j + c - 3)
                                nc.vector.tensor_copy(pt[:, c % 2, :], ptslot(c)).then_inc(ev_d, 1)
                    if u in (QT + 1, SB_NU):
                        h = 0 if u <= QT + 1 else 1
                        dve.wait_ge(pv, SB_NV * j + SB_NV // 2 * (h + 1))
                        dve.wait_ge(pt_t, SB_NCH * j)
                        nc.vector.tensor_copy(ot[:, :, h * HD:(h + 1) * HD],
                                              m.PS[:, 6 + h, :].rearrange("p (t d) -> p t d", d=HD)).then_inc(o_c, 1)
                    if u == SB_NU - 4 and not last:
                        for n in range(2):
                            split(j + 1, n)

            nc.vector.memset(prod[:, 0:1], 1.0).then_inc(one, 1)
            dve.wait_ge(one, 1)
            for n in range(2):
                split(0, n)
            with dve.Fori(0, PAIRS - 1) as j:
                pair(j, False)
            pair(PAIRS - 1, True)

        @block.tensor
        def _(pe):
            with pe.Fori(0, PAIRS) as j:
                def wait_bank(c):
                    if c >= 2:
                        pe.wait_ge(ev_d if sb_on_dve(c - 2) else ev_a,
                                   (SB_NCH_D if sb_on_dve(c - 2) else SB_NCH_A) * j + sb_done(c - 2))
                    else:
                        pe.wait_ge(ev_a, SB_NCH_A * j)
                        pe.wait_ge(ev_d, SB_NCH_D * j)

                def wait_kept(c):
                    pe.wait_ge(ev_d if sb_on_dve(c) else ev_a, (SB_NCH_D if sb_on_dve(c) else SB_NCH_A) * j + sb_done(c))

                def scores(u):
                    h, q = SB_UNITS[u]
                    if u == 0:
                        pe.wait_ge(qkv, 2 * j + 2)
                        pe.wait_ge(vst, 2 * j + 1)
                    elif u == 1:
                        pe.wait_ge(vst, 2 * j + 2)
                    else:
                        pe.wait_ge(z_free, SB_NU * j + u - 1)
                    for n in range(SEQ - (q + 1) * P, SEQ, HALF):
                        end = min(n + HALF, SEQ)
                        first = SEQ - (q + 1) * P
                        out = strip_psum(m, (u + 1) % 2)[:, n - first:end - first]
                        nc.tensor.matmul(out, q1[:, h, q * P:(q + 1) * P], k1[:, h, n:end], start=True, stop=False)
                        last = nc.tensor.matmul(out, q1[own(h), h, q * P:(q + 1) * P], klo[own(h), n:end],
                                                start=False, stop=True)
                    last.then_inc(z_r, 1)

                def turn(c, tiles):
                    wait_bank(c)
                    for n, x in enumerate(tiles):
                        last = nc.tensor.transpose(ptslot(c)[:, n * P:(n + 1) * P], x, m.ident[:])
                    last.then_inc(pt_t, 1)

                def values(u, k):
                    h, q = SB_UNITS[u]
                    c = SB_FIRST[u] + k
                    t0, t1 = SB_CHUNKS[u][k]
                    wait_kept(c)
                    if u % QT == 0 and k == 0:
                        pe.wait_ge(o_c, 2 * j)
                    for t in range(t0, t1):
                        last = nc.tensor.matmul(m.PS[:, 6 + h, q * HD:(q + 1) * HD], pt[:, c % 2, (t - t0) * P:(t - t0 + 1) * P],
                                                vtok[:, t, own(h)], start=(t == QT - 1 - q), stop=(t == QT - 1))
                    last.then_inc(pv, 1)

                for n, slot in enumerate((0, 1, 0)):
                    pe.wait_ge(st.low, 3 * j + n + 1)
                    if n < 2:
                        pe.wait_ge(z_free, SB_NU * j)
                    else:
                        pe.wait_ge(qkv, 2 * j + 1)
                    strip_products(nc, strip_psum(m, slot), m.WHI[:, slot], m.WLO[:, slot], m.XH, m.XL,
                                   KT).then_inc(st.multiplied, 1)
                scores(0)
                pe.wait_ge(vst, 2 * j + 2)
                for c in range(2):
                    turn(c, [keep[:, t * P:(t + 1) * P] for t in range(4 * c, 4 * c + 4)])
                wait_kept(1)
                before = None
                for u in range(SB_NU):
                    if u + 1 < SB_NU:
                        scores(u + 1)
                    pe.wait_ge(a_r, SB_NU * j + u + 1)
                    for k, (t0, t1) in enumerate(SB_CHUNKS[u]):
                        first = SB_CHUNKS[u][0][0]
                        turn(SB_FIRST[u] + k, [beta[:, u % 2, (t - first) * P:(t - first + 1) * P] for t in range(t0, t1)])
                        if before:
                            values(*before)
                        before = (u, k)
                values(*before)
                pe.wait_ge(o_c, 2 * j + 2)
                for c in range(2):
                    turn(SB_NCH - 2 + c, [ot[:, q, :] for q in range(4 * c, 4 * c + 4)])


def strips(w):
    r, c = w.shape
    return np.ascontiguousarray(w.reshape(r // P, P, c // P, P).transpose(2, 1, 0, 3))


def features_first(a):
    return np.ascontiguousarray(a.T.reshape(KT, P, SEQ).transpose(1, 0, 2))


def build_trunk(nc, x, gains, nsa_in, nsa_gate, gate_b, cmp_w1, cmp_w2, cmp_pe, nsa_out, sb_in, sb_out,
                w1, w3, w2, out):
    m = Memory(nc)
    nsa_memory(m)
    load_input(nc, m, x, gains)
    for layer in range(2):
        held = set(nc.free_semaphores)
        rmsnorm(nc, m, 2 * layer)
        if layer == 0:
            nsa_projection(nc, m, nsa_in, nsa_gate, gate_b)
            nsa_compress(nc, m, cmp_w1, cmp_w2, cmp_pe)
            nsa_attention(nc, m)
            residual_projection(nc, m, "no", nsa_out)
        else:
            stick_breaking(nc, m, sb_in)
            residual_projection(nc, m, "so", sb_out)
        rmsnorm(nc, m, 2 * layer + 1)
        f0 = 0
        for nf in FFN_CHUNKS:
            ffn_chunk(nc, m, f"f{layer}_{f0}", w1[layer], w3[layer], w2[layer], f0, nf)
            f0 += nf
        if layer == 0:
            nc.clear_and_free_semaphores(sorted(held - set(nc.free_semaphores)))
            nc.all_engine_barrier()
    rmsnorm(nc, m, 4, out=out)


def kernel(x, mix_norm_g, ffn_norm_g, final_norm_g, nsa_w_in, nsa_gate_b, nsa_cmp_pe, nsa_cmp_w1, nsa_cmp_w2,
           nsa_w_out, sb_w_in, sb_w_out, ffn_w1, ffn_w3, ffn_w2):
    import concourse.bacc as bacc
    from concourse.bass_utils import run_bass_kernel_spmd

    mix, ffn, final, w_in = (np.asarray(a) for a in (mix_norm_g, ffn_norm_g, final_norm_g, nsa_w_in))
    qkv = NSA_TILES * P
    gains = np.stack([mix[0], ffn[0], mix[1], ffn[1], final])
    arrays = {
        "x": features_first(np.asarray(x)[0]),
        "gains": np.ascontiguousarray(gains.reshape(5, KT, P).transpose(2, 0, 1)),
        "nsa_in": strips(w_in[0][:, :qkv]),
        "nsa_gate": np.ascontiguousarray(w_in[0][:, qkv:].reshape(KT, P, -1).transpose(1, 0, 2)),
        "gate_b": np.ascontiguousarray(np.asarray(nsa_gate_b)[0]),
        "cmp_w1": np.ascontiguousarray(np.asarray(nsa_cmp_w1)[0].reshape(2, 2 * KT, P, HID).transpose(2, 0, 1, 3)),
        "cmp_w2": np.ascontiguousarray(np.asarray(nsa_cmp_w2)[0].reshape(2, 2, P, HD).transpose(2, 0, 1, 3)),
        "cmp_pe": np.ascontiguousarray(np.asarray(nsa_cmp_pe)[0].reshape(2, 2 * KT, P).transpose(2, 0, 1)),
        "nsa_out": strips(np.asarray(nsa_w_out)[0]),
        "sb_in": strips(np.asarray(sb_w_in)[0]),
        "sb_out": strips(np.asarray(sb_w_out)[0]),
        "w1": np.stack([strips(w) for w in np.asarray(ffn_w1)]),
        "w3": np.stack([strips(w) for w in np.asarray(ffn_w3)]),
        "w2": np.stack([strips(w) for w in np.asarray(ffn_w2)]),
    }
    nc = bacc.Bacc("TRN2", target_bir_lowering=False, num_devices=1)
    args = {n: nc.dram_tensor(n, a.shape, mybir.dt.from_np(a.dtype), kind="ExternalInput").ap()
            for n, a in arrays.items()}
    out = nc.dram_tensor("out", (P, KT, SEQ), F32, kind="ExternalOutput").ap()
    build_trunk(nc, out=out, **args)
    r = run_bass_kernel_spmd(nc, [arrays], core_ids=[0])
    got = r.results[0]["out"]
    return np.ascontiguousarray(got.transpose(2, 1, 0)).reshape(1, SEQ, D)
```

```python
import concourse.bass as bass
from concourse import mybir
import numpy as np

F32 = mybir.dt.float32
F32R = mybir.dt.float32r
ACT = mybir.ActivationFunctionType
ALU = mybir.AluOpType
AX = mybir.AxisListType

P = 128
SEQ = 1024
D = 1024
HALF = 512
KT = D // P
QT = SEQ // P
HEADS = 16
HD = D // HEADS
GROUPS = 4
HPG = HEADS // GROUPS
KVW = GROUPS * HD
BRANCHES = 3
CMP_LEN, CMP_STEP = 32, 16
NCP = SEQ // CMP_STEP
NC = NCP - 1
HID = 4 * HD
BLK = 64
NBLK = SEQ // BLK
N_SEL = 8
WIN = 512
WT = WIN // P
D_FF = 2816
FT = D_FF // P
EPS = 1e-6
BIG = 1e30
QSCALE = HD ** -0.5
NSA_TILES = (D + 6 * KVW) // P
FFN_CHUNKS = (8, 8, 6)
assert sum(FFN_CHUNKS) == FT


class Memory:

    def __init__(self, nc):
        self.nc = nc
        tile = SEQ * 4
        self.base = 16512
        self.xr = self.base + KT * tile
        self.st = self.xr + 2 * KT * tile
        self.big = self.st + 6 * tile
        self.small = self.big + NSA_TILES * tile
        at = self.at
        self.H = at("H", self.base, [P, KT, SEQ])
        self.XH = at("XH", self.xr, [P, KT, SEQ], F32R)
        self.XL = at("XL", self.xr + KT * tile, [P, KT, SEQ], F32R)
        self.W32 = at("W32", self.st, [P, 2, KT, P])
        self.WHI = at("WHI", self.st + 2 * tile, [P, 2, KT, P], F32R)
        self.WLO = at("WLO", self.st + 4 * tile, [P, 2, KT, P], F32R)
        o = self.small
        self.ident = at("ident", o, [P, P]); o += P * 4
        self.ones = at("ones", o, [P, P], F32R); o += P * 4
        self.slopes = at("slopes", o, [P, HEADS]); o += HEADS * 4
        self.gains = at("gains", o, [P, 5, KT]); o += 5 * KT * 4
        self.eps = at("eps", o, [P, 8]); o += 32
        self.gates_at = o
        self.gates = at("gates", o, [P, QT, BRANCHES * HEADS]); o += QT * BRANCHES * HEADS * 4
        self.gate_bias = at("gate_bias", o, [P, BRANCHES * HEADS])
        self.proj = at("proj", self.big, [P, NSA_TILES, SEQ])
        self.small_end = o
        self.PS = nc.alloc_psum_tensor("PS", [P, 8, HALF], F32)

    def at(self, name, offset, shape, dt=F32):
        return self.nc.alloc_sbuf_tensor_at(name, shape, dt, offset=offset)


def sems(nc, prefix, *names):
    return [nc.alloc_semaphore(f"{prefix}_{n}") for n in names]


def strip_products(nc, out, whi, wlo, xh, xl, n):
    for k in range(n):
        for w, x in ((whi, xh), (whi, xl), (wlo, xh)):
            for half in range(2):
                cols = slice(half * HALF, half * HALF + HALF)
                last = nc.tensor.matmul(out[:, cols], w[:, k, :], x[:, k, cols],
                                        start=(k == 0 and w is whi and x is xh),
                                        stop=(k == n - 1 and w is wlo))
    return last


def strip_psum(m, slot):
    return m.PS[:, 2 * slot:2 * slot + 2, :].rearrange("p a n -> p (a n)")


def load_input(nc, m, x, gains):
    ones32 = m.at("ones32", m.big, [P, P])
    loaded, made, rounded = sems(nc, "in", "loaded", "made", "rounded")
    with nc.Block() as block:
        @block.sync
        def _(sp):
            sp.dma_start(m.gains[:], gains).then_inc(loaded, 16)
            for k in range(0, KT, 2):
                sp.dma_start(m.H[:, k:k + 2, :], x[:, k:k + 2, :]).then_inc(loaded, 16)
            sp.wait_ge(loaded, 16 * (1 + KT // 2))

        @block.gpsimd
        def _(pool):
            nc.gpsimd.memset(m.ident[:], 0.0).then_inc(made, 1)
            pool.wait_ge(made, 1)
            nc.gpsimd.affine_select(out=m.ident[:], in_=m.ident[:], compare_op=ALU.not_equal, fill=1.0,
                                    base=0, pattern=[[-1, P]], channel_multiplier=1).then_inc(made, 1)
            nc.gpsimd.memset(ones32[:], 1.0).then_inc(made, 1)
            nc.gpsimd.memset(m.eps[:], EPS).then_inc(made, 1)
            for h in range(HEADS):
                slope = float(np.float32(2.0 ** (-8.0 * (h + 1) / HEADS)))
                nc.gpsimd.memset(m.slopes[:, h:h + 1], slope).then_inc(made, 1)
            pool.wait_ge(made, 4 + HEADS)

        @block.vector
        def _(dve):
            dve.wait_ge(made, 3)
            nc.vector.tensor_copy(m.ones[:], ones32[:]).then_inc(rounded, 1)
            dve.wait_ge(rounded, 1)


def rmsnorm(nc, m, n, out=None):
    t = SEQ * 4
    sq = m.at(f"sq{n}", m.big, [P, 2, SEQ])
    sqh = m.at(f"sqh{n}", m.big + 2 * t, [P, 2, SEQ], F32R)
    sql = m.at(f"sql{n}", m.big + 4 * t, [P, 2, SEQ], F32R)
    lnv = m.at(f"lnv{n}", m.big + 6 * t, [P, SEQ])
    rstd = m.at(f"rstd{n}", m.big + 7 * t, [P, SEQ])
    y = m.at(f"y{n}", m.big + 8 * t, [P, 2, SEQ])
    squared, hi, lo, summed, rs, yv, yh, yl, stored = sems(
        nc, f"n{n}", "squared", "hi", "lo", "summed", "rstd", "y", "yh", "yl", "stored")
    with nc.Block() as block:
        @block.scalar
        def _(act):
            for k in range(KT):
                if k >= 2:
                    act.wait_ge(lo, k - 1)
                nc.scalar.activation(sq[:, k % 2, :], m.H[:, k, :], ACT.Square).then_inc(squared, 1)
                if k >= 2:
                    act.wait_ge(summed, k - 1)
                act.wait_ge(squared, k + 1)
                nc.scalar.copy(sqh[:, k % 2, :], sq[:, k % 2, :]).then_inc(hi, 1)
            act.wait_ge(summed, KT)
            nc.scalar.activation(lnv[:], strip_psum(m, 0), ACT.Ln, bias=m.eps[:, 0:1], scale=1.0 / D).then_inc(rs, 1)
            act.wait_ge(rs, 1)
            nc.scalar.activation(rstd[:], lnv[:], ACT.Exp, scale=-0.5).then_inc(rs, 1)
            if out is None:
                for k in range(KT):
                    act.wait_ge(yv, k + 1)
                    nc.scalar.copy(m.XH[:, k, :], y[:, k % 2, :]).then_inc(yh, 1)

        @block.vector
        def _(dve):
            def low_part(k):
                dve.wait_ge(yh, k + 1)
                nc.vector.tensor_tensor(m.XL[:, k, :], y[:, k % 2, :], m.XH[:, k, :].bitcast(F32),
                                        ALU.subtract).then_inc(yl, 1)

            for k in range(KT):
                if k >= 2:
                    dve.wait_ge(summed, k - 1)
                dve.wait_ge(hi, k + 1)
                nc.vector.tensor_tensor(sql[:, k % 2, :], sq[:, k % 2, :], sqh[:, k % 2, :].bitcast(F32),
                                        ALU.subtract).then_inc(lo, 1)
            dve.wait_ge(rs, 2)
            for k in range(KT):
                dst = m.H[:, k, :] if out is not None else y[:, k % 2, :]
                if k >= 2 and out is None:
                    dve.wait_ge(yl, k - 1)
                nc.vector.scalar_tensor_tensor(out=dst, in0=m.H[:, k, :], scalar=m.gains[:, n, k:k + 1],
                                               in1=rstd[:], op0=ALU.mult, op1=ALU.mult).then_inc(yv, 1)
                if out is None and k >= 1:
                    low_part(k - 1)
            if out is None:
                low_part(KT - 1)

        @block.tensor
        def _(pe):
            for k in range(KT):
                pe.wait_ge(lo, k + 1)
                for part in (sqh, sql):
                    for half in range(2):
                        cols = slice(half * HALF, half * HALF + HALF)
                        last = nc.tensor.matmul(strip_psum(m, 0)[:, cols], m.ones[:], part[:, k % 2, cols],
                                                start=(k == 0 and part is sqh), stop=(k == KT - 1 and part is sql))
                last.then_inc(summed, 1)

        if out is not None:
            @block.sync
            def _(sp):
                for k in range(KT):
                    sp.wait_ge(yv, k + 1)
                    sp.dma_start(out[:, k, :], m.H[:, k, :]).then_inc(stored, 16)
                sp.wait_ge(stored, 16 * KT)


class Strips:

    def __init__(self, nc, m, tag):
        self.nc, self.m = nc, m
        self.loaded = sems(nc, tag, "loaded0", "loaded1")
        self.high, self.low, self.multiplied, self.drained = sems(nc, tag, "high", "low", "multiplied", "drained")

    def load(self, sp, s, slot, src, n=KT, cols=P):
        sp.wait_ge(self.low, s + 1)
        sp.dma_start(self.m.W32[:, slot, 0:n, 0:cols], src).then_inc(self.loaded[slot], 16)

    def split_high(self, act, s, slot, rounds, n=KT, cols=P):
        act.wait_ge(self.loaded[slot], rounds * 16)
        act.wait_ge(self.multiplied, s + 1)
        self.nc.scalar.copy(self.m.WHI[:, slot, 0:n, 0:cols], self.m.W32[:, slot, 0:n, 0:cols]).then_inc(self.high, 1)

    def split_low(self, dve, s, slot, n=KT, cols=P):
        dve.wait_ge(self.high, s + 1)
        self.nc.vector.tensor_tensor(self.m.WLO[:, slot, 0:n, 0:cols], self.m.W32[:, slot, 0:n, 0:cols],
                                     self.m.WHI[:, slot, 0:n, 0:cols].bitcast(F32), ALU.subtract).then_inc(self.low, 1)

    def multiply(self, pe, s, slot, xh, xl, n=KT):
        pe.wait_ge(self.low, s + 3)
        strip_products(self.nc, strip_psum(self.m, slot), self.m.WHI[:, slot], self.m.WLO[:, slot],
                       xh, xl, n).then_inc(self.multiplied, 1)


def strip_of(w, s, n=KT, k0=0):
    return w[bass.ds(s, 1), :, k0:k0 + n, :].rearrange("a p k c -> (a p) k c")


def row(t, i):
    return t[:, bass.ds(i, 1), :].rearrange("p a n -> p (a n)")


def nsa_projection(nc, m, w_in, w_gate, gate_b):
    st = Strips(nc, m, "ni")
    biased, gated, bias_loaded = sems(nc, "ni", "biased", "gated", "bias")
    GC = BRANCHES * HEADS
    N = NSA_TILES
    with nc.Block() as block:
        @block.sync
        def _(sp):
            sp.dma_start(m.gate_bias[:], gate_b.partition_broadcast(P)).then_inc(bias_loaded, 16)
            with sp.Fori(0, N // 2) as i:
                for slot in range(2):
                    st.load(sp, 2 * i + slot, slot, strip_of(w_in, 2 * i + slot))
            st.load(sp, N, 0, w_gate, cols=GC)

        @block.scalar
        def _(act):
            with act.Fori(0, N // 2) as i:
                for slot in range(2):
                    st.split_high(act, 2 * i + slot, slot, i + 1)
            st.split_high(act, N, 0, N // 2 + 1, cols=GC)
            act.wait_ge(biased, 1)
            nc.scalar.activation(m.gates[:], m.gates[:], ACT.Sigmoid).then_inc(gated, 1)

        @block.vector
        def _(dve):
            def drain(s, slot):
                dve.wait_ge(st.multiplied, s + 3)
                nc.vector.tensor_copy(row(m.proj, s), strip_psum(m, slot)).then_inc(st.drained, 1)

            dve.sem_inc(st.low, 2)
            dve.sem_inc(st.drained, 2)
            for slot in range(2):
                st.split_low(dve, slot, slot)
            with dve.Fori(0, N // 2 - 1) as i:
                for slot in range(2):
                    drain(2 * i + slot, slot)
                    st.split_low(dve, 2 * i + slot + 2, slot)
            drain(N - 2, 0)
            st.split_low(dve, N, 0, cols=GC)
            drain(N - 1, 1)
            dve.wait_ge(st.multiplied, N + 3)
            dve.wait_ge(bias_loaded, 16)
            for t in range(QT):
                last = nc.vector.tensor_tensor(m.gates[:, t, :], m.PS[:, 0, t * GC:(t + 1) * GC],
                                               m.gate_bias[:], ALU.add)
            last.then_inc(biased, 1)

        @block.tensor
        def _(pe):
            pe.sem_inc(st.multiplied, 2)
            with pe.Fori(0, N // 2) as i:
                for slot in range(2):
                    pe.wait_ge(st.drained, 2 * i + slot + 1)
                    st.multiply(pe, 2 * i + slot, slot, m.XH, m.XL)
            pe.wait_ge(st.low, N + 3)
            pe.wait_ge(st.drained, N + 1)
            for t in range(QT):
                rows = slice(t * P, (t + 1) * P)
                for k in range(KT):
                    for x, w in ((m.XH, m.WHI), (m.XL, m.WHI), (m.XH, m.WLO)):
                        last = nc.tensor.matmul(m.PS[:, 0, t * GC:(t + 1) * GC], x[:, k, rows], w[:, 0, k, 0:GC],
                                                start=(k == 0 and w is m.WHI and x is m.XH),
                                                stop=(k == KT - 1 and w is m.WLO))
            last.then_inc(st.multiplied, 1)


def add_residual(nc, m, st, dve, tile, slot, s):
    dve.wait_ge(st.multiplied, s + 3)
    nc.vector.tensor_tensor(row(m.H, tile), row(m.H, tile), strip_psum(m, slot), ALU.add).then_inc(st.drained, 1)


def residual_projection(nc, m, tag, w):
    st = Strips(nc, m, tag)
    oh, ol = sems(nc, tag, "oh", "ol")
    with nc.Block() as block:
        @block.sync
        def _(sp):
            with sp.Fori(0, KT // 2) as i:
                for slot in range(2):
                    st.load(sp, 2 * i + slot, slot, strip_of(w, 2 * i + slot))

        @block.scalar
        def _(act):
            for k in range(KT):
                nc.scalar.copy(m.XH[:, k, :], m.proj[:, k, :]).then_inc(oh, 1)
            with act.Fori(0, KT // 2) as i:
                for slot in range(2):
                    st.split_high(act, 2 * i + slot, slot, i + 1)

        @block.vector
        def _(dve):
            dve.sem_inc(st.low, 2)
            dve.sem_inc(st.drained, 2)
            for k in range(KT):
                dve.wait_ge(oh, k + 1)
                nc.vector.tensor_tensor(m.XL[:, k, :], m.proj[:, k, :], m.XH[:, k, :].bitcast(F32),
                                        ALU.subtract).then_inc(ol, 1)
            for slot in range(2):
                st.split_low(dve, slot, slot)
            with dve.Fori(0, KT // 2 - 1) as i:
                for slot in range(2):
                    add_residual(nc, m, st, dve, 2 * i + slot, slot, 2 * i + slot)
                    st.split_low(dve, 2 * i + slot + 2, slot)
            for slot in range(2):
                add_residual(nc, m, st, dve, KT - 2 + slot, slot, KT - 2 + slot)

        @block.tensor
        def _(pe):
            pe.sem_inc(st.multiplied, 2)
            pe.wait_ge(ol, KT)
            with pe.Fori(0, KT // 2) as i:
                for slot in range(2):
                    pe.wait_ge(st.drained, 2 * i + slot + 1)
                    st.multiply(pe, 2 * i + slot, slot, m.XH, m.XL)


def ffn_chunk(nc, m, tag, w1, w3, w2, f0, nf):
    t = SEQ * 4
    mh = m.at(f"mh{tag}", m.big, [P, 8, SEQ], F32R)
    ml = m.at(f"ml{tag}", m.big + 8 * t, [P, 8, SEQ], F32R)
    sil = m.at(f"sil{tag}", m.big + 16 * t, [P, SEQ])
    prod = m.at(f"prod{tag}", m.big + 17 * t, [P, SEQ])
    st = Strips(nc, m, tag)
    silu, mul, mhi, mlo = sems(nc, tag, "silu", "mul", "mhi", "mlo")
    N1 = 2 * nf
    with nc.Block() as block:
        @block.sync
        def _(sp):
            with sp.Fori(0, nf) as i:
                for slot, w in ((0, w1), (1, w3)):
                    st.load(sp, 2 * i + slot, slot, strip_of(w, i + f0))
            with sp.Fori(0, KT // 2) as i:
                for slot in range(2):
                    st.load(sp, 2 * i + slot + N1, slot, strip_of(w2, 2 * i + slot, nf, f0), nf)

        @block.scalar
        def _(act):
            def gate(i, between):
                act.wait_ge(st.multiplied, 2 * i + 3)
                act.wait_ge(mul, i)
                nc.scalar.activation(sil[:], strip_psum(m, 0), ACT.Silu).then_inc(silu, 1)
                between()
                act.wait_ge(mul, i + 1)
                nc.scalar.copy(row(mh, i), prod[:]).then_inc(mhi, 1)

            for slot in range(2):
                st.split_high(act, slot, slot, 1)
            with act.Fori(0, nf - 1) as i:
                gate(i, lambda: st.split_high(act, 2 * i + 2, 0, i + 2))
                st.split_high(act, 2 * i + 3, 1, i + 2)
            gate(nf - 1, lambda: st.split_high(act, N1, 0, nf + 1, nf))
            st.split_high(act, N1 + 1, 1, nf + 1, nf)
            with act.Fori(1, KT // 2) as i:
                for slot in range(2):
                    st.split_high(act, 2 * i + slot + N1, slot, i + nf + 1, nf)

        @block.vector
        def _(dve):
            def product(i):
                dve.wait_ge(st.multiplied, 2 * i + 4)
                dve.wait_ge(silu, i + 1)
                dve.wait_ge(mlo, i)
                nc.vector.tensor_tensor(prod[:], sil[:], strip_psum(m, 1), ALU.mult).then_inc(mul, 1)
                dve.wait_ge(mhi, i + 1)
                nc.vector.tensor_tensor(row(ml, i), prod[:], row(mh, i).bitcast(F32), ALU.subtract).then_inc(mlo, 1)

            dve.sem_inc(st.low, 2)
            for slot in range(2):
                st.split_low(dve, slot, slot)
            with dve.Fori(0, nf - 1) as i:
                st.split_low(dve, 2 * i + 2, 0)
                product(i)
                st.split_low(dve, 2 * i + 3, 1)
            st.split_low(dve, N1, 0, nf)
            product(nf - 1)
            st.split_low(dve, N1 + 1, 1, nf)
            with dve.Fori(0, KT // 2 - 1) as i:
                for slot in range(2):
                    add_residual(nc, m, st, dve, 2 * i + slot, slot, 2 * i + slot + N1)
                    st.split_low(dve, 2 * i + slot + 2 + N1, slot, nf)
            for slot in range(2):
                add_residual(nc, m, st, dve, KT - 2 + slot, slot, KT - 2 + slot + N1)

        @block.tensor
        def _(pe):
            pe.sem_inc(st.multiplied, 2)
            with pe.Fori(0, nf) as i:
                pe.wait_ge(silu, i)
                st.multiply(pe, 2 * i, 0, m.XH, m.XL)
                pe.wait_ge(mul, i)
                st.multiply(pe, 2 * i + 1, 1, m.XH, m.XL)
            pe.wait_ge(mlo, nf)
            for slot in range(2):
                st.multiply(pe, slot + N1, slot, mh, ml, nf)
            with pe.Fori(1, KT // 2) as i:
                for slot in range(2):
                    pe.wait_ge(st.drained, 2 * i + slot - 1)
                    st.multiply(pe, 2 * i + slot + N1, slot, mh, ml, nf)


def nsa_memory(m):
    t = SEQ * 4
    o = m.xr
    m.Q1 = m.at("Q1", o, [P, HPG, SEQ], F32R); o += HPG * t
    m.Q2 = m.at("Q2", o, [P, HPG, HALF], F32R); o += HPG * HALF * 4
    m.KS1 = m.at("KS1", o, [P, SEQ], F32R); o += t
    m.KS2 = m.at("KS2", o, [P, SEQ], F32R); o += t
    m.KW1 = m.at("KW1", o, [P, SEQ], F32R); o += t
    m.KW2 = m.at("KW2", o, [P, SEQ], F32R); o += t
    m.BS = m.at("BS", o, [P, 2, SEQ]); o += 2 * t
    m.T = m.at("T", o, [P, TS, SEQ])
    m.TMPQ = m.at("TMPQ", o + 2 * t, [P, 2, SEQ])
    o += TS * t
    assert o <= m.st
    o = m.st
    m.DIST = m.at("DIST", o, [P, SEQ]); o += t
    m.VWG = m.at("VWG", o, [P, QT, HD]); o += QT * HD * 4
    m.VCG = m.at("VCG", o, [P, 2, HD]); o += 2 * HD * 4
    m.BW = m.at("BW", o, [P, 2, WIN + P]); o += 2 * (WIN + P) * 4
    m.DISTC = m.at("DISTC", o, [P, QT, NCP]); o += QT * NCP * 4
    m.LOWER = m.at("LOWER", o, [P, NBLK, NBLK]); o += NBLK * NBLK * 4
    m.FORCED = m.at("FORCED", o, [P, QT // 2, NBLK]); o += QT // 2 * NBLK * 4
    m.IMP = m.at("IMP", o, [P, QT // 2, NBLK]); o += QT // 2 * NBLK * 4
    m.RANK = m.at("RANK", o, [P, QT // 2, NBLK]); o += QT // 2 * NBLK * 4
    m.NM = m.at("NM", o, [P, 2 * TS]); o += 2 * TS * 4
    m.SUM = m.at("SUM", o, [P, 2 * TS]); o += 2 * TS * 4
    m.REC = m.at("REC", o, [P, 2 * TS]); o += 2 * TS * 4
    m.MX = m.at("MX", o, [P, 2, QT]); o += 16 * 4
    m.DEN = m.at("DEN", o, [P, 2, QT]); o += 16 * 4
    m.SOME = m.at("SOME", o, [P, 8]); o += 32
    m.PTC = m.at("PTC", o, [P, HPG, HALF]); o += HPG * HALF * 4
    assert o <= m.big
    m.VS = m.at("VS", m.big + 8 * t, [P, QT, KVW])
    m.VW = m.at("VW", m.big + 10 * t, [P, QT, KVW])
    m.PT = m.at("PT", m.big + 16 * t, [P, 2, QT, 2 * P])
    m.IND = m.at("IND", m.xr + 16 * t - t, [P, SEQ])
    o = m.small_end
    m.KC1 = m.at("KC1", o, [P, GROUPS, NCP], F32R); o += GROUPS * NCP * 4
    m.KC2 = m.at("KC2", o, [P, GROUPS, NCP], F32R); o += GROUPS * NCP * 4
    m.VC = m.at("VC", o, [P, GROUPS, HD]); o += GROUPS * HD * 4
    m.VSG = m.at("VSG", o, [P, QT, HD]); o += QT * HD * 4
    m.PG = m.at("PG", m.xr + 11 * t, [P, QT // 2, NCP])
    assert o <= 229368, o


def nsa_compress(nc, m, cmp_w1, cmp_w2, cmp_pe):
    t = SEQ * 4
    o = m.xr
    w1 = m.at("cw1", o, [P, 2, KT * 2, HID]); o += 2 * 2 * KT * HID * 4
    x2 = m.at("cx2", o, [P, 2, GROUPS, CMP_STEP // 2, NCP]); o += 2 * GROUPS * CMP_STEP // 2 * NCP * 4
    gel = m.at("cgel", o, [P, 2, 2, GROUPS, NCP]); o += 4 * GROUPS * NCP * 4
    w2 = m.at("cw2", o, [P, 2, 2, HD]); o += 4 * HD * 4
    pe_ = m.at("cpe", o, [P, 2, 2 * KT]); o += 4 * KT * 4
    hb = m.at("chb", o, [P, 4]); o += 16
    kc = m.at("ckc", o + 16, [P, GROUPS, NCP]); o += GROUPS * NCP * 4 + 16
    assert o <= m.st
    loaded, pairs_a, pairs_v, biased, bias_kept, hidden, gelu, zero, kready, vready, kc_kept, kc_hi, kc_done, \
        turned, vt_kept, made, vc_done, vzero = sems(nc, "c", "loaded", "pairsa", "pairsv", "biased", "biaskept", "hidden", "gelu",
                                     "zero", "kready", "vready", "kckept", "kchi", "kcdone", "turned", "vtkept",
                                     "made", "vcdone", "vzero")
    MM = CMP_LEN // 2
    with nc.Block() as block:
        @block.sync
        def _(sp):
            sp.dma_start(w1[:], cmp_w1).then_inc(loaded, 16)
            sp.dma_start(w2[:], cmp_w2).then_inc(loaded, 16)
            sp.dma_start(pe_[:], cmp_pe).then_inc(loaded, 16)
            sp.wait_ge(loaded, 48)

        def pair_copies(which):
            for g in range(GROUPS):
                src = m.proj[HD * (g % 2):HD * (g % 2) + HD, 8 + 2 * which + g // 2, :].rearrange(
                    "p (n r a) -> p a r n", r=CMP_STEP // 2, a=2)
                for par in range(2):
                    yield x2[HD * par:HD * par + HD, which, g], src[:, par]

        @block.scalar
        def _(act):
            for dst, src in pair_copies(0):
                last = nc.scalar.copy(dst, src)
            last.then_inc(pairs_a, 1)
            act.wait_ge(zero, 1)
            act.wait_ge(bias_kept, 1)
            for n in range(4):
                act.wait_ge(hidden, n + 1)
                nc.scalar.activation(gel[:, n // 2, n % 2, :, 0:NC],
                                     m.PS[:, n % 2, 0:GROUPS * NC].rearrange("p (g n) -> p g n", g=GROUPS),
                                     ACT.Gelu_apprx_tanh, bias=hb[:, n:n + 1]).then_inc(gelu, 1)
            act.wait_ge(kc_kept, 1)
            nc.scalar.copy(m.KC1[0:HD], kc[0:HD]).then_inc(kc_hi, 1)
            for n in range(4):
                act.wait_ge(turned, n + 1)
                v = m.VS if n < 2 else m.VW
                nc.scalar.copy(v[:, :, (n % 2) * P:(n % 2) * P + P],
                               strip_psum(m, 2 + n % 2).rearrange("p (t c) -> p t c", c=P)).then_inc(vt_kept, 1)

        @block.vector
        def _(dve):
            nc.vector.memset(gel[:], 0.0).then_inc(zero, 1)
            nc.vector.memset(m.VCG[:], 0.0).then_inc(vzero, 1)
            for dst, src in pair_copies(1):
                last = nc.vector.tensor_copy(dst, src)
            last.then_inc(pairs_v, 1)
            dve.wait_ge(biased, 1)
            nc.vector.tensor_copy(hb[:], m.PS[:, 3, 0:4]).then_inc(bias_kept, 1)
            dve.wait_ge(kready, 1)
            nc.vector.tensor_copy(kc[0:HD], m.PS[0:HD, 2, 0:GROUPS * NCP].rearrange("p (g n) -> p g n", g=GROUPS)
                                  ).then_inc(kc_kept, 1)
            dve.wait_ge(kc_hi, 1)
            nc.vector.tensor_copy(m.KC1[HD:P], m.KC1[0:HD].bitcast(F32)).then_inc(kc_done, 1)
            nc.vector.tensor_tensor(m.KC2[0:HD], kc[0:HD], m.KC1[0:HD].bitcast(F32), ALU.subtract).then_inc(kc_done, 1)
            dve.wait_ge(vready, 1)
            dve.wait_ge(vzero, 1)
            for half in range(2):
                nc.vector.tensor_copy(m.VC[HD * half:HD * half + HD],
                                      m.PS[0:NCP, 3, 0:KVW].rearrange("p (g d) -> p g d", g=GROUPS)).then_inc(vc_done, 1)

        @block.tensor
        def _(pe):
            pe.wait_ge(loaded, 48)
            for n in range(4):
                for mm in range(MM):
                    last = nc.tensor.matmul(m.PS[:, 3, n:n + 1], w1[:, n // 2, mm, (n % 2) * P:(n % 2) * P + P],
                                            pe_[:, n // 2, mm:mm + 1], start=(mm == 0), stop=(mm == MM - 1))
            last.then_inc(biased, 1)
            pe.wait_ge(pairs_a, 1)
            for n in range(4):
                if n == 2:
                    pe.wait_ge(pairs_v, 1)
                if n >= 2:
                    pe.wait_ge(gelu, n - 1)
                for mm in range(MM):
                    r, first = mm % (CMP_STEP // 2), mm // (CMP_STEP // 2)
                    last = nc.tensor.matmul(m.PS[:, n % 2, 0:GROUPS * NC].rearrange("p (g n) -> p g n", g=GROUPS),
                                            w1[:, n // 2, mm, (n % 2) * P:(n % 2) * P + P],
                                            x2[:, n // 2, :, r, first:first + NC],
                                            start=(mm == 0), stop=(mm == MM - 1))
                last.then_inc(hidden, 1)
            pe.wait_ge(gelu, 4)
            pe.wait_ge(bias_kept, 1)
            for half in range(2):
                last = nc.tensor.matmul(m.PS[0:HD, 2, 0:GROUPS * NCP], w2[:, 0, half, :],
                                        gel[:, 0, half, :, :].rearrange("p g n -> p (g n)"), start=(half == 0), stop=(half == 1))
            last.then_inc(kready, 1)
            for g in range(GROUPS):
                for half in range(2):
                    last = nc.tensor.matmul(m.PS[0:NCP, 3, g * HD:(g + 1) * HD], gel[:, 1, half, g, :], w2[:, 1, half, :],
                                            start=(half == 0), stop=(half == 1))
            last.then_inc(vready, 1)
            for n in range(4):
                tile = 16 + n
                if n >= 2:
                    pe.wait_ge(vt_kept, n - 1)
                for kt in range(QT):
                    last = nc.tensor.transpose(strip_psum(m, 2 + n % 2)[:, kt * P:(kt + 1) * P],
                                               m.proj[:, tile, kt * P:(kt + 1) * P], m.ident[:])
                last.then_inc(turned, 1)

        @block.gpsimd
        def _(pool):
            count = 0

            def put(ins):
                nonlocal count
                count += 1
                ins.then_inc(made, 1)
                pool.wait_ge(made, count)

            def keep(out, op, base, pattern, mult, fill):
                put(nc.gpsimd.affine_select(out=out, in_=out, compare_op=op, fill=fill, base=base,
                                            pattern=pattern, channel_multiplier=mult))

            exact = dict(allow_small_or_imprecise_dtypes=True)
            put(nc.gpsimd.iota(m.DIST[:], pattern=[[1, SEQ]], base=P - SEQ, channel_multiplier=-1, **exact))
            keep(m.DIST[:], ALU.is_ge, SEQ - P, [[-1, SEQ]], 1, -BIG)
            put(nc.gpsimd.iota(m.DISTC[:], pattern=[[-P, QT], [CMP_STEP, NCP]], base=CMP_LEN - 1,
                               channel_multiplier=-1, **exact))
            keep(m.DISTC[:], ALU.is_ge, 1 - CMP_LEN, [[P, QT], [-CMP_STEP, NCP]], 1, -BIG)
            put(nc.gpsimd.memset(m.SOME[:], 1.0))
            keep(m.SOME[:], ALU.is_ge, 1 - CMP_LEN, [[0, 8]], 1, 0.0)
            put(nc.gpsimd.memset(m.LOWER[:], 1.0))
            keep(m.LOWER[:], ALU.is_gt, 0, [[1, NBLK], [-1, NBLK]], 0, 0.0)
            put(nc.gpsimd.memset(m.FORCED[:], 0.0))
            put(nc.gpsimd.memset(m.FORCED[:, :, 0:1], BIG))
            for q in range(QT // 2):
                for half in range(2):
                    cur = (q + QT // 2) * (P // BLK) + half
                    rows = m.FORCED[half * BLK:half * BLK + BLK, q]
                    put(nc.gpsimd.memset(rows[:, cur - 1:cur + 1], BIG))
                    if cur + 1 < NBLK:
                        put(nc.gpsimd.memset(rows[:, cur + 1:], -BIG))
            ind = m.IND[HD:HD + NBLK, :]
            put(nc.gpsimd.memset(ind, 1.0))
            keep(ind, ALU.is_ge, 0, [[1, SEQ]], -BLK, 0.0)
            keep(ind, ALU.is_ge, BLK - 1, [[-1, SEQ]], BLK, 0.0)


TS = 4
UNITS = [(h, 2 * i + p, b) for h in range(HPG) for i in range(QT // 2) for b in range(2) for p in range(2)]
NU = len(UNITS)
UPH = 2 * QT
NB = NU // 2
BPH = NB // HPG


def unit_tiles(u):
    _, q, b = UNITS[u]
    return (q - min(q, WT), q + 1) if b else (0, q + 1)


def chunk_table():
    out = []
    for u in range(len(UNITS)):
        a, b = unit_tiles(u)
        n = b - a
        cut = b if n <= 4 else a + (3 if n == 5 else 4)
        out.append([(a, cut)] + ([(cut, b)] if cut < b else []))
    return out


CHUNKS = chunk_table()
FIRST_CHUNK = [HPG + sum(len(c) for c in CHUNKS[:u]) for u in range(len(UNITS) + 1)]
NCH = FIRST_CHUNK[-1]
NS = HPG + NU
assert NS % 2 == 0 and NCH % 2 == 0


def nsa_attention(nc, m):
    st_t, st_h, st_l, s_ready, s_free, c_sub, c_exp, c_p, pt_t, kept, pv, drained, mk, mk_t, q2m, \
        b_r, b_w, v_r, p_r, scaled, ch, ind_r, begun, begun_p = sems(
            nc, "a", "shifted", "high", "low", "scores", "scorefree", "csub", "cexp", "cp", "turned", "kept",
            "values", "drained", "mask", "maskturned", "maskkept", "bias", "windowbias", "valuesready", "probs", "scaled",
            "chain", "ind", "begun", "begunpool")
    CHAIN = HPG * 6 + 9 + NU

    def ptslot(c):
        return m.PS[:, 4 + c % 2, :]

    with nc.Block() as block:
        @block.scalar
        def _(act):
            act.activation(m.KS2[HD:HD + NBLK, :], m.IND[HD:HD + NBLK, :], ACT.Copy).then_inc(ind_r, 1)
            act.sem_inc(kept, 2)
            with act.Fori(0, GROUPS // 2) as j:
                for gi in range(2):
                    g = 2 * j + gi
                    act.wait_ge(pv, NB * g + 2)

                    def bias(h):
                        nc.scalar.activation(m.BS[:, h % 2, :], m.DIST[:], ACT.Copy,
                                             scale=m.slopes[:, bass.ds(HPG * g + h, 1)])
                        nc.scalar.activation(m.BW[:, h % 2, :], m.DIST[:, SEQ - WIN - P:], ACT.Copy,
                                             scale=m.slopes[:, bass.ds(HPG * g + h, 1)]).then_inc(b_r, 1)

                    for n in range(2 + HPG):
                        if n < 2:
                            src = m.proj[HD * gi:HD * gi + HD, bass.ds((12, 14)[n] + j, 1), :]
                            hi = (m.KS1, m.KW1)[n][0:HD, :]
                        else:
                            h = n - 2
                            src = m.proj[HD * (h % 2):HD * (h % 2) + HD, bass.ds(2 * g + h // 2, 1), :]
                            hi = m.Q1[0:HD, h, :]
                        if n >= 2:
                            act.wait_ge(st_l, (2 + HPG) * g + n - 1)
                        else:
                            act.wait_ge(ind_r, 1)
                        nc.scalar.activation(m.TMPQ[0:HD, n % 2, :], src.rearrange("p a n -> p (a n)"), ACT.Copy,
                                             scale=1.0 if n < 2 else QSCALE).then_inc(st_t, 1)
                        act.wait_ge(st_t, (2 + HPG) * g + n + 1)
                        nc.scalar.copy(hi, m.TMPQ[0:HD, n % 2, :]).then_inc(st_h, 1)
                    bias(0)
                    for h in range(HPG + 1):
                        if h < HPG:
                            act.wait_ge(c_sub, HPG * g + h + 1)
                            nc.scalar.activation(m.T[:, h % 2, 0:HALF], m.T[:, h % 2, 0:HALF], ACT.Exp).then_inc(c_exp, 1)
                        if h >= 1:
                            act.wait_ge(pt_t, NCH * g + h)
                            nc.scalar.copy(m.PTC[:, h - 1, :], ptslot(h - 1)).then_inc(kept, 1)
                    act.wait_ge(mk_t, g + 1)
                    for h in range(HPG):
                        nc.scalar.copy(m.Q2[HD:HD + NBLK, h, :], m.PS[0:NBLK, 7, :]).then_inc(q2m, 1)

                    def exponentials(u):
                        a, e = unit_tiles(u)
                        t = m.T[:, u % TS, 0:(e - a) * P]
                        act.wait_ge(s_free, NS * g + HPG + u + 3)
                        nc.scalar.activation(t, t, ACT.Exp, bias=m.NM[:, u % TS:u % TS + 1], scale=-1.0,
                                             accum_out=m.SUM[:, u % TS:u % TS + 1]).then_inc(p_r, 1)

                    def keep(u):
                        block_, p = u // 2, u % 2
                        for c, (t0, t1) in zip(range(FIRST_CHUNK[u], FIRST_CHUNK[u + 1]), CHUNKS[u]):
                            act.wait_ge(pt_t, NCH * g + c + 1)
                            act.wait_ge(pv, NB * g + block_ + 1)
                            nc.scalar.copy(m.PT[:, block_ % 2, t0:t1, p * P:p * P + P],
                                           ptslot(c)[:, 0:(t1 - t0) * P].rearrange("p (t n) -> p t n", n=P)
                                           ).then_inc(kept, 1)

                    for v in range(1, NU + 3):
                        if v <= NU:
                            exponentials(v - 1)
                        if v >= 3:
                            keep(v - 3)
                        if v % UPH == UPH // 2 and v // UPH + 1 < HPG:
                            bias(v // UPH + 1)

        @block.gpsimd
        def _(pool):
            with pool.Fori(0, GROUPS // 2) as j:
                for h in range(2 * HPG):
                    pool.wait_ge(b_r, 2 * HPG * j + h + 1)
                    pool.sem_inc(begun_p, 1)
                    nc.gpsimd.affine_select(out=m.BW[:, h % 2, 0:P], in_=m.BW[:, h % 2, 0:P], compare_op=ALU.is_gt,
                                            fill=-BIG, base=0, pattern=[[1, P]], channel_multiplier=-1).then_inc(b_w, 1)

        @block.vector
        def _(dve):
            dve.sem_inc(s_free, 2)
            dve.sem_inc(drained, 2)
            with dve.Fori(0, GROUPS // 2) as j:
                for gi in range(2):
                    g = 2 * j + gi
                    links = 0

                    def link(ins):
                        nonlocal links
                        links += 1
                        ins.then_inc(ch, 1)
                        dve.wait_ge(ch, CHAIN * g + links)

                    dve.wait_ge(pv, NB * g + 2)
                    nc.vector.tensor_copy(m.VSG[:], m.VS[:, :, bass.ds(HD * g, HD)])
                    nc.vector.tensor_copy(m.VWG[:], m.VW[:, :, bass.ds(HD * g, HD)])
                    for half in range(2):
                        r = slice(HD * half, HD * half + HD)
                        ins = nc.vector.tensor_copy(m.VCG[r, half, :], m.VC[r, bass.ds(g, 1), :].rearrange("p a d -> p (a d)"))
                    ins.then_inc(v_r, 1)
                    for n in range(2 + HPG):
                        dve.wait_ge(st_h, (2 + HPG) * g + n + 1)
                        if n < 2:
                            k1, k2 = ((m.KS1, m.KS2), (m.KW1, m.KW2))[n]
                            nc.vector.tensor_copy(k1[HD:P, :], k1[0:HD, :].bitcast(F32))
                            nc.vector.tensor_tensor(k2[0:HD, :], m.TMPQ[0:HD, n % 2, :], k1[0:HD, :].bitcast(F32),
                                                    ALU.subtract).then_inc(st_l, 1)
                        else:
                            q1 = m.Q1[:, n - 2, :]
                            nc.vector.tensor_copy(m.Q2[0:HD, n - 2, :], q1[0:HD, HALF:].bitcast(F32))
                            nc.vector.tensor_tensor(q1[HD:P, :], m.TMPQ[0:HD, n % 2, :], q1[0:HD, :].bitcast(F32),
                                                    ALU.subtract).then_inc(st_l, 1)

                    def over_heads(x):
                        return x.unsqueeze(2).broadcast_to([P, QT, NCP])

                    for h in range(HPG + 1):
                        if h < HPG:
                            t = m.T[:, h % 2, 0:HALF].rearrange("p (t n) -> p t n", n=NCP)
                            dve.wait_ge(s_ready, NS * g + h + 1)
                            if h >= 2:
                                dve.wait_ge(pt_t, NCH * g + h - 1)
                            nc.vector.scalar_tensor_tensor(
                                out=m.T[:, h % 2, 0:HALF], in0=m.DISTC[:].rearrange("p t n -> p (t n)"),
                                scalar=m.slopes[:, bass.ds(HPG * g + h, 1)], in1=m.PS[:, 2 * (h % 2), :],
                                op0=ALU.mult, op1=ALU.add).then_inc(s_free, 1)
                            dve.wait_ge(s_free, NS * g + h + 3)
                            link(nc.vector.tensor_reduce(m.MX[:, h % 2, :], t, AX.X, ALU.max))
                            nc.vector.tensor_tensor(t, t, over_heads(m.MX[:, h % 2, :]), ALU.subtract).then_inc(c_sub, 1)
                        if h >= 1:
                            k = h - 1
                            t = m.T[:, k % 2, 0:HALF].rearrange("p (t n) -> p t n", n=NCP)
                            late = t[:, QT // 2:QT, :]
                            den = m.DEN[:, k % 2, :]
                            dve.wait_ge(c_exp, HPG * g + k + 1)
                            link(nc.vector.tensor_reduce(den, t, AX.X, ALU.add))
                            link(nc.vector.reciprocal(den, den))
                            link(nc.vector.tensor_tensor(den[:, 0:1], den[:, 0:1], m.SOME[:, 0:1], ALU.mult))
                            link(nc.vector.tensor_tensor(t, t, over_heads(den), ALU.mult))
                            if k == 0:
                                link(nc.vector.tensor_copy(m.PG[:], late))
                            else:
                                link(nc.vector.tensor_tensor(m.PG[:], m.PG[:], late, ALU.add))
                            nc.vector.tensor_tensor(
                                t, t, m.gates[:, :, bass.ds(HPG * g + k, 1)].broadcast_to([P, QT, NCP]),
                                ALU.mult).then_inc(c_p, 1)

                    v = m.PG[:].rearrange("p t (j r) -> p t j r", r=4)
                    imp = m.IMP[:]
                    link(nc.vector.tensor_tensor(imp, v[:, :, :, 0], v[:, :, :, 1], ALU.add))
                    link(nc.vector.tensor_tensor(imp, imp, v[:, :, :, 2], ALU.add))
                    link(nc.vector.scalar_tensor_tensor(out=imp, in0=imp, scalar=2.0, in1=v[:, :, :, 3],
                                                        op0=ALU.mult, op1=ALU.add))
                    link(nc.vector.tensor_tensor(imp[:, :, 1:], imp[:, :, 1:], v[:, :, 0:NBLK - 1, 3], ALU.add))
                    link(nc.vector.tensor_tensor(imp, imp, m.FORCED[:], ALU.add))
                    dve.wait_ge(pt_t, NCH * g + HPG)
                    QH = QT // 2
                    gt = m.T[:, 0, :].rearrange("p (t j i) -> p t j i", t=QH, j=NBLK)
                    eq = m.T[:, 1, :].rearrange("p (t j i) -> p t j i", t=QH, j=NBLK)
                    for q in range(QH):
                        ii = imp[:, q, :].unsqueeze(1).broadcast_to([P, NBLK, NBLK])
                        jj = imp[:, q, :].unsqueeze(2).broadcast_to([P, NBLK, NBLK])
                        nc.vector.tensor_tensor(gt[:, q], ii, jj, ALU.is_gt)
                        ins = nc.vector.tensor_tensor(eq[:, q], ii, jj, ALU.is_equal)
                    link(ins)
                    for q in range(QH):
                        ins = nc.vector.tensor_tensor(eq[:, q], eq[:, q], m.LOWER[:], ALU.mult)
                    link(ins)
                    link(nc.vector.tensor_tensor(m.T[:, 0, :], m.T[:, 0, :], m.T[:, 1, :], ALU.add))
                    link(nc.vector.tensor_reduce(m.RANK[:], gt, AX.X, ALU.add))
                    nc.vector.tensor_scalar(m.RANK[:], m.RANK[:], float(N_SEL), -BIG, ALU.is_ge, ALU.mult).then_inc(mk, 1)

                    def bias_and_max(u):
                        h, q, b = UNITS[u]
                        a, e = unit_tiles(u)
                        n = (e - a) * P
                        bias = m.BW[:, h % 2, WIN + P - n:] if b else m.BS[:, h % 2, SEQ - n:]
                        if u % UPH == 0:
                            dve.wait_ge(b_w, HPG * g + h + 1)
                        dve.wait_ge(s_ready, NS * g + HPG + u + 1)
                        if u >= TS:
                            dve.wait_ge(pt_t, NCH * g + FIRST_CHUNK[u - TS + 1])
                        else:
                            dve.wait_ge(mk, g + 1)
                        dve.sem_inc(begun, 1)
                        nc.vector.tensor_tensor_reduce(m.T[:, u % TS, 0:n], strip_psum(m, u % 2)[:, 0:n], bias, -1.0,
                                                       3e38, ALU.add, ALU.min, m.NM[:, u % TS:u % TS + 1]
                                                       ).then_inc(s_free, 1)

                    def scale(u):
                        h, q, b = UNITS[u]
                        a, e = unit_tiles(u)
                        t = m.T[:, u % TS, 0:(e - a) * P]
                        rec = m.REC[:, u % TS:u % TS + 1]
                        dve.wait_ge(p_r, NU * g + u + 1)
                        link(nc.vector.reciprocal(rec, m.SUM[:, u % TS:u % TS + 1]))
                        nc.vector.tensor_scalar(t, t, rec, m.gates[:, q, bass.ds(HEADS * (b + 1) + h + HPG * g, 1)],
                                                ALU.mult, ALU.mult).then_inc(scaled, 1)

                    def drain(h, half):
                        dve.wait_ge(pv, NB * g + BPH * h + BPH // 2 * (half + 1) + 2)
                        nc.vector.tensor_copy(
                            m.proj[HD * (h % 2):HD * (h % 2) + HD, bass.ds(2 * g + h // 2, 1),
                                   half * HALF:half * HALF + HALF].rearrange("p a n -> p (a n)"),
                            m.PS[0:HD, 6 + half, :]).then_inc(drained, 1)

                    for v in range(NU + 2):
                        if v >= 2:
                            scale(v - 2)
                        if v < NU:
                            bias_and_max(v)
                        if v >= UPH // 2 + 5 and (v - 5) % (UPH // 2) == 0:
                            n = (v - 5) // (UPH // 2) - 1
                            drain(n // 2, n % 2)
                    drain(HPG - 1, 1)
                    assert links == CHAIN, links

        @block.tensor
        def _(pe):
            pe.sem_inc(pv, 2)
            pe.wait_ge(ind_r, 1)
            with pe.Fori(0, GROUPS // 2) as j:
                for gi in range(2):
                    g = 2 * j + gi

                    def comp_scores(h):
                        pe.wait_ge(st_l, (2 + HPG) * g + 3 + h)
                        pe.wait_ge(s_free, NS * g + h + 1)
                        for q in range(QT):
                            out = m.PS[:, 2 * (h % 2), q * NCP:(q + 1) * NCP]
                            nc.tensor.matmul(out, m.Q1[:, h, q * P:(q + 1) * P], row(m.KC1, g), start=True, stop=False)
                            last = nc.tensor.matmul(out, m.Q1[0:HD, h, q * P:(q + 1) * P],
                                                    m.KC2[0:HD, bass.ds(g, 1), :].rearrange("p a n -> p (a n)"),
                                                    start=False, stop=True)
                        last.then_inc(s_ready, 1)

                    def turn_comp(h):
                        pe.wait_ge(c_p, HPG * g + h + 1)
                        pe.wait_ge(kept, NCH * g + h + 1)
                        for k in range(4):
                            last = nc.tensor.transpose(ptslot(h)[:, k * P:(k + 1) * P], m.T[:, h % 2, k * P:(k + 1) * P],
                                                       m.ident[:])
                        last.then_inc(pt_t, 1)

                    def scores(u):
                        h, q, b = UNITS[u]
                        a, e = unit_tiles(u)
                        if u == 0:
                            pe.wait_ge(q2m, HPG * g + HPG)
                        pe.wait_ge(s_free, NS * g + HPG + u + 1)
                        k1, k2 = (m.KW1, m.KW2) if b else (m.KS1, m.KS2)
                        rows, q2 = (HD, m.Q1[0:HD, h, q * P:(q + 1) * P])
                        if not b and q >= QT // 2:
                            rows, q2 = HD + NBLK, m.Q2[0:HD + NBLK, h, (q - QT // 2) * P:(q - QT // 2 + 1) * P]
                        spans = [(n, min(n + HALF, e * P)) for n in range(a * P, e * P, HALF)]
                        for n, end in spans:
                            nc.tensor.matmul(strip_psum(m, u % 2)[:, n - a * P:end - a * P],
                                             m.Q1[:, h, q * P:(q + 1) * P], k1[:, n:end], start=True, stop=False)
                        for n, end in spans:
                            last = nc.tensor.matmul(strip_psum(m, u % 2)[:, n - a * P:end - a * P],
                                                    q2, k2[0:rows, n:end], start=False, stop=True)
                        last.then_inc(s_ready, 1)

                    def turn(u, k):
                        a, e = unit_tiles(u)
                        c = FIRST_CHUNK[u] + k
                        t0, t1 = CHUNKS[u][k]
                        pe.wait_ge(kept, NCH * g + c + 1)
                        for t in range(t0, t1):
                            last = nc.tensor.transpose(ptslot(c)[:, (t - t0) * P:(t - t0 + 1) * P],
                                                       m.T[:, u % TS, (t - a) * P:(t - a + 1) * P], m.ident[:])
                        last.then_inc(pt_t, 1)

                    def block_products(n):
                        h, q, b = UNITS[2 * n]
                        bank = m.PS[0:HD, 6 + q // 4, :]
                        if n % (BPH // 2) == 0:
                            half = q // 4
                            both = bank.rearrange("p (k a n) -> p a k n", k=2, a=2)
                            ptc = m.PTC[:, h, half * 2 * P:(half + 1) * 2 * P].rearrange("p (k n) -> p k n", k=2)
                            for par in range(2):
                                yield both[:, par], m.VCG[:, par, :], ptc, par == 0, False
                        col = (q % 4) * P
                        v = m.VWG if b else m.VSG
                        first = [unit_tiles(2 * n + p)[0] for p in range(2)]
                        for t in range(first[0], q + 2):
                            lo = P if t > q else 0
                            hi = P if t < first[1] else 2 * P
                            yield (bank[:, col + lo:col + hi], v[:, t, :],
                                   m.PT[:, n % 2, t, lo:hi], False,
                                   n % (BPH // 2) == BPH // 2 - 1 and t == q + 1)

                    for h in range(HPG + 1):
                        if h < HPG:
                            comp_scores(h)
                        if h >= 1:
                            turn_comp(h - 1)
                    pe.wait_ge(mk, g + 1)
                    pe.wait_ge(drained, 2 * HPG * g + 2)
                    for q in range(QT // 2):
                        last = nc.tensor.transpose(m.PS[0:NBLK, 7, q * P:(q + 1) * P], m.RANK[:, q, :], m.ident[:])
                    last.then_inc(mk_t, 1)

                    def products(n, items, last_of_block):
                        for out, lhs, rhs, start, stop in items:
                            last = nc.tensor.matmul(out, lhs, rhs, start=start, stop=stop)
                        if last_of_block:
                            last.then_inc(pv, 1)

                    def begin_block(n):
                        if n == 0:
                            pe.wait_ge(v_r, g + 1)
                        if n % (BPH // 2) == 0:
                            pe.wait_ge(drained, 2 * HPG * g + 2 * (n // BPH) + (n // (BPH // 2)) % 2 + 1)
                        pe.wait_ge(kept, NCH * g + FIRST_CHUNK[2 * n + 2] + 2)
                        return list(block_products(n))

                    for v in range(NU + 3):
                        if v < NU:
                            scores(v)
                        if v >= 3:
                            u = v - 3
                            pe.wait_ge(scaled, NU * g + u + 1)
                            n = u // 2
                            slots = len(CHUNKS[2 * n]) + len(CHUNKS[2 * n + 1])
                            for k in range(len(CHUNKS[u])):
                                turn(u, k)
                                if n:
                                    if u % 2 == 0 and k == 0:
                                        todo, used = begin_block(n - 1), 0
                                    i = k + (u % 2) * len(CHUNKS[2 * n])
                                    upto = len(todo) * (i + 1) // slots
                                    if upto > used:
                                        products(n - 1, todo[used:upto], upto == len(todo))
                                    used = upto
                    products(NB - 1, begin_block(NB - 1), True)


SB_UNITS = [(h, q) for h in range(2) for q in range(QT)]
SB_NU = len(SB_UNITS)
SB_ITEMS = [(h, q, t) for h in range(2) for q in range(0, QT, 2) for t in ((4, 0) if q >= QT // 2 else (4,))]
SB_NI = len(SB_ITEMS)


def sb_chunk_table():
    out = []
    for h, q in SB_UNITS:
        mine = [n for n, it in enumerate(SB_ITEMS) if it[0] == h and it[1] == q - q % 2]
        out.append([(n, max(SB_ITEMS[n][2], QT - 1 - q), SB_ITEMS[n][2] + 4) for n in mine])
    return out


SB_CHUNKS = sb_chunk_table()
SB_FIRST = [2 + sum(len(c) for c in SB_CHUNKS[:u]) for u in range(SB_NU + 1)]
SB_NCH = SB_FIRST[-1]
SB_LAST = {item: SB_FIRST[u] + k for u in range(SB_NU) for k, (item, _, _) in enumerate(SB_CHUNKS[u])}
SB_SLOTS = 3
assert SB_NCH % 2 == 0 and SB_NI % 2 == 0


def stick_breaking(nc, m, w_in):
    t = SEQ * 4
    o = m.big + 8 * t
    q1 = m.at("sq1", o, [P, 2, SEQ], F32R); o += 2 * t
    k1 = m.at("sk1", o, [P, 2, SEQ], F32R); o += 2 * t
    klo = m.at("sklo", o, [P, SEQ], F32R); o += t
    vtok = m.at("svtok", o, [P, QT, P]); o += t
    keep = m.at("skeep", o, [P, SEQ]); o += t
    beta = m.at("sbeta", o, [P, SB_SLOTS, SEQ]); o += SB_SLOTS * t
    pt = m.at("spt", o, [P, 2, 4, 2 * P]); o += 2 * t
    assert o <= m.small
    prod = m.at("sprod", m.gates_at, [P, SEQ + 8])
    assert m.gates_at + t + 32 <= 229368
    st = Strips(nc, m, "s")
    hi, qkv, vst, z_r, kp_r, kp_s, z_free, b_s, scn, a_r, pt_t, kept, pv, drained, one, begun = sems(
        nc, "s", "stackhigh", "stacklow", "vstaged", "zready", "keepready", "keepselected", "zfree", "betaselected",
        "scanned", "aready", "turned", "kept", "values", "outdrained", "one", "begun")
    PAIRS = HEADS // 2

    def ptslot(c):
        return m.PS[:, 4 + c % 2, :]

    def own(h):
        return slice(HD * h, HD * h + HD)

    def other(h):
        return slice(HD - HD * h, 2 * HD - HD * h)

    with nc.Block() as block:
        @block.sync
        def _(sp):
            with sp.Fori(0, PAIRS) as j:
                for n, slot in enumerate((0, 1, 0)):
                    sp.wait_ge(st.low, 3 * j + (2, 1, 3)[n])
                    sp.dma_start(m.W32[:, slot], strip_of(w_in, j + n * PAIRS)).then_inc(st.loaded[slot], 16)

        @block.scalar
        def _(act):
            def split(j, n):
                slot = n % 2
                act.wait_ge(st.loaded[slot], 16 * (j + 1) if slot else 16 * (2 * j + n // 2 + 1))
                act.wait_ge(st.multiplied, 3 * j + (2, 1, 3)[n])
                nc.scalar.copy(m.WHI[:, slot], m.W32[:, slot]).then_inc(st.high, 1)

            def stack_high(j, n):
                act.wait_ge(st.multiplied, 3 * j + n + 3)
                for h in range(2):
                    dst = q1[own(h), h, :] if n == 0 else k1[own(h), h, ::-1]
                    nc.scalar.activation(dst, strip_psum(m, n)[own(h)], ACT.Copy,
                                         scale=QSCALE if n == 0 else 1.0).then_inc(hi, 1)

            def sigmoids(j, u):
                h, q = SB_UNITS[u]
                n = (q + 1) * P
                z = strip_psum(m, (u + 1) % 2)[:, 0:n]
                act.wait_ge(z_r, SB_NU * j + u + 1)
                act.wait_ge(scn, SB_NU * j + u + 1)
                nc.scalar.activation(keep[:, 0:n], z, ACT.Sigmoid, scale=-1.0).then_inc(kp_r, 1)
                if u >= SB_SLOTS:
                    act.wait_ge(pt_t, SB_NCH * j + SB_FIRST[u - SB_SLOTS + 1])
                nc.scalar.activation(beta[:, u % SB_SLOTS, 0:n], z, ACT.Sigmoid).then_inc(z_free, 1)

            def keep_chunks(j, u):
                for k, (item, t0, t1) in enumerate(SB_CHUNKS[u]):
                    act.wait_ge(pt_t, SB_NCH * j + SB_FIRST[u] + k + 1)
                    act.wait_ge(pv, SB_NI * j + item + 1)
                    nc.scalar.copy(pt[:, item % 2, t0 % 4:4, (u % 2) * P:(u % 2) * P + P],
                                   ptslot(SB_FIRST[u] + k)[:, 0:(t1 - t0) * P].rearrange("p (t n) -> p t n", n=P)
                                   ).then_inc(kept, 1)

            def pair(j, last):
                stack_high(j, 1)
                split(j, 2)
                act.wait_ge(hi, 4 * j + 4)
                for h in range(2):
                    ins = nc.scalar.copy(k1[other(h), h, :], k1[own(h), h, :].bitcast(F32))
                ins.then_inc(vst, 1)
                act.wait_ge(st.multiplied, 3 * j + 5)
                nc.scalar.copy(keep[:, ::-1], strip_psum(m, 0)).then_inc(vst, 1)
                for c in range(2):
                    act.wait_ge(pt_t, SB_NCH * j + c + 1)
                    nc.scalar.copy(vtok[:, 4 * c:4 * c + 4, :].rearrange("p t d -> p (t d)"), ptslot(c)).then_inc(kept, 1)
                for v in range(SB_NU + 2):
                    if v < SB_NU:
                        sigmoids(j, v)
                    if v >= 2:
                        keep_chunks(j, v - 2)
                    if v == SB_NU - 4 and not last:
                        for n in range(2):
                            split(j + 1, n)
                    if v == SB_NU and not last:
                        stack_high(j + 1, 0)

            act.sem_inc(kept, 2)
            for n in range(2):
                split(0, n)
            stack_high(0, 0)
            with act.Fori(0, PAIRS - 1) as j:
                pair(j, False)
            pair(PAIRS - 1, True)

        @block.gpsimd
        def _(pool):
            def select(x, fill, done):
                pool.sem_inc(begun, 1)
                nc.gpsimd.affine_select(out=x, in_=x, compare_op=ALU.is_gt, fill=fill, base=1 - P,
                                        pattern=[[1, P]], channel_multiplier=1).then_inc(done, 1)

            with pool.Fori(0, PAIRS) as j:
                for u in range(SB_NU):
                    pool.wait_ge(kp_r, SB_NU * j + u + 1)
                    select(keep[:, 0:P], 1.0, kp_s)
                    pool.wait_ge(z_free, SB_NU * j + u + 1)
                    select(beta[:, u % SB_SLOTS, 0:P], 0.0, b_s)

        @block.vector
        def _(dve):
            def split(j, n):
                dve.wait_ge(st.high, 3 * j + n + 1)
                nc.vector.tensor_tensor(m.WLO[:, n % 2], m.W32[:, n % 2], m.WHI[:, n % 2].bitcast(F32),
                                        ALU.subtract).then_inc(st.low, 1)

            def stack_low(j, n):
                for h in range(2):
                    dve.wait_ge(hi, 4 * j + 2 * n + h + 1)
                    src = strip_psum(m, n)[own(h)]
                    if n == 0:
                        ins = nc.vector.scalar_tensor_tensor(
                            out=q1[other(h), h, :], in0=src, scalar=QSCALE, in1=q1[own(h), h, :].bitcast(F32),
                            op0=ALU.mult, op1=ALU.subtract)
                    else:
                        ins = nc.vector.tensor_tensor(klo[own(h), ::-1], src, k1[own(h), h, ::-1].bitcast(F32),
                                                      ALU.subtract)
                ins.then_inc(qkv, 1)

            def drain(j, h, half):
                dve.wait_ge(pv, SB_NI * j + SB_NI // 2 * h + (4 * half + 2) + 2)
                nc.vector.tensor_copy(row(m.proj, j)[own(h), half * HALF:half * HALF + HALF],
                                      m.PS[0:HD, 6 + half, :]).then_inc(drained, 1)

            def pair(j, last):
                stack_low(j, 1)
                split(j, 2)
                for u in range(SB_NU):
                    h, q = SB_UNITS[u]
                    n = (q + 1) * P
                    b = beta[:, u % SB_SLOTS, 0:n]
                    dve.wait_ge(kp_s, SB_NU * j + u + 1)
                    if u:
                        dve.wait_ge(a_r, SB_NU * j + u)
                    nc.vector.tensor_tensor_scan(prod[:, 1:n + 1], keep[:, 0:n], keep[:, 0:n], 1.0,
                                                 ALU.mult, ALU.bypass).then_inc(scn, 1)
                    dve.wait_ge(scn, SB_NU * j + u + 2)
                    dve.wait_ge(b_s, SB_NU * j + u + 1)
                    nc.vector.tensor_tensor(b, b, prod[:, 0:n], ALU.mult).then_inc(a_r, 1)
                    if u in (7, 11, 15):
                        drain(j, *((0, 0), (0, 1), (1, 0))[(u - 7) // 4])
                    if u == SB_NU - 4 and not last:
                        for n in range(2):
                            split(j + 1, n)
                if not last:
                    stack_low(j + 1, 0)
                drain(j, 1, 1)

            nc.vector.memset(prod[:, 0:1], 1.0).then_inc(one, 1)
            dve.wait_ge(one, 1)
            dve.sem_inc(st.low, 2)
            dve.sem_inc(scn, 1)
            dve.sem_inc(drained, 2)
            for n in range(2):
                split(0, n)
            stack_low(0, 0)
            with dve.Fori(0, PAIRS - 1) as j:
                pair(j, False)
            pair(PAIRS - 1, True)

        @block.tensor
        def _(pe):
            def strip(j, n):
                pe.wait_ge(st.low, 3 * j + n + 3)
                slot = n % 2
                strip_products(nc, strip_psum(m, slot), m.WHI[:, slot], m.WLO[:, slot], m.XH, m.XL,
                               KT).then_inc(st.multiplied, 1)

            def scores(j, u):
                h, q = SB_UNITS[u]
                if u == 0:
                    pe.wait_ge(qkv, 2 * j + 2)
                    pe.wait_ge(vst, 2 * j + 1)
                elif u == 1:
                    pe.wait_ge(vst, 2 * j + 2)
                else:
                    pe.wait_ge(z_free, SB_NU * j + u - 1)
                first = SEQ - (q + 1) * P
                spans = [(n, min(n + HALF, SEQ)) for n in range(first, SEQ, HALF)]
                for n, end in spans:
                    nc.tensor.matmul(strip_psum(m, (u + 1) % 2)[:, n - first:end - first],
                                     q1[:, h, q * P:(q + 1) * P], k1[:, h, n:end], start=True, stop=False)
                for n, end in spans:
                    last = nc.tensor.matmul(strip_psum(m, (u + 1) % 2)[:, n - first:end - first],
                                            q1[own(h), h, q * P:(q + 1) * P], klo[own(h), n:end],
                                            start=False, stop=True)
                last.then_inc(z_r, 1)

            def turn(j, c, tiles):
                pe.wait_ge(kept, SB_NCH * j + c + 1)
                for n, x in enumerate(tiles):
                    last = nc.tensor.transpose(ptslot(c)[:, n * P:(n + 1) * P], x, m.ident[:])
                last.then_inc(pt_t, 1)

            def products(j, item):
                h, q, first = SB_ITEMS[item]
                starts = q % 4 == 0 and first == 4
                if starts:
                    pe.wait_ge(drained, 4 * j + 2 * h + q // 4 + 1)
                pe.wait_ge(kept, SB_NCH * j + SB_LAST[item] + 3)
                tiles = [t for t in range(first, first + 4) if t >= QT - 2 - q]
                tiles.sort(key=lambda t: t < QT - 1 - q)
                col = (q % 4) * P
                for t in tiles:
                    lo = P if t < QT - 1 - q else 0
                    last = nc.tensor.matmul(m.PS[0:HD, 6 + q // 4, col + lo:col + 2 * P], vtok[:, t, own(h)],
                                            pt[:, item % 2, t % 4, lo:2 * P], start=starts and t == tiles[0],
                                            stop=q % 4 == 2 and (item + 1 == SB_NI or SB_ITEMS[item + 1][1] != q)
                                            and t == tiles[-1])
                last.then_inc(pv, 1)

            def pair(j, last):
                strip(j, 1)
                pe.wait_ge(qkv, 2 * j + 1)
                strip(j, 2)
                scores(j, 0)
                pe.wait_ge(vst, 2 * j + 2)
                for c in range(2):
                    turn(j, c, [keep[:, t * P:(t + 1) * P] for t in range(4 * c, 4 * c + 4)])
                waiting = []
                for v in range(1, SB_NU + 2):
                    if v < SB_NU:
                        scores(j, v)
                    if v >= 2:
                        u = v - 2
                        pe.wait_ge(a_r, SB_NU * j + u + 1)
                        start = SB_CHUNKS[u][0][1] if len(SB_CHUNKS[u]) == 1 else SB_CHUNKS[u][1][1]
                        for k, (item, t0, t1) in enumerate(SB_CHUNKS[u]):
                            c = SB_FIRST[u] + k
                            turn(j, c, [beta[:, u % SB_SLOTS, (t - start) * P:(t - start + 1) * P] for t in range(t0, t1)])
                            while waiting:
                                products(j, waiting.pop(0))
                            if c == SB_LAST[item]:
                                waiting.append(item)
                    if v == SB_NU and not last:
                        pe.wait_ge(z_free, SB_NU * j + SB_NU)
                        strip(j + 1, 0)
                products(j, waiting.pop())
                assert not waiting

            pe.sem_inc(st.multiplied, 2)
            pe.sem_inc(pv, 2)
            strip(0, 0)
            with pe.Fori(0, PAIRS - 1) as j:
                pair(j, False)
            pair(PAIRS - 1, True)


def strips(w):
    r, c = w.shape
    return np.ascontiguousarray(w.reshape(r // P, P, c // P, P).transpose(2, 1, 0, 3))


def features_first(a):
    return np.ascontiguousarray(a.T.reshape(KT, P, SEQ).transpose(1, 0, 2))


def build_trunk(nc, x, gains, nsa_in, nsa_gate, gate_b, cmp_w1, cmp_w2, cmp_pe, nsa_out, sb_in, sb_out,
                w1, w3, w2, out):
    m = Memory(nc)
    nsa_memory(m)
    load_input(nc, m, x, gains)
    for layer in range(2):
        held = set(nc.free_semaphores)
        rmsnorm(nc, m, 2 * layer)
        if layer == 0:
            nsa_projection(nc, m, nsa_in, nsa_gate, gate_b)
            nsa_compress(nc, m, cmp_w1, cmp_w2, cmp_pe)
            nsa_attention(nc, m)
            residual_projection(nc, m, "no", nsa_out)
        else:
            stick_breaking(nc, m, sb_in)
            residual_projection(nc, m, "so", sb_out)
        rmsnorm(nc, m, 2 * layer + 1)
        f0 = 0
        for nf in FFN_CHUNKS:
            ffn_chunk(nc, m, f"f{layer}_{f0}", w1[layer], w3[layer], w2[layer], f0, nf)
            f0 += nf
        if layer == 0:
            nc.clear_and_free_semaphores(sorted(held - set(nc.free_semaphores)))
            nc.all_engine_barrier()
    rmsnorm(nc, m, 4, out=out)


def kernel(x, mix_norm_g, ffn_norm_g, final_norm_g, nsa_w_in, nsa_gate_b, nsa_cmp_pe, nsa_cmp_w1, nsa_cmp_w2,
           nsa_w_out, sb_w_in, sb_w_out, ffn_w1, ffn_w3, ffn_w2):
    import concourse.bacc as bacc
    from concourse.bass_utils import run_bass_kernel_spmd

    mix, ffn, final, w_in = (np.asarray(a) for a in (mix_norm_g, ffn_norm_g, final_norm_g, nsa_w_in))
    qkv = NSA_TILES * P
    cuts = np.cumsum([0, D] + 6 * [KVW])
    order = np.concatenate([np.arange(cuts[n], cuts[n + 1]) for n in (0, 1, 2, 3, 5, 4, 6)])
    gains = np.stack([mix[0], ffn[0], mix[1], ffn[1], final])
    arrays = {
        "x": features_first(np.asarray(x)[0]),
        "gains": np.ascontiguousarray(gains.reshape(5, KT, P).transpose(2, 0, 1)),
        "nsa_in": strips(w_in[0][:, order]),
        "nsa_gate": np.ascontiguousarray(w_in[0][:, qkv:].reshape(KT, P, -1).transpose(1, 0, 2)),
        "gate_b": np.ascontiguousarray(np.asarray(nsa_gate_b)[0]),
        "cmp_w1": np.ascontiguousarray(np.asarray(nsa_cmp_w1)[0].reshape(2, 2 * KT, P, HID).transpose(2, 0, 1, 3)),
        "cmp_w2": np.ascontiguousarray(np.asarray(nsa_cmp_w2)[0].reshape(2, 2, P, HD).transpose(2, 0, 1, 3)),
        "cmp_pe": np.ascontiguousarray(np.asarray(nsa_cmp_pe)[0].reshape(2, 2 * KT, P).transpose(2, 0, 1)),
        "nsa_out": strips(np.asarray(nsa_w_out)[0]),
        "sb_in": strips(np.asarray(sb_w_in)[0]),
        "sb_out": strips(np.asarray(sb_w_out)[0]),
        "w1": np.stack([strips(w) for w in np.asarray(ffn_w1)]),
        "w3": np.stack([strips(w) for w in np.asarray(ffn_w3)]),
        "w2": np.stack([strips(w) for w in np.asarray(ffn_w2)]),
    }
    nc = bacc.Bacc("TRN2", target_bir_lowering=False, num_devices=1)
    args = {n: nc.dram_tensor(n, a.shape, mybir.dt.from_np(a.dtype), kind="ExternalInput").ap()
            for n, a in arrays.items()}
    out = nc.dram_tensor("out", (P, KT, SEQ), F32, kind="ExternalOutput").ap()
    build_trunk(nc, out=out, **args)
    r = run_bass_kernel_spmd(nc, [arrays], core_ids=[0])
    got = r.results[0]["out"]
    return np.ascontiguousarray(got.transpose(2, 1, 0)).reshape(1, SEQ, D)
```

```python
import concourse.bass as bass
from concourse import mybir
import numpy as np

F32 = mybir.dt.float32
F32R = mybir.dt.float32r
ACT = mybir.ActivationFunctionType
ALU = mybir.AluOpType
AX = mybir.AxisListType

P = 128
SEQ = 1024
D = 1024
HALF = 512
KT = D // P
QT = SEQ // P
HEADS = 16
HD = D // HEADS
GROUPS = 4
HPG = HEADS // GROUPS
KVW = GROUPS * HD
BRANCHES = 3
CMP_LEN, CMP_STEP = 32, 16
NCP = SEQ // CMP_STEP
NC = NCP - 1
HID = 4 * HD
BLK = 64
NBLK = SEQ // BLK
N_SEL = 8
WIN = 512
WT = WIN // P
D_FF = 2816
FT = D_FF // P
EPS = 1e-6
BIG = 1e30
QSCALE = HD ** -0.5
NSA_TILES = (D + 6 * KVW) // P
FFN_CHUNKS = (8, 8, 6)
assert sum(FFN_CHUNKS) == FT


class Memory:

    def __init__(self, nc):
        self.nc = nc
        tile = SEQ * 4
        self.base = 16512
        self.xr = self.base + KT * tile
        self.st = self.xr + 2 * KT * tile
        self.big = self.st + 6 * tile
        self.small = self.big + NSA_TILES * tile
        at = self.at
        self.H = at("H", self.base, [P, KT, SEQ])
        self.XH = at("XH", self.xr, [P, KT, SEQ], F32R)
        self.XL = at("XL", self.xr + KT * tile, [P, KT, SEQ], F32R)
        self.W32 = at("W32", self.st, [P, 2, KT, P])
        self.WHI = at("WHI", self.st + 2 * tile, [P, 2, KT, P], F32R)
        self.WLO = at("WLO", self.st + 4 * tile, [P, 2, KT, P], F32R)
        o = self.small
        self.ident = at("ident", o, [P, P]); o += P * 4
        self.ones = at("ones", o, [P, P], F32R); o += P * 4
        self.slopes = at("slopes", o, [P, HEADS]); o += HEADS * 4
        self.gains = at("gains", o, [P, 5, KT]); o += 5 * KT * 4
        self.eps = at("eps", o, [P, 8]); o += 32
        self.gates_at = o
        self.gates = at("gates", o, [P, QT, BRANCHES * HEADS]); o += QT * BRANCHES * HEADS * 4
        self.gate_bias = at("gate_bias", o, [P, BRANCHES * HEADS])
        self.proj = at("proj", self.big, [P, NSA_TILES, SEQ])
        self.small_end = o
        self.PS = nc.alloc_psum_tensor("PS", [P, 8, HALF], F32)

    def at(self, name, offset, shape, dt=F32):
        return self.nc.alloc_sbuf_tensor_at(name, shape, dt, offset=offset)


def sems(nc, prefix, *names):
    return [nc.alloc_semaphore(f"{prefix}_{n}") for n in names]


def strip_tile_products(nc, out, whi, wlo, xh, xl, k, n):
    for w, x in ((whi, xh), (whi, xl), (wlo, xh)):
        for half in range(2):
            cols = slice(half * HALF, half * HALF + HALF)
            last = nc.tensor.matmul(out[:, cols], w[:, k, :], x[:, k, cols],
                                    start=(k == 0 and w is whi and x is xh), stop=(k == n - 1 and w is wlo))
    return last


def strip_products(nc, out, whi, wlo, xh, xl, n):
    for k in range(n):
        last = strip_tile_products(nc, out, whi, wlo, xh, xl, k, n)
    return last


def strip_psum(m, slot):
    return m.PS[:, 2 * slot:2 * slot + 2, :].rearrange("p a n -> p (a n)")


class Norm:

    def __init__(self, nc, m, n, scratch=16, slots=1):
        t = SEQ * 4
        self.nc, self.m, self.n, self.slots = nc, m, n, slots
        at = m.big + scratch * t
        self.sqh = m.at(f"sqh{n}", at, [P, 2, SEQ], F32R)
        self.sq = m.at(f"sq{n}", at + 2 * t, [P, slots, SEQ])
        self.sql = m.at(f"sql{n}", at + (2 + slots) * t, [P, slots, SEQ], F32R)
        self.lnv = m.at(f"lnv{n}", m.big + 6 * t, [P, SEQ])
        self.rstd = m.at(f"rstd{n}", m.big + 7 * t, [P, SEQ])
        self.y = m.at(f"y{n}", m.big + 8 * t, [P, 2, SEQ])
        self.squared, self.hi, self.lo, self.summed, self.rs, self.yv, self.yh, self.yl = sems(
            nc, f"n{n}", "squared", "hi", "lo", "summed", "rstd", "y", "yh", "yl")


    def square(self, act, k, odd):
        act.wait_ge(self.lo, k - self.slots + 3)
        sq = self.sq[:, odd % self.slots, :]
        self.nc.scalar.activation(sq, row(self.m.H, k), ACT.Square).then_inc(self.squared, 1)
        act.wait_ge(self.summed, k + 1)
        act.wait_ge(self.squared, k + 1)
        self.nc.scalar.copy(self.sqh[:, odd, :], sq).then_inc(self.hi, 1)

    def square_low(self, dve, k, odd):
        dve.wait_ge(self.summed, k - self.slots + 3)
        dve.wait_ge(self.hi, k + 1)
        self.nc.vector.tensor_tensor(self.sql[:, odd % self.slots, :], self.sq[:, odd % self.slots, :],
                                     self.sqh[:, odd, :].bitcast(F32), ALU.subtract).then_inc(self.lo, 1)

    def sum(self, pe, k, odd, first=False, last=False):
        pe.wait_ge(self.lo, k + 3)
        for low, part in enumerate((self.sqh[:, odd, :], self.sql[:, odd % self.slots, :])):
            for half in range(2):
                cols = slice(half * HALF, half * HALF + HALF)
                ins = self.nc.tensor.matmul(strip_psum(self.m, 2)[:, cols], self.m.ones[:], part[:, cols],
                                            start=(first and not low), stop=(last and low == 1))
        ins.then_inc(self.summed, 1)

    def root(self, act):
        act.wait_ge(self.summed, KT + 2)
        self.nc.scalar.activation(self.lnv[:], strip_psum(self.m, 2), ACT.Ln, bias=self.m.eps[:, 0:1],
                                  scale=1.0 / D).then_inc(self.rs, 1)
        act.wait_ge(self.rs, 1)
        self.nc.scalar.activation(self.rstd[:], self.lnv[:], ACT.Exp, scale=-0.5).then_inc(self.rs, 1)

    def high_parts(self, act, split):
        for k in range(KT):
            if k < 2:
                split(k)
            act.wait_ge(self.yv, k + 1)
            self.nc.scalar.copy(self.m.XH[:, k, :], self.y[:, k % 2, :]).then_inc(self.yh, 1)

    def scaled(self, k, dst):
        self.nc.vector.scalar_tensor_tensor(out=dst, in0=self.m.H[:, k, :], scalar=self.m.gains[:, self.n, k:k + 1],
                                            in1=self.rstd[:], op0=ALU.mult, op1=ALU.mult).then_inc(self.yv, 1)

    def scale_and_low_parts(self, dve, split):
        def low_part(k):
            dve.wait_ge(self.yh, k + 1)
            self.nc.vector.tensor_tensor(self.m.XL[:, k, :], self.y[:, k % 2, :],
                                         self.m.XH[:, k, :].bitcast(F32), ALU.subtract).then_inc(self.yl, 1)

        dve.wait_ge(self.rs, 2)
        for k in range(KT):
            if k >= 2:
                dve.wait_ge(self.yl, k - 1)
            self.scaled(k, self.y[:, k % 2, :])
            if k < 2:
                split(k)
                low_part(k)
            elif k > 2:
                low_part(k - 1)
        low_part(KT - 1)


def load_input(nc, m, x, gains, norm):
    ones32 = m.at("ones32", m.big, [P, P])
    made, rounded, gains_in = sems(nc, "in", "made", "rounded", "gains")
    parts = sems(nc, "in", *[f"x{k}" for k in range(0, KT, 2)])
    with nc.Block() as block:
        @block.sync
        def _(sp):
            for k in range(0, KT, 2):
                sp.dma_start(m.H[:, k:k + 2, :], x[:, k:k + 2, :]).then_inc(parts[k // 2], 16)
            sp.dma_start(m.gains[:], gains).then_inc(gains_in, 16)
            sp.wait_ge(gains_in, 16)

        @block.gpsimd
        def _(pool):
            nc.gpsimd.memset(ones32[:], 1.0).then_inc(made, 1)
            nc.gpsimd.memset(m.ident[:], 0.0).then_inc(made, 1)
            pool.wait_ge(made, 2)
            nc.gpsimd.affine_select(out=m.ident[:], in_=m.ident[:], compare_op=ALU.not_equal, fill=1.0,
                                    base=0, pattern=[[-1, P]], channel_multiplier=1).then_inc(made, 1)
            nc.gpsimd.memset(m.eps[:], EPS).then_inc(made, 1)
            for h in range(HEADS):
                slope = float(np.float32(2.0 ** (-8.0 * (h + 1) / HEADS)))
                nc.gpsimd.memset(m.slopes[:, h:h + 1], slope).then_inc(made, 1)
            pool.wait_ge(made, 4 + HEADS)

        @block.scalar
        def _(act):
            for k in range(KT):
                if k % 2 == 0:
                    act.wait_ge(parts[k // 2], 16)
                norm.square(act, k, k % 2)

        @block.vector
        def _(dve):
            dve.sem_inc(norm.lo, 2)
            dve.wait_ge(made, 1)
            nc.vector.tensor_copy(m.ones[:], ones32[:]).then_inc(rounded, 1)
            for k in range(KT):
                norm.square_low(dve, k, k % 2)

        @block.tensor
        def _(pe):
            pe.sem_inc(norm.summed, 2)
            pe.wait_ge(rounded, 1)
            for k in range(KT):
                norm.sum(pe, k, k % 2, k == 0, k == KT - 1)


def store_normalised(nc, m, norm, out):
    stored, = sems(nc, "out", "stored")
    with nc.Block() as block:
        @block.scalar
        def _(act):
            norm.root(act)

        @block.vector
        def _(dve):
            dve.wait_ge(norm.rs, 2)
            for k in range(KT):
                norm.scaled(k, m.H[:, k, :])

        @block.sync
        def _(sp):
            for k in range(KT):
                sp.wait_ge(norm.yv, k + 1)
                sp.dma_start(out[:, k, :], m.H[:, k, :]).then_inc(stored, 16)
            sp.wait_ge(stored, 16 * KT)


class Strips:

    def __init__(self, nc, m, tag):
        self.nc, self.m = nc, m
        self.loaded = sems(nc, tag, "loaded0", "loaded1")
        self.high, self.low, self.multiplied, self.drained = sems(nc, tag, "high", "low", "multiplied", "drained")

    def load(self, sp, s, slot, src, n=KT, cols=P):
        sp.wait_ge(self.low, s + 1)
        sp.dma_start(self.m.W32[:, slot, 0:n, 0:cols], src).then_inc(self.loaded[slot], 16)

    def split_high(self, act, s, slot, rounds, n=KT, cols=P):
        act.wait_ge(self.loaded[slot], rounds * 16)
        act.wait_ge(self.multiplied, s + 1)
        self.nc.scalar.copy(self.m.WHI[:, slot, 0:n, 0:cols], self.m.W32[:, slot, 0:n, 0:cols]).then_inc(self.high, 1)

    def split_low(self, dve, s, slot, n=KT, cols=P):
        dve.wait_ge(self.high, s + 1)
        self.nc.vector.tensor_tensor(self.m.WLO[:, slot, 0:n, 0:cols], self.m.W32[:, slot, 0:n, 0:cols],
                                     self.m.WHI[:, slot, 0:n, 0:cols].bitcast(F32), ALU.subtract).then_inc(self.low, 1)

    def multiply(self, pe, s, slot, xh, xl, n=KT):
        pe.wait_ge(self.low, s + 3)
        strip_products(self.nc, strip_psum(self.m, slot), self.m.WHI[:, slot], self.m.WLO[:, slot],
                       xh, xl, n).then_inc(self.multiplied, 1)


def first_pair(nc, m, st, pe, ready):
    for k in range(KT):
        pe.wait_ge(ready, k + 1)
        for slot in range(2):
            if k == 0:
                pe.wait_ge(st.low, slot + 3)
            last = strip_tile_products(nc, strip_psum(m, slot), m.WHI[:, slot], m.WLO[:, slot], m.XH, m.XL, k, KT)
            if k == KT - 1:
                last.then_inc(st.multiplied, 1)


def strip_of(w, s, n=KT, k0=0):
    return w[bass.ds(s, 1), :, k0:k0 + n, :].rearrange("a p k c -> (a p) k c")


def row(t, i):
    return t[:, bass.ds(i, 1), :].rearrange("p a n -> p (a n)")


def nsa_projection(nc, m, norm, w_in, w_gate, gate_b):
    st = Strips(nc, m, "ni")
    biased, gated, bias_loaded = sems(nc, "ni", "biased", "gated", "bias")
    GC = BRANCHES * HEADS
    N = NSA_TILES
    with nc.Block() as block:
        @block.sync
        def _(sp):
            sp.dma_start(m.gate_bias[:], gate_b.partition_broadcast(P)).then_inc(bias_loaded, 16)
            with sp.Fori(0, N // 2) as i:
                for slot in range(2):
                    st.load(sp, 2 * i + slot, slot, strip_of(w_in, 2 * i + slot))
            st.load(sp, N, 0, w_gate, cols=GC)

        @block.scalar
        def _(act):
            norm.root(act)
            norm.high_parts(act, lambda n: st.split_high(act, n, n, 1))
            with act.Fori(1, N // 2) as i:
                for slot in range(2):
                    st.split_high(act, 2 * i + slot, slot, i + 1)
            st.split_high(act, N, 0, N // 2 + 1, cols=GC)
            act.wait_ge(biased, 1)
            nc.scalar.activation(m.gates[:], m.gates[:], ACT.Sigmoid).then_inc(gated, 1)

        @block.vector
        def _(dve):
            def drain(s, slot):
                dve.wait_ge(st.multiplied, s + 3)
                nc.vector.tensor_copy(row(m.proj, s), strip_psum(m, slot)).then_inc(st.drained, 1)

            dve.sem_inc(st.low, 2)
            dve.sem_inc(st.drained, 2)
            norm.scale_and_low_parts(dve, lambda n: st.split_low(dve, n, n))
            with dve.Fori(0, N // 2 - 1) as i:
                for slot in range(2):
                    drain(2 * i + slot, slot)
                    st.split_low(dve, 2 * i + slot + 2, slot)
            drain(N - 2, 0)
            st.split_low(dve, N, 0, cols=GC)
            drain(N - 1, 1)
            dve.wait_ge(st.multiplied, N + 3)
            dve.wait_ge(bias_loaded, 16)
            for t in range(QT):
                last = nc.vector.tensor_tensor(m.gates[:, t, :], m.PS[:, 0, t * GC:(t + 1) * GC],
                                               m.gate_bias[:], ALU.add)
            last.then_inc(biased, 1)

        @block.tensor
        def _(pe):
            pe.sem_inc(st.multiplied, 2)
            first_pair(nc, m, st, pe, norm.yl)
            with pe.Fori(1, N // 2) as i:
                for slot in range(2):
                    pe.wait_ge(st.drained, 2 * i + slot + 1)
                    st.multiply(pe, 2 * i + slot, slot, m.XH, m.XL)
            pe.wait_ge(st.low, N + 3)
            pe.wait_ge(st.drained, N + 1)
            for t in range(QT):
                rows = slice(t * P, (t + 1) * P)
                for k in range(KT):
                    for x, w in ((m.XH, m.WHI), (m.XL, m.WHI), (m.XH, m.WLO)):
                        last = nc.tensor.matmul(m.PS[:, 0, t * GC:(t + 1) * GC], x[:, k, rows], w[:, 0, k, 0:GC],
                                                start=(k == 0 and w is m.WHI and x is m.XH),
                                                stop=(k == KT - 1 and w is m.WLO))
            last.then_inc(st.multiplied, 1)


def add_residual(nc, m, st, dve, tile, slot, s):
    dve.wait_ge(st.multiplied, s + 3)
    nc.vector.tensor_tensor(row(m.H, tile), row(m.H, tile), strip_psum(m, slot), ALU.add).then_inc(st.drained, 1)


def residual_projection(nc, m, tag, w, norm, h_store=None):
    st = Strips(nc, m, tag)
    oh, ol, reloaded = sems(nc, tag, "oh", "ol", "reloaded")
    with nc.Block() as block:
        @block.sync
        def _(sp):
            for slot in range(2):
                st.load(sp, slot, slot, strip_of(w, slot))
            if h_store is not None:
                for k in range(0, KT, 2):
                    sp.dma_start(m.H[:, k:k + 2, :], h_store[:, k:k + 2, :]).then_inc(reloaded, 16)
            with sp.Fori(1, KT // 2) as i:
                for slot in range(2):
                    st.load(sp, 2 * i + slot, slot, strip_of(w, 2 * i + slot))

        @block.scalar
        def _(act):
            for k in range(KT):
                nc.scalar.copy(m.XH[:, k, :], m.proj[:, k, :]).then_inc(oh, 1)
                if k < 2:
                    st.split_high(act, k, k, 1)
            with act.Fori(1, KT // 2) as i:
                for slot in range(2):
                    st.split_high(act, 2 * i + slot, slot, i + 1)
                    square_added(act, norm, st, 2 * i + slot - 2, slot, 0)
            for slot in range(2):
                square_added(act, norm, st, KT - 2 + slot, slot, 0)

        @block.vector
        def _(dve):
            dve.sem_inc(st.low, 2)
            dve.sem_inc(st.drained, 2)
            dve.sem_inc(norm.lo, 2)
            for k in range(KT):
                dve.wait_ge(oh, k + 1)
                nc.vector.tensor_tensor(m.XL[:, k, :], m.proj[:, k, :], m.XH[:, k, :].bitcast(F32),
                                        ALU.subtract).then_inc(ol, 1)
                if k < 2:
                    st.split_low(dve, k, k)
            if h_store is not None:
                dve.wait_ge(reloaded, 16 * KT // 2)
            with dve.Fori(0, KT // 2 - 1) as i:
                for slot in range(2):
                    add_residual(nc, m, st, dve, 2 * i + slot, slot, 2 * i + slot)
                    st.split_low(dve, 2 * i + slot + 2, slot)
                    norm.square_low(dve, 2 * i + slot, slot)
            for slot in range(2):
                add_residual(nc, m, st, dve, KT - 2 + slot, slot, KT - 2 + slot)
                norm.square_low(dve, KT - 2 + slot, slot)

        @block.tensor
        def _(pe):
            pe.sem_inc(st.multiplied, 2)
            pe.sem_inc(norm.summed, 2)
            first_pair(nc, m, st, pe, ol)
            norm.sum(pe, 0, 0, first=True)
            with pe.Fori(1, KT // 2) as i:
                for slot in range(2):
                    pe.wait_ge(st.drained, 2 * i + slot + 1)
                    st.multiply(pe, 2 * i + slot, slot, m.XH, m.XL)
                    norm.sum(pe, 2 * i + slot - 1, 1 - slot)
            norm.sum(pe, KT - 1, 1, last=True)


def square_added(act, norm, st, tile, odd, before):
    act.wait_ge(st.drained, before + tile + 3)
    norm.square(act, tile, odd)


def ffn(nc, m, layer, w1, w3, w2, norm, next_norm):
    t = SEQ * 4
    tag = f"f{layer}"
    mh = m.at(f"mh{tag}", m.big, [P, 8, SEQ], F32R)
    ml = m.at(f"ml{tag}", m.big + 8 * t, [P, 8, SEQ], F32R)
    sil = m.at(f"sil{tag}", m.big + 16 * t, [P, SEQ])
    prod = m.at(f"prod{tag}", m.big + 17 * t, [P, SEQ])
    st = Strips(nc, m, tag)
    silu, mul, mhi, mlo = sems(nc, tag, "silu", "mul", "mhi", "mlo")
    chunks = [(sum(FFN_CHUNKS[:c]), nf, 2 * sum(FFN_CHUNKS[:c]) + KT * c, KT * c, c == len(FFN_CHUNKS) - 1)
              for c, nf in enumerate(FFN_CHUNKS)]
    with nc.Block() as block:
        @block.sync
        def _(sp):
            for f0, nf, s0, _, _ in chunks:
                with sp.Fori(0, nf) as i:
                    for slot, w in ((0, w1), (1, w3)):
                        st.load(sp, 2 * i + slot + s0, slot, strip_of(w, i + f0))
                with sp.Fori(0, KT // 2) as i:
                    for slot in range(2):
                        st.load(sp, 2 * i + slot + s0 + 2 * nf, slot, strip_of(w2, 2 * i + slot, nf, f0), nf)

        @block.scalar
        def _(act):
            def split(s, slot, n=KT):
                st.split_high(act, s, slot, (s - slot) // 2 + 1, n)

            def gate(s0, f0, i, between):
                act.wait_ge(st.multiplied, s0 + 2 * i + 3)
                act.wait_ge(mul, f0 + i + 1)
                nc.scalar.activation(sil[:], strip_psum(m, 0), ACT.Silu).then_inc(silu, 1)
                between()
                act.wait_ge(mul, f0 + i + 2)
                nc.scalar.copy(row(mh, i), prod[:]).then_inc(mhi, 1)

            norm.root(act)
            norm.high_parts(act, lambda n: split(n, n))
            for f0, nf, s0, before, final in chunks:
                n1 = s0 + 2 * nf
                with act.Fori(0, nf - 1) as i:
                    gate(s0, f0, i, lambda: st.split_high(act, 2 * i + 2 + s0, 0, i + 2 + s0 // 2))
                    st.split_high(act, 2 * i + 3 + s0, 1, i + 2 + s0 // 2)
                gate(s0, f0, nf - 1, lambda: split(n1, 0, nf))
                split(n1 + 1, 1, nf)
                with act.Fori(1, KT // 2) as i:
                    for slot in range(2):
                        st.split_high(act, 2 * i + slot + n1, slot, i + n1 // 2 + 1, nf)
                        if final:
                            square_added(act, next_norm, st, 2 * i + slot - 2, slot, before)
                for slot in range(2):
                    if final:
                        square_added(act, next_norm, st, KT - 2 + slot, slot, before)
                    else:
                        split(n1 + KT + slot, slot)

        @block.vector
        def _(dve):
            def product(s0, f0, i):
                dve.wait_ge(st.multiplied, s0 + 2 * i + 4)
                dve.wait_ge(silu, f0 + i + 1)
                dve.wait_ge(mlo, f0 + i + 1)
                nc.vector.tensor_tensor(prod[:], sil[:], strip_psum(m, 1), ALU.mult).then_inc(mul, 1)
                dve.wait_ge(mhi, f0 + i + 1)
                nc.vector.tensor_tensor(row(ml, i), prod[:], row(mh, i).bitcast(F32), ALU.subtract).then_inc(mlo, 1)

            dve.sem_inc(st.low, 2)
            dve.sem_inc(mul, 1)
            dve.sem_inc(mlo, 1)
            dve.sem_inc(next_norm.lo, 2)
            norm.scale_and_low_parts(dve, lambda n: st.split_low(dve, n, n))
            for f0, nf, s0, before, final in chunks:
                n1 = s0 + 2 * nf
                with dve.Fori(0, nf - 1) as i:
                    st.split_low(dve, 2 * i + 2 + s0, 0)
                    product(s0, f0, i)
                    st.split_low(dve, 2 * i + 3 + s0, 1)
                st.split_low(dve, n1, 0, nf)
                product(s0, f0, nf - 1)
                st.split_low(dve, n1 + 1, 1, nf)
                with dve.Fori(0, KT // 2 - 1) as i:
                    for slot in range(2):
                        add_residual(nc, m, st, dve, 2 * i + slot, slot, 2 * i + slot + n1)
                        st.split_low(dve, 2 * i + slot + 2 + n1, slot, nf)
                        if final:
                            next_norm.square_low(dve, 2 * i + slot, slot)
                for slot in range(2):
                    add_residual(nc, m, st, dve, KT - 2 + slot, slot, KT - 2 + slot + n1)
                    if final:
                        next_norm.square_low(dve, KT - 2 + slot, slot)
                    else:
                        st.split_low(dve, n1 + KT + slot, slot)

        @block.tensor
        def _(pe):
            pe.sem_inc(st.multiplied, 2)
            pe.sem_inc(st.drained, 2)
            pe.sem_inc(next_norm.summed, 2)
            for f0, nf, s0, before, final in chunks:
                n1 = s0 + 2 * nf
                if f0 == 0:
                    first_pair(nc, m, st, pe, norm.yl)
                else:
                    for slot in range(2):
                        pe.wait_ge(st.drained, before + 1 + slot)
                        st.multiply(pe, s0 + slot, slot, m.XH, m.XL)
                with pe.Fori(1, nf) as i:
                    pe.wait_ge(silu, f0 + i)
                    st.multiply(pe, 2 * i + s0, 0, m.XH, m.XL)
                    pe.wait_ge(mul, f0 + i + 1)
                    st.multiply(pe, 2 * i + 1 + s0, 1, m.XH, m.XL)
                pe.wait_ge(silu, f0 + nf)
                pe.wait_ge(st.low, n1 + 3)
                pe.wait_ge(mlo, f0 + nf)
                for k in range(nf):
                    if k == nf - 1:
                        pe.wait_ge(mlo, f0 + nf + 1)
                    ins = strip_tile_products(nc, strip_psum(m, 0), m.WHI[:, 0], m.WLO[:, 0], mh, ml, k, nf)
                ins.then_inc(st.multiplied, 1)
                st.multiply(pe, n1 + 1, 1, mh, ml, nf)
                if final:
                    next_norm.sum(pe, 0, 0, first=True)
                with pe.Fori(1, KT // 2) as i:
                    for slot in range(2):
                        pe.wait_ge(st.drained, 2 * i + slot + 1 + before)
                        st.multiply(pe, 2 * i + slot + n1, slot, mh, ml, nf)
                        if final:
                            next_norm.sum(pe, 2 * i + slot - 1, 1 - slot)
                if final:
                    next_norm.sum(pe, KT - 1, 1, last=True)


def nsa_memory(m):
    t = SEQ * 4
    o = m.xr
    m.Q1 = m.at("Q1", o, [P, HPG, SEQ], F32R); o += HPG * t
    m.Q2 = m.at("Q2", o, [P, HPG, HALF], F32R); o += HPG * HALF * 4
    m.KS1 = m.at("KS1", o, [P, SEQ], F32R); o += t
    m.KS2 = m.at("KS2", o, [P, SEQ], F32R); o += t
    m.KW1 = m.at("KW1", o, [P, SEQ], F32R); o += t
    m.KW2 = m.at("KW2", o, [P, SEQ], F32R); o += t
    m.BS = m.at("BS", o, [P, 2, SEQ]); o += 2 * t
    m.T = m.at("T", o, [P, TS, SEQ])
    m.TMPQ = m.at("TMPQ", o + 2 * t, [P, 2, SEQ])
    o += TS * t
    assert o <= m.st
    o = m.st
    m.DIST = m.at("DIST", o, [P, SEQ]); o += t
    m.VWG = m.at("VWG", o, [P, QT, HD]); o += QT * HD * 4
    m.VCG = m.at("VCG", o, [P, 2, HD]); o += 2 * HD * 4
    m.BW = m.at("BW", o, [P, 2, WIN + P]); o += 2 * (WIN + P) * 4
    m.DISTC = m.at("DISTC", o, [P, QT, NCP]); o += QT * NCP * 4
    m.LOWER = m.at("LOWER", o, [P, NBLK, NBLK]); o += NBLK * NBLK * 4
    m.FORCED = m.at("FORCED", o, [P, QT // 2, NBLK]); o += QT // 2 * NBLK * 4
    m.KC1G = m.at("KC1G", o, [P, NCP], F32R)
    m.KC2G = m.at("KC2G", o + NCP * 4, [P, NCP], F32R)
    assert QT // 2 * NBLK == NCP
    m.IMP = m.at("IMP", o, [P, QT // 2, NBLK]); o += QT // 2 * NBLK * 4
    m.RANK = m.at("RANK", o, [P, QT // 2, NBLK]); o += QT // 2 * NBLK * 4
    m.NM = m.at("NM", o, [P, 2 * TS]); o += 2 * TS * 4
    m.SUM = m.at("SUM", o, [P, 2 * TS]); o += 2 * TS * 4
    m.REC = m.at("REC", o, [P, 2 * TS]); o += 2 * TS * 4
    m.MX = m.at("MX", o, [P, 2, 2 * QT]); o += 32 * 4
    m.DEN = m.at("DEN", o, [P, 2, 2 * QT]); o += 32 * 4
    m.SOME = m.at("SOME", o, [P, 8]); o += 32
    m.PTC = m.at("PTC", o, [P, HPG, HALF]); o += HPG * HALF * 4
    assert o <= m.big
    m.VS = m.at("VS", m.big + 8 * t, [P, QT, KVW])
    m.VW = m.at("VW", m.big + 10 * t, [P, QT, KVW])
    m.PT = m.at("PT", m.big + 16 * t, [P, 2, QT, 2 * P])
    m.IND = m.at("IND", m.xr + 16 * t - t, [P, SEQ])
    o = m.small_end
    m.KC1 = m.at("KC1", o, [P, GROUPS, NCP], F32R); o += GROUPS * NCP * 4
    m.KC2 = m.at("KC2", o, [P, GROUPS, NCP], F32R); o += GROUPS * NCP * 4
    m.VC = m.at("VC", o, [P, GROUPS, HD]); o += GROUPS * HD * 4
    m.VSG = m.at("VSG", o, [P, QT, HD]); o += QT * HD * 4
    m.PG = m.at("PG", m.xr + 11 * t, [P, QT // 2, NCP])
    m.LARGER = m.at("LARGER", m.xr + 11 * t + 1024, [P, NBLK, NBLK])
    m.EQUAL = m.at("EQUAL", m.xr + 11 * t + 2048, [P, NBLK, NBLK])
    assert o <= 229368, o


def nsa_compress(nc, m, cmp_w1, cmp_w2, cmp_pe):
    t = SEQ * 4
    o = m.xr
    w1 = m.at("cw1", o, [P, 2, KT * 2, HID]); o += 2 * 2 * KT * HID * 4
    x2 = m.at("cx2", o, [P, 2, GROUPS + 1, CMP_STEP // 2, NCP]); o += 2 * (GROUPS + 1) * CMP_STEP // 2 * NCP * 4
    gel = m.at("cgel", o, [P, 2, 2, GROUPS, NCP]); o += 4 * GROUPS * NCP * 4
    w2 = m.at("cw2", o, [P, 2, 2, HD]); o += 4 * HD * 4
    pe_ = m.at("cpe", o, [P, 2, 2 * KT]); o += 4 * KT * 4
    hb = m.at("chb", o, [P, 4]); o += 16
    kc = m.at("ckc", o + 16, [P, GROUPS, NCP]); o += GROUPS * NCP * 4 + 16
    assert o <= m.st
    used = sems(nc, "c", "loadedv", "loaded", "placed", "pairsa", "pairsv", "biaskept", "hidden", "gelu", "zero",
                "kready", "vready", "kckept", "kchi", "kcdone", "turned", "vtkept", "made", "vcdone", "vzero")
    loaded_v, loaded, placed, pairs_a, pairs_v, bias_kept, hidden, gelu, zero, kready, vready, kc_kept, kc_hi, \
        kc_done, turned, vt_kept, made, vc_done, vzero = used
    MM = CMP_LEN // 2
    with nc.Block() as block:
        @block.sync
        def _(sp):
            sp.dma_start(pe_[:], cmp_pe).then_inc(loaded, 16)
            sp.dma_start(w1[:, 0], cmp_w1[:, 0]).then_inc(loaded, 16)
            sp.dma_start(w2[:], cmp_w2).then_inc(loaded, 16)
            sp.dma_start(w1[:, 1], cmp_w1[:, 1]).then_inc(loaded_v, 16)

        def pair_copies(which):
            for g in range(GROUPS):
                src = m.proj[HD * (g % 2):HD * (g % 2) + HD, 8 + 2 * which + g // 2, :].rearrange(
                    "p (n r a) -> p a r n", r=CMP_STEP // 2, a=2)
                for par in range(2):
                    yield x2[HD * par:HD * par + HD, which, g], src[:, par]

        @block.scalar
        def _(act):
            for dst, src in pair_copies(0):
                last = nc.scalar.copy(dst, src)
            last.then_inc(pairs_a, 1)
            def keep_turned(n):
                act.wait_ge(turned, n + 1)
                v = m.VS if n < 2 else m.VW
                nc.scalar.copy(v[:, :, (n % 2) * P:(n % 2) * P + P],
                               strip_psum(m, 2 + n % 2).rearrange("p (t c) -> p t c", c=P)).then_inc(vt_kept, 1)

            act.wait_ge(pairs_a, 1)
            act.wait_ge(pairs_v, 1)
            for n in range(4):
                keep_turned(n)
            act.wait_ge(zero, 1)
            for n in range(4):
                act.wait_ge(bias_kept, n + 1)
                nc.scalar.activation(gel[:, n // 2, n % 2, :, 0:NC],
                                     m.PS[:, n % 2, 0:GROUPS * NC].rearrange("p (g n) -> p g n", g=GROUPS),
                                     ACT.Gelu_apprx_tanh, bias=hb[:, n:n + 1]).then_inc(gelu, 1)
            act.wait_ge(kc_kept, 1)
            nc.scalar.copy(m.KC1[0:HD], kc[0:HD]).then_inc(kc_hi, 1)

        @block.vector
        def _(dve):
            nc.vector.memset(gel[:], 0.0).then_inc(zero, 1)
            nc.vector.memset(x2[:, :, GROUPS], 0.0).then_inc(zero, 1)
            nc.vector.memset(m.VCG[:], 0.0).then_inc(vzero, 1)
            for dst, src in pair_copies(1):
                last = nc.vector.tensor_copy(dst, src)
            last.then_inc(pairs_v, 1)
            dve.wait_ge(loaded, 48)
            dve.wait_ge(zero, 2)
            for which in range(2):
                last = nc.vector.tensor_copy(x2[:, which, GROUPS, :, 0:2], pe_[:, which].rearrange("p (a r) -> p r a", a=2))
            last.then_inc(placed, 1)
            for n in range(4):
                dve.wait_ge(hidden, n + 1)
                nc.vector.tensor_copy(hb[:, n:n + 1], m.PS[:, n % 2, GROUPS * NC:GROUPS * NC + 1]).then_inc(bias_kept, 1)
            dve.wait_ge(kready, 1)
            nc.vector.tensor_copy(kc[0:HD], m.PS[0:HD, 2, 0:GROUPS * NCP].rearrange("p (g n) -> p g n", g=GROUPS)
                                  ).then_inc(kc_kept, 1)
            dve.wait_ge(kc_hi, 1)
            nc.vector.tensor_copy(m.KC1[HD:P], m.KC1[0:HD].bitcast(F32)).then_inc(kc_done, 1)
            nc.vector.tensor_tensor(m.KC2[0:HD], kc[0:HD], m.KC1[0:HD].bitcast(F32), ALU.subtract).then_inc(kc_done, 1)
            dve.wait_ge(vready, 1)
            dve.wait_ge(vzero, 1)
            for half in range(2):
                nc.vector.tensor_copy(m.VC[HD * half:HD * half + HD],
                                      m.PS[0:NCP, 3, 0:KVW].rearrange("p (g d) -> p g d", g=GROUPS)).then_inc(vc_done, 1)

        @block.tensor
        def _(pe):
            for n in range(4):
                if n >= 2:
                    pe.wait_ge(vt_kept, n - 1)
                for kt in range(QT):
                    last = nc.tensor.transpose(strip_psum(m, 2 + n % 2)[:, kt * P:(kt + 1) * P],
                                               m.proj[:, 16 + n, kt * P:(kt + 1) * P], m.ident[:])
                last.then_inc(turned, 1)
            pe.wait_ge(loaded, 48)
            pe.wait_ge(placed, 1)
            pe.wait_ge(pairs_a, 1)
            for n in range(4):
                if n == 2:
                    pe.wait_ge(pairs_v, 1)
                    pe.wait_ge(loaded_v, 16)
                if n >= 2:
                    pe.wait_ge(gelu, n - 1)
                for mm in range(MM):
                    r, first = mm % (CMP_STEP // 2), mm // (CMP_STEP // 2)
                    last = nc.tensor.matmul(m.PS[:, n % 2, 0:(GROUPS + 1) * NC].rearrange("p (g n) -> p g n", g=GROUPS + 1),
                                            w1[:, n // 2, mm, (n % 2) * P:(n % 2) * P + P],
                                            x2[:, n // 2, :, r, first:first + NC],
                                            start=(mm == 0), stop=(mm == MM - 1))
                last.then_inc(hidden, 1)
            pe.wait_ge(gelu, 4)
            pe.wait_ge(vt_kept, 4)
            for half in range(2):
                last = nc.tensor.matmul(m.PS[0:HD, 2, 0:GROUPS * NCP], w2[:, 0, half, :],
                                        gel[:, 0, half, :, :].rearrange("p g n -> p (g n)"), start=(half == 0), stop=(half == 1))
            last.then_inc(kready, 1)
            for g in range(GROUPS):
                for half in range(2):
                    last = nc.tensor.matmul(m.PS[0:NCP, 3, g * HD:(g + 1) * HD], gel[:, 1, half, g, :], w2[:, 1, half, :],
                                            start=(half == 0), stop=(half == 1))
            last.then_inc(vready, 1)

        @block.gpsimd
        def _(pool):
            count = 0

            def put(ins):
                nonlocal count
                count += 1
                ins.then_inc(made, 1)
                pool.wait_ge(made, count)

            def keep(out, op, base, pattern, mult, fill):
                put(nc.gpsimd.affine_select(out=out, in_=out, compare_op=op, fill=fill, base=base,
                                            pattern=pattern, channel_multiplier=mult))

            exact = dict(allow_small_or_imprecise_dtypes=True)
            put(nc.gpsimd.iota(m.DIST[:], pattern=[[1, SEQ]], base=P - SEQ, channel_multiplier=-1, **exact))
            keep(m.DIST[:], ALU.is_ge, SEQ - P, [[-1, SEQ]], 1, -BIG)
            put(nc.gpsimd.iota(m.DISTC[:], pattern=[[-P, QT], [CMP_STEP, NCP]], base=CMP_LEN - 1,
                               channel_multiplier=-1, **exact))
            keep(m.DISTC[:], ALU.is_ge, 1 - CMP_LEN, [[P, QT], [-CMP_STEP, NCP]], 1, -BIG)
            put(nc.gpsimd.memset(m.SOME[:], 1.0))
            keep(m.SOME[:], ALU.is_ge, 1 - CMP_LEN, [[0, 8]], 1, 0.0)
            put(nc.gpsimd.memset(m.LOWER[:], 1.0))
            keep(m.LOWER[:], ALU.is_gt, 0, [[1, NBLK], [-1, NBLK]], 0, 0.0)
            put(nc.gpsimd.memset(m.FORCED[:], 0.0))
            put(nc.gpsimd.memset(m.FORCED[:, :, 0:1], BIG))
            for q in range(QT // 2):
                for half in range(2):
                    cur = (q + QT // 2) * (P // BLK) + half
                    rows = m.FORCED[half * BLK:half * BLK + BLK, q]
                    put(nc.gpsimd.memset(rows[:, cur - 1:cur + 1], BIG))
                    if cur + 1 < NBLK:
                        put(nc.gpsimd.memset(rows[:, cur + 1:], -BIG))
            ind = m.IND[HD:HD + NBLK, :]
            put(nc.gpsimd.memset(ind, 1.0))
            keep(ind, ALU.is_ge, 0, [[1, SEQ]], -BLK, 0.0)
            keep(ind, ALU.is_ge, BLK - 1, [[-1, SEQ]], BLK, 0.0)
    return used


TS = 4
UNITS = [(h, 2 * i + p, b) for h in range(HPG) for i in range(QT // 2) for b in range(2) for p in range(2)]
NU = len(UNITS)
UPH = 2 * QT
NB = NU // 2
BPH = NB // HPG


def unit_tiles(u):
    _, q, b = UNITS[u]
    return (q - min(q, WT), q + 1) if b else (0, q + 1)


def chunk_table():
    out = []
    for u in range(len(UNITS)):
        a, b = unit_tiles(u)
        n = b - a
        cut = b if n <= 4 else a + (3 if n == 5 else 4)
        out.append([(a, cut)] + ([(cut, b)] if cut < b else []))
    return out


CHUNKS = chunk_table()
FIRST_CHUNK = [HPG + sum(len(c) for c in CHUNKS[:u]) for u in range(len(UNITS) + 1)]
NCH = FIRST_CHUNK[-1]
NS = HPG + NU
MASKED_FROM = next(u for u, (_, q, b) in enumerate(UNITS) if q >= QT // 2 and b == 0)
MASK_AT = MASKED_FROM - 2
assert NS % 2 == 0 and NCH % 2 == 0


def nsa_attention(nc, m):
    st_t, st_h, st_l, st_c, s_ready, s_free, c_sub, c_exp, c_p, pt_t, kept, pv, drained, mk, mk_t, q2m, \
        b_r, b_w, v_r, p_r, scaled, ch, ind_r, begun, begun_p = sems(
            nc, "a", "shifted", "high", "low", "copied", "scores", "scorefree", "csub", "cexp", "cp", "turned", "kept",
            "values", "drained", "mask", "maskturned", "maskkept", "bias", "windowbias", "valuesready", "probs", "scaled",
            "chain", "ind", "begun", "begunpool")
    CHAIN = HPG // 2 * 7 + 5 + QT // 2 * 4 + NU

    def ptslot(c):
        return m.PS[:, 4 + c % 2, :]

    with nc.Block() as block:
        @block.scalar
        def _(act):
            act.activation(m.KS2[HD:HD + NBLK, :], m.IND[HD:HD + NBLK, :], ACT.Copy).then_inc(ind_r, 1)
            act.sem_inc(kept, 2)
            with act.Fori(0, GROUPS // 2) as j:
                for gi in range(2):
                    g = 2 * j + gi
                    act.wait_ge(pv, NB * g + 2)

                    def bias(h):
                        nc.scalar.activation(m.BS[:, h % 2, :], m.DIST[:], ACT.Copy,
                                             scale=m.slopes[:, bass.ds(HPG * g + h, 1)])
                        nc.scalar.activation(m.BW[:, h % 2, :], m.DIST[:, SEQ - WIN - P:], ACT.Copy,
                                             scale=m.slopes[:, bass.ds(HPG * g + h, 1)]).then_inc(b_r, 1)

                    def stage(n):
                        if n < HPG:
                            src = m.proj[HD * (n % 2):HD * (n % 2) + HD, bass.ds(2 * g + n // 2, 1), :]
                            hi = m.Q1[0:HD, n, :]
                        else:
                            src = m.proj[HD * gi:HD * gi + HD, bass.ds((12, 14)[n - HPG] + j, 1), :]
                            hi = (m.KS1, m.KW1)[n - HPG][0:HD, :]
                        if n >= 2:
                            act.wait_ge(st_l, (2 + HPG) * g + n - 1)
                        else:
                            act.wait_ge(ind_r, 1)
                        nc.scalar.activation(m.TMPQ[0:HD, n % 2, :], src.rearrange("p a n -> p (a n)"), ACT.Copy,
                                             scale=QSCALE if n < HPG else 1.0).then_inc(st_t, 1)
                        act.wait_ge(st_t, (2 + HPG) * g + n + 1)
                        nc.scalar.copy(hi, m.TMPQ[0:HD, n % 2, :]).then_inc(st_h, 1)

                    for n in range(HPG):
                        stage(n)
                    for pair in range(HPG // 2 + 1):
                        if pair < HPG // 2:
                            stage(HPG + pair)
                            act.wait_ge(c_sub, HPG // 2 * g + pair + 1)
                            nc.scalar.activation(m.T[:, pair, :], m.T[:, pair, :], ACT.Exp).then_inc(c_exp, 1)
                        if pair == HPG // 2 - 1:
                            bias(0)
                        if pair >= 1:
                            for h in (2 * pair - 2, 2 * pair - 1):
                                act.wait_ge(pt_t, NCH * g + h + 1)
                                nc.scalar.copy(m.PTC[:, h, :], ptslot(h)).then_inc(kept, 1)
                    def keep_mask():
                        act.wait_ge(mk_t, g + 1)
                        for h in range(HPG):
                            nc.scalar.copy(m.Q2[HD:HD + NBLK, h, :], m.PS[0:NBLK, 7, :]).then_inc(q2m, 1)

                    def exponentials(u):
                        a, e = unit_tiles(u)
                        t = m.T[:, u % TS, 0:(e - a) * P]
                        act.wait_ge(s_free, NS * g + HPG + u + 3)
                        nc.scalar.activation(t, t, ACT.Exp, bias=m.NM[:, u % TS:u % TS + 1], scale=-1.0,
                                             accum_out=m.SUM[:, u % TS:u % TS + 1]).then_inc(p_r, 1)

                    def keep(u):
                        block_, p = u // 2, u % 2
                        for c, (t0, t1) in zip(range(FIRST_CHUNK[u], FIRST_CHUNK[u + 1]), CHUNKS[u]):
                            act.wait_ge(pt_t, NCH * g + c + 1)
                            act.wait_ge(pv, NB * g + block_ + 1)
                            nc.scalar.copy(m.PT[:, block_ % 2, t0:t1, p * P:p * P + P],
                                           ptslot(c)[:, 0:(t1 - t0) * P].rearrange("p (t n) -> p t n", n=P)
                                           ).then_inc(kept, 1)

                    for v in range(1, NU + 3):
                        if v <= NU:
                            exponentials(v - 1)
                        if v == MASK_AT:
                            keep_mask()
                        if v >= 3:
                            keep(v - 3)
                        if v % UPH == UPH // 2 and v // UPH + 1 < HPG:
                            bias(v // UPH + 1)

        @block.gpsimd
        def _(pool):
            with pool.Fori(0, GROUPS // 2) as j:
                for h in range(2 * HPG):
                    if h % HPG == 0:
                        for n in range(2 + HPG):
                            pool.wait_ge(st_h, (2 + HPG) * (2 * j + h // HPG) + n + 1)
                            pool.sem_inc(begun_p, 1)
                            if n < HPG:
                                nc.gpsimd.tensor_copy(m.Q2[0:HD, n, :], m.Q1[0:HD, n, HALF:].bitcast(F32)
                                                      ).then_inc(st_c, 1)
                            else:
                                k1 = (m.KS1, m.KW1)[n - HPG]
                                nc.gpsimd.tensor_copy(k1[HD:P, :], k1[0:HD, :].bitcast(F32)).then_inc(st_c, 1)
                        pool.wait_ge(st_c, (2 + HPG) * (2 * j + h // HPG + 1))
                    pool.wait_ge(b_r, 2 * HPG * j + h + 1)
                    pool.sem_inc(begun_p, 1)
                    nc.gpsimd.affine_select(out=m.BW[:, h % 2, 0:P], in_=m.BW[:, h % 2, 0:P], compare_op=ALU.is_gt,
                                            fill=-BIG, base=0, pattern=[[1, P]], channel_multiplier=-1).then_inc(b_w, 1)
                    pool.wait_ge(b_w, 2 * HPG * j + h + 1)

        @block.vector
        def _(dve):
            dve.sem_inc(s_free, 2)
            dve.sem_inc(drained, 2)
            with dve.Fori(0, GROUPS // 2) as j:
                for gi in range(2):
                    g = 2 * j + gi
                    links = 0

                    def link(ins):
                        nonlocal links
                        links += 1
                        ins.then_inc(ch, 1)
                        dve.wait_ge(ch, CHAIN * g + links)

                    dve.wait_ge(pv, NB * g + 2)
                    nc.vector.tensor_copy(m.KC1G[:], row(m.KC1, g).bitcast(F32))
                    nc.vector.tensor_copy(m.KC2G[0:HD], m.KC2[0:HD, bass.ds(g, 1), :].rearrange("p a n -> p (a n)").bitcast(F32))

                    def stack_low(n):
                        dve.wait_ge(st_h, (2 + HPG) * g + n + 1)
                        if n < HPG:
                            q1 = m.Q1[:, n, :]
                            nc.vector.tensor_tensor(q1[HD:P, :], m.TMPQ[0:HD, n % 2, :], q1[0:HD, :].bitcast(F32),
                                                    ALU.subtract).then_inc(st_l, 1)
                        else:
                            k1, k2 = ((m.KS1, m.KS2), (m.KW1, m.KW2))[n - HPG]
                            nc.vector.tensor_tensor(k2[0:HD, :], m.TMPQ[0:HD, n % 2, :], k1[0:HD, :].bitcast(F32),
                                                    ALU.subtract).then_inc(st_l, 1)

                    for n in range(HPG):
                        stack_low(n)

                    HT = 2 * QT

                    def over_positions(x):
                        return x.unsqueeze(2).broadcast_to([P, HT, NCP])

                    for pair in range(HPG // 2 + 1):
                        if pair < HPG // 2:
                            t = m.T[:, pair, :].rearrange("p (t n) -> p t n", n=NCP)
                            for i in range(2):
                                h = 2 * pair + i
                                dve.wait_ge(s_ready, NS * g + h + 1)
                                nc.vector.scalar_tensor_tensor(
                                    out=m.T[:, pair, i * HALF:(i + 1) * HALF],
                                    in0=m.DISTC[:].rearrange("p t n -> p (t n)"),
                                    scalar=m.slopes[:, bass.ds(HPG * g + h, 1)], in1=m.PS[:, h, :],
                                    op0=ALU.mult, op1=ALU.add).then_inc(s_free, 1)
                            dve.wait_ge(s_free, NS * g + 2 * pair + 4)
                            link(nc.vector.tensor_reduce(m.MX[:, pair, :], t, AX.X, ALU.max))
                            nc.vector.tensor_tensor(t, t, over_positions(m.MX[:, pair, :]),
                                                    ALU.subtract).then_inc(c_sub, 1)
                            stack_low(HPG + pair)
                        if pair >= 1:
                            k = pair - 1
                            t = m.T[:, k, :].rearrange("p (t n) -> p t n", n=NCP)
                            den = m.DEN[:, k, :]
                            first = den.rearrange("p (h t) -> p h t", h=2)[:, :, 0:1]
                            dve.wait_ge(c_exp, HPG // 2 * g + pair)
                            link(nc.vector.tensor_reduce(den, t, AX.X, ALU.add))
                            link(nc.vector.reciprocal(den, den))
                            link(nc.vector.tensor_tensor(first, first, m.SOME[:, 0:2].unsqueeze(2), ALU.mult))
                            link(nc.vector.tensor_tensor(t, t, over_positions(den), ALU.mult))
                            for i in range(2):
                                late = t[:, i * QT + QT // 2:(i + 1) * QT, :]
                                if pair == 1 and i == 0:
                                    link(nc.vector.tensor_copy(m.PG[:], late))
                                else:
                                    link(nc.vector.tensor_tensor(m.PG[:], m.PG[:], late, ALU.add))
                            for i in range(2):
                                ti = t[:, i * QT:(i + 1) * QT, :]
                                nc.vector.tensor_tensor(
                                    ti, ti, m.gates[:, :, bass.ds(HPG * g + 2 * k + i, 1)].broadcast_to([P, QT, NCP]),
                                    ALU.mult).then_inc(c_p, 1)

                    v = m.PG[:].rearrange("p t (j r) -> p t j r", r=4)
                    imp = m.IMP[:]
                    link(nc.vector.tensor_tensor(imp, v[:, :, :, 0], v[:, :, :, 1], ALU.add))
                    link(nc.vector.tensor_tensor(imp, imp, v[:, :, :, 2], ALU.add))
                    link(nc.vector.scalar_tensor_tensor(out=imp, in0=imp, scalar=2.0, in1=v[:, :, :, 3],
                                                        op0=ALU.mult, op1=ALU.add))
                    link(nc.vector.tensor_tensor(imp[:, :, 1:], imp[:, :, 1:], v[:, :, 0:NBLK - 1, 3], ALU.add))
                    link(nc.vector.tensor_tensor(imp, imp, m.FORCED[:], ALU.add))
                    def rank(q):
                        ii = imp[:, q, :].unsqueeze(1).broadcast_to([P, NBLK, NBLK])
                        jj = imp[:, q, :].unsqueeze(2).broadcast_to([P, NBLK, NBLK])
                        nc.vector.tensor_tensor(m.LARGER[:], ii, jj, ALU.is_gt)
                        link(nc.vector.tensor_tensor(m.EQUAL[:], ii, jj, ALU.is_equal))
                        link(nc.vector.tensor_tensor(m.EQUAL[:], m.EQUAL[:], m.LOWER[:], ALU.mult))
                        link(nc.vector.tensor_tensor(m.LARGER[:], m.LARGER[:], m.EQUAL[:], ALU.add))
                        link(nc.vector.tensor_reduce(m.RANK[:, q, :], m.LARGER[:], AX.X, ALU.add))
                        if q == QT // 2 - 1:
                            nc.vector.tensor_scalar(m.RANK[:], m.RANK[:], float(N_SEL), -BIG, ALU.is_ge,
                                                    ALU.mult).then_inc(mk, 1)

                    nc.vector.tensor_copy(m.VSG[:], m.VS[:, :, bass.ds(HD * g, HD)])
                    nc.vector.tensor_copy(m.VWG[:], m.VW[:, :, bass.ds(HD * g, HD)])
                    for half in range(2):
                        r = slice(HD * half, HD * half + HD)
                        ins = nc.vector.tensor_copy(m.VCG[r, half, :], m.VC[r, bass.ds(g, 1), :].rearrange("p a d -> p (a d)"))
                    ins.then_inc(v_r, 1)

                    def bias_and_max(u):
                        h, q, b = UNITS[u]
                        a, e = unit_tiles(u)
                        n = (e - a) * P
                        bias = m.BW[:, h % 2, WIN + P - n:] if b else m.BS[:, h % 2, SEQ - n:]
                        if u % UPH == 0:
                            dve.wait_ge(b_w, HPG * g + h + 1)
                        dve.wait_ge(s_ready, NS * g + HPG + u + 1)
                        if u >= TS:
                            dve.wait_ge(pt_t, NCH * g + FIRST_CHUNK[u - TS + 1])
                        else:
                            dve.wait_ge(pt_t, NCH * g + HPG)
                        dve.sem_inc(begun, 1)
                        nc.vector.tensor_tensor_reduce(m.T[:, u % TS, 0:n], strip_psum(m, u % 2)[:, 0:n], bias, -1.0,
                                                       3e38, ALU.add, ALU.min, m.NM[:, u % TS:u % TS + 1]
                                                       ).then_inc(s_free, 1)

                    def scale(u):
                        h, q, b = UNITS[u]
                        a, e = unit_tiles(u)
                        t = m.T[:, u % TS, 0:(e - a) * P]
                        rec = m.REC[:, u % TS:u % TS + 1]
                        dve.wait_ge(p_r, NU * g + u + 1)
                        link(nc.vector.reciprocal(rec, m.SUM[:, u % TS:u % TS + 1]))
                        nc.vector.tensor_scalar(t, t, rec, m.gates[:, q, bass.ds(HEADS * (b + 1) + h + HPG * g, 1)],
                                                ALU.mult, ALU.mult).then_inc(scaled, 1)

                    def drain(h, half):
                        dve.wait_ge(pv, NB * g + BPH * h + BPH // 2 * (half + 1) + 2)
                        nc.vector.tensor_copy(
                            m.proj[HD * (h % 2):HD * (h % 2) + HD, bass.ds(2 * g + h // 2, 1),
                                   half * HALF:half * HALF + HALF].rearrange("p a n -> p (a n)"),
                            m.PS[0:HD, 6 + half, :]).then_inc(drained, 1)

                    for v in range(NU + 2):
                        if v >= 2:
                            scale(v - 2)
                        if v < NU:
                            bias_and_max(v)
                        if 1 <= v <= QT // 2:
                            rank(v - 1)
                        if v >= UPH // 2 + 5 and (v - 5) % (UPH // 2) == 0:
                            n = (v - 5) // (UPH // 2) - 1
                            drain(n // 2, n % 2)
                    drain(HPG - 1, 1)
                    assert links == CHAIN, links

        @block.tensor
        def _(pe):
            pe.sem_inc(pv, 2)
            pe.wait_ge(ind_r, 1)
            with pe.Fori(0, GROUPS // 2) as j:
                for gi in range(2):
                    g = 2 * j + gi

                    def comp_scores(h):
                        pe.wait_ge(st_l, (2 + HPG) * g + 1 + h)
                        pe.wait_ge(s_free, NS * g + 2)
                        for q in range(QT):
                            out = m.PS[:, h, q * NCP:(q + 1) * NCP]
                            nc.tensor.matmul(out, m.Q1[:, h, q * P:(q + 1) * P], m.KC1G[:], start=True, stop=False)
                            last = nc.tensor.matmul(out, m.Q1[0:HD, h, q * P:(q + 1) * P],
                                                    m.KC2G[0:HD, :],
                                                    start=False, stop=True)
                        last.then_inc(s_ready, 1)

                    def turn_comp(h):
                        pe.wait_ge(c_p, HPG * g + h + 1)
                        pe.wait_ge(kept, NCH * g + h + 1)
                        for k in range(4):
                            last = nc.tensor.transpose(ptslot(h)[:, k * P:(k + 1) * P], m.T[:, h // 2, (h % 2) * HALF + k * P:(h % 2) * HALF + (k + 1) * P],
                                                       m.ident[:])
                        last.then_inc(pt_t, 1)

                    def scores(u):
                        h, q, b = UNITS[u]
                        a, e = unit_tiles(u)
                        if u == 0:
                            pe.wait_ge(st_c, (2 + HPG) * (g + 1))
                        if u == MASKED_FROM:
                            pe.wait_ge(q2m, HPG * g + HPG)
                        pe.wait_ge(s_free, NS * g + HPG + u + 1)
                        k1, k2 = (m.KW1, m.KW2) if b else (m.KS1, m.KS2)
                        rows, q2 = (HD, m.Q1[0:HD, h, q * P:(q + 1) * P])
                        if not b and q >= QT // 2:
                            rows, q2 = HD + NBLK, m.Q2[0:HD + NBLK, h, (q - QT // 2) * P:(q - QT // 2 + 1) * P]
                        spans = [(n, min(n + HALF, e * P)) for n in range(a * P, e * P, HALF)]
                        for n, end in spans:
                            nc.tensor.matmul(strip_psum(m, u % 2)[:, n - a * P:end - a * P],
                                             m.Q1[:, h, q * P:(q + 1) * P], k1[:, n:end], start=True, stop=False)
                        for n, end in spans:
                            last = nc.tensor.matmul(strip_psum(m, u % 2)[:, n - a * P:end - a * P],
                                                    q2, k2[0:rows, n:end], start=False, stop=True)
                        last.then_inc(s_ready, 1)

                    def turn(u, k):
                        a, e = unit_tiles(u)
                        c = FIRST_CHUNK[u] + k
                        t0, t1 = CHUNKS[u][k]
                        pe.wait_ge(kept, NCH * g + c + 1)
                        for t in range(t0, t1):
                            last = nc.tensor.transpose(ptslot(c)[:, (t - t0) * P:(t - t0 + 1) * P],
                                                       m.T[:, u % TS, (t - a) * P:(t - a + 1) * P], m.ident[:])
                        last.then_inc(pt_t, 1)

                    def block_products(n):
                        h, q, b = UNITS[2 * n]
                        bank = m.PS[0:HD, 6 + q // 4, :]
                        if n % (BPH // 2) == 0:
                            half = q // 4
                            both = bank.rearrange("p (k a n) -> p a k n", k=2, a=2)
                            ptc = m.PTC[:, h, half * 2 * P:(half + 1) * 2 * P].rearrange("p (k n) -> p k n", k=2)
                            for par in range(2):
                                yield both[:, par], m.VCG[:, par, :], ptc, par == 0, False
                        col = (q % 4) * P
                        v = m.VWG if b else m.VSG
                        first = [unit_tiles(2 * n + p)[0] for p in range(2)]
                        for t in range(first[0], q + 2):
                            lo = P if t > q else 0
                            hi = P if t < first[1] else 2 * P
                            yield (bank[:, col + lo:col + hi], v[:, t, :],
                                   m.PT[:, n % 2, t, lo:hi], False,
                                   n % (BPH // 2) == BPH // 2 - 1 and t == q + 1)

                    for h in range(HPG):
                        comp_scores(h)
                    for h in range(HPG):
                        turn_comp(h)
                    def turn_mask():
                        pe.wait_ge(mk, g + 1)
                        pe.wait_ge(drained, 2 * HPG * g + 2)
                        for q in range(QT // 2):
                            last = nc.tensor.transpose(m.PS[0:NBLK, 7, q * P:(q + 1) * P], m.RANK[:, q, :], m.ident[:])
                        last.then_inc(mk_t, 1)

                    def products(n, items, last_of_block):
                        for out, lhs, rhs, start, stop in items:
                            last = nc.tensor.matmul(out, lhs, rhs, start=start, stop=stop)
                        if last_of_block:
                            last.then_inc(pv, 1)

                    def begin_block(n):
                        if n == 0:
                            pe.wait_ge(v_r, g + 1)
                        if n % (BPH // 2) == 0:
                            pe.wait_ge(drained, 2 * HPG * g + 2 * (n // BPH) + (n // (BPH // 2)) % 2 + 1)
                        pe.wait_ge(kept, NCH * g + FIRST_CHUNK[2 * n + 2] + 2)
                        return list(block_products(n))

                    for v in range(NU + 3):
                        if v < NU:
                            scores(v)
                        if v == MASK_AT:
                            turn_mask()
                        if v >= 3:
                            u = v - 3
                            pe.wait_ge(scaled, NU * g + u + 1)
                            n = u // 2
                            slots = len(CHUNKS[2 * n]) + len(CHUNKS[2 * n + 1])
                            for k in range(len(CHUNKS[u])):
                                turn(u, k)
                                if n:
                                    if u % 2 == 0 and k == 0:
                                        todo, used = begin_block(n - 1), 0
                                    i = k + (u % 2) * len(CHUNKS[2 * n])
                                    upto = len(todo) * (i + 1) // slots
                                    if upto > used:
                                        products(n - 1, todo[used:upto], upto == len(todo))
                                    used = upto
                    products(NB - 1, begin_block(NB - 1), True)


SB_UNITS = [(h, q) for h in range(2) for q in range(QT)]
SB_NU = len(SB_UNITS)
SB_ITEMS = [(h, q, t) for h in range(2) for q in range(0, QT, 2) for t in ((4, 0) if q >= QT // 2 else (4,))]
SB_NI = len(SB_ITEMS)


def sb_chunk_table():
    out = []
    for h, q in SB_UNITS:
        mine = [n for n, it in enumerate(SB_ITEMS) if it[0] == h and it[1] == q - q % 2]
        out.append([(n, max(SB_ITEMS[n][2], QT - 1 - q), SB_ITEMS[n][2] + 4) for n in mine])
    return out


SB_CHUNKS = sb_chunk_table()
SB_FIRST = [2 + sum(len(c) for c in SB_CHUNKS[:u]) for u in range(SB_NU + 1)]
SB_NCH = SB_FIRST[-1]
SB_LAST = {item: SB_FIRST[u] + k for u in range(SB_NU) for k, (item, _, _) in enumerate(SB_CHUNKS[u])}
SB_SLOTS = 4
SB_AHEAD = 3
SB_ON_DVE = [False, False] + [k == 1 for u in range(SB_NU) for k in range(len(SB_CHUNKS[u]))]
SB_KEPT = {engine: sum(d == engine for d in SB_ON_DVE) for engine in (False, True)}
assert SB_NCH % 2 == 0 and SB_NI % 2 == 0


def stick_breaking(nc, m, norm, w_in, h_store):
    t = SEQ * 4
    o = m.big + 8 * t
    q1 = m.at("sq1", o, [P, 2, SEQ], F32R); o += 2 * t
    k1 = m.at("sk1", o, [P, 2, SEQ], F32R); o += 2 * t
    klo = m.at("sklo", o, [P, SEQ], F32R); o += t
    vtok = m.at("svtok", o, [P, QT, P]); o += t
    beta = m.at("sbeta", m.base, [P, SB_SLOTS, SEQ])
    keep = m.at("skeep", m.base + SB_SLOTS * t, [P, 2, SEQ])
    vfeat = m.at("svfeat", m.base + (SB_SLOTS + 2) * t, [P, SEQ])
    pt = m.at("spt", o, [P, 2, 4, 2 * P]); o += 2 * t
    assert o <= m.small
    prod = m.at("sprod", m.gates_at, [P, SEQ + 8])
    assert m.gates_at + t + 32 <= 229368
    st = Strips(nc, m, "s")
    hi, qkv, vst, z_r, kp_r, kp_s, z_free, b_s, scn, a_r, pt_t, kept_a, kept_d, pv, drained, one, begun, spilled = sems(
        nc, "s", "stackhigh", "stacklow", "vstaged", "zready", "keepready", "keepselected", "zfree", "betaselected",
        "scanned", "aready", "turned", "keptact", "keptdve", "values", "outdrained", "one", "begun",
        "spilled")
    PAIRS = HEADS // 2

    def ptslot(c):
        return m.PS[:, 4 + c % 2, :]

    def own(h):
        return slice(HD * h, HD * h + HD)

    def other(h):
        return slice(HD - HD * h, 2 * HD - HD * h)

    def keep_chunk(engine, copy, done, j, u, k):
        item, t0, t1 = SB_CHUNKS[u][k]
        engine.wait_ge(pt_t, SB_NCH * j + SB_FIRST[u] + k + 1)
        engine.wait_ge(pv, SB_NI * j + item + 1)
        copy(pt[:, item % 2, t0 % 4:4, (u % 2) * P:(u % 2) * P + P],
             ptslot(SB_FIRST[u] + k)[:, 0:(t1 - t0) * P].rearrange("p (t n) -> p t n", n=P)).then_inc(done, 1)

    with nc.Block() as block:
        @block.sync
        def _(sp):
            with sp.Fori(0, PAIRS) as j:
                for n, slot in enumerate((0, 1, 0)):
                    sp.wait_ge(st.low, 3 * j + (2, 1, 3)[n])
                    sp.dma_start(m.W32[:, slot], strip_of(w_in, j + n * PAIRS)).then_inc(st.loaded[slot], 16)

        @block.scalar
        def _(act):
            def split(j, n):
                slot = n % 2
                act.wait_ge(st.loaded[slot], 16 * (j + 1) if slot else 16 * (2 * j + n // 2 + 1))
                act.wait_ge(st.multiplied, 3 * j + (2, 1, 3)[n])
                nc.scalar.copy(m.WHI[:, slot], m.W32[:, slot]).then_inc(st.high, 1)

            def stack_high(j, n):
                act.wait_ge(st.multiplied, 3 * j + n + 3)
                for h in range(2):
                    dst = q1[own(h), h, :] if n == 0 else k1[own(h), h, ::-1]
                    nc.scalar.activation(dst, strip_psum(m, n)[own(h)], ACT.Copy,
                                         scale=QSCALE if n == 0 else 1.0).then_inc(hi, 1)

            def unit_scores(u):
                n = (SB_UNITS[u][1] + 1) * P
                return n, strip_psum(m, (u + 1) % 2)[:, 0:n]

            def keep_factors(j, u):
                n, z = unit_scores(u)
                act.wait_ge(z_r, SB_NU * j + u + 1)
                act.wait_ge(scn, SB_NU * j + u + 1)
                nc.scalar.activation(keep[:, u % 2, 0:n], z, ACT.Sigmoid, scale=-1.0).then_inc(kp_r, 1)

            def betas(j, u):
                n, z = unit_scores(u)
                if u >= SB_SLOTS:
                    act.wait_ge(pt_t, SB_NCH * j + SB_FIRST[u - SB_SLOTS + 1])
                nc.scalar.activation(beta[:, u % SB_SLOTS, 0:n], z, ACT.Sigmoid).then_inc(z_free, 1)

            def pair(j, last):
                split(j, 2)
                stack_high(j, 1)
                act.wait_ge(hi, 4 * j + 4)
                for h in range(2):
                    ins = nc.scalar.copy(k1[other(h), h, :], k1[own(h), h, :].bitcast(F32))
                ins.then_inc(vst, 1)
                keep_factors(j, 0)
                betas(j, 0)
                act.wait_ge(st.multiplied, 3 * j + 5)
                nc.scalar.copy(vfeat[:, ::-1], strip_psum(m, 0)).then_inc(vst, 1)
                keep_factors(j, 1)
                betas(j, 1)
                for c in range(2):
                    act.wait_ge(pt_t, SB_NCH * j + c + 1)
                    nc.scalar.copy(vtok[:, 4 * c:4 * c + 4, :].rearrange("p t d -> p (t d)"), ptslot(c)).then_inc(kept_a, 1)
                for v in range(2, SB_NU + SB_AHEAD):
                    if v < SB_NU:
                        keep_factors(j, v)
                    if v >= SB_AHEAD:
                        keep_chunk(act, nc.scalar.copy, kept_a, j, v - SB_AHEAD, 0)
                    if v < SB_NU:
                        betas(j, v)
                    if v == SB_NU - 4 and not last:
                        for n in range(2):
                            split(j + 1, n)
                    if v == SB_NU + SB_AHEAD - 1 and not last:
                        stack_high(j + 1, 0)

            act.sem_inc(kept_a, 1)
            norm.root(act)
            for k in range(0, KT, 2):
                act.dma_start(h_store[:, k:k + 2, :], m.H[:, k:k + 2, :]).then_inc(spilled, 16)
            norm.high_parts(act, lambda n: split(0, n))
            stack_high(0, 0)
            act.wait_ge(spilled, 16 * KT // 2)
            with act.Fori(0, PAIRS - 1) as j:
                pair(j, False)
            pair(PAIRS - 1, True)

        @block.gpsimd
        def _(pool):
            def select(x, fill, done):
                pool.sem_inc(begun, 1)
                nc.gpsimd.affine_select(out=x, in_=x, compare_op=ALU.is_gt, fill=fill, base=1 - P,
                                        pattern=[[1, P]], channel_multiplier=1).then_inc(done, 1)

            with pool.Fori(0, PAIRS) as j:
                for u in range(SB_NU):
                    pool.wait_ge(kp_r, SB_NU * j + u + 1)
                    select(keep[:, u % 2, 0:P], 1.0, kp_s)
                    pool.wait_ge(z_free, SB_NU * j + u + 1)
                    select(beta[:, u % SB_SLOTS, 0:P], 0.0, b_s)

        @block.vector
        def _(dve):
            def split(j, n):
                dve.wait_ge(st.high, 3 * j + n + 1)
                nc.vector.tensor_tensor(m.WLO[:, n % 2], m.W32[:, n % 2], m.WHI[:, n % 2].bitcast(F32),
                                        ALU.subtract).then_inc(st.low, 1)

            def stack_low(j, n):
                for h in range(2):
                    dve.wait_ge(hi, 4 * j + 2 * n + h + 1)
                    src = strip_psum(m, n)[own(h)]
                    if n == 0:
                        ins = nc.vector.scalar_tensor_tensor(
                            out=q1[other(h), h, :], in0=src, scalar=QSCALE, in1=q1[own(h), h, :].bitcast(F32),
                            op0=ALU.mult, op1=ALU.subtract)
                    else:
                        ins = nc.vector.tensor_tensor(klo[own(h), ::-1], src, k1[own(h), h, ::-1].bitcast(F32),
                                                      ALU.subtract)
                ins.then_inc(qkv, 1)

            def drain(j, h, half):
                dve.wait_ge(pv, SB_NI * j + SB_NI // 2 * h + (4 * half + 2) + 2)
                nc.vector.tensor_copy(row(m.proj, j)[own(h), half * HALF:half * HALF + HALF],
                                      m.PS[0:HD, 6 + half, :]).then_inc(drained, 1)

            def pair(j, last):
                split(j, 2)
                stack_low(j, 1)
                for u in range(SB_NU + SB_AHEAD):
                    turned = u - SB_AHEAD
                    if u >= SB_NU:
                        if len(SB_CHUNKS[turned]) == 2:
                            keep_chunk(dve, nc.vector.tensor_copy, kept_d, j, turned, 1)
                        if u == SB_NU + SB_AHEAD - 1 and not last:
                            stack_low(j + 1, 0)
                        continue
                    h, q = SB_UNITS[u]
                    n = (q + 1) * P
                    b = beta[:, u % SB_SLOTS, 0:n]
                    if turned >= 0 and len(SB_CHUNKS[turned]) == 2:
                        keep_chunk(dve, nc.vector.tensor_copy, kept_d, j, turned, 1)
                    dve.wait_ge(kp_s, SB_NU * j + u + 1)
                    if u:
                        dve.wait_ge(a_r, SB_NU * j + u)
                    nc.vector.tensor_tensor_scan(prod[:, 1:n + 1], keep[:, u % 2, 0:n], keep[:, u % 2, 0:n], 1.0,
                                                 ALU.mult, ALU.bypass).then_inc(scn, 1)
                    dve.wait_ge(scn, SB_NU * j + u + 3)
                    dve.wait_ge(b_s, SB_NU * j + u + 1)
                    nc.vector.tensor_tensor(b, b, prod[:, 0:n], ALU.mult).then_inc(a_r, 1)
                    if u in (7, 11, 15):
                        drain(j, *((0, 0), (0, 1), (1, 0))[(u - 7) // 4])
                    if u == SB_NU - 4 and not last:
                        for n in range(2):
                            split(j + 1, n)
                drain(j, 1, 1)

            nc.vector.memset(prod[:, 0:1], 1.0).then_inc(one, 1)
            dve.wait_ge(one, 1)
            dve.sem_inc(st.low, 2)
            dve.sem_inc(scn, 2)
            dve.sem_inc(kept_d, 1)
            dve.sem_inc(drained, 2)
            norm.scale_and_low_parts(dve, lambda n: split(0, n))
            stack_low(0, 0)
            with dve.Fori(0, PAIRS - 1) as j:
                pair(j, False)
            pair(PAIRS - 1, True)

        @block.tensor
        def _(pe):
            def strip(j, n, at=KT, between=None):
                pe.wait_ge(st.low, 3 * j + n + 3)
                slot = n % 2
                for k in range(KT):
                    if k == at:
                        between()
                    last = strip_tile_products(nc, strip_psum(m, slot), m.WHI[:, slot], m.WLO[:, slot],
                                               m.XH, m.XL, k, KT)
                last.then_inc(st.multiplied, 1)

            def scores(j, u):
                h, q = SB_UNITS[u]
                if u == 0:
                    pe.wait_ge(qkv, 2 * j + 2)
                    pe.wait_ge(vst, 2 * j + 1)
                elif u == 1:
                    pe.wait_ge(vst, 2 * j + 2)
                else:
                    pe.wait_ge(z_free, SB_NU * j + u - 1)
                first = SEQ - (q + 1) * P
                spans = [(n, min(n + HALF, SEQ)) for n in range(first, SEQ, HALF)]
                for n, end in spans:
                    nc.tensor.matmul(strip_psum(m, (u + 1) % 2)[:, n - first:end - first],
                                     q1[:, h, q * P:(q + 1) * P], k1[:, h, n:end], start=True, stop=False)
                for n, end in spans:
                    last = nc.tensor.matmul(strip_psum(m, (u + 1) % 2)[:, n - first:end - first],
                                            q1[own(h), h, q * P:(q + 1) * P], klo[own(h), n:end],
                                            start=False, stop=True)
                last.then_inc(z_r, 1)

            def wait_kept(j, c):
                on_dve = SB_ON_DVE[c]
                count = sum(d == on_dve for d in SB_ON_DVE[:c + 1]) if c >= 0 else 0
                pe.wait_ge(kept_d if on_dve else kept_a, SB_KEPT[on_dve] * j + count + 1)

            def turn(j, c, tiles):
                wait_kept(j, c - 2)
                for n, x in enumerate(tiles):
                    last = nc.tensor.transpose(ptslot(c)[:, n * P:(n + 1) * P], x, m.ident[:])
                last.then_inc(pt_t, 1)

            def item_chunks(item):
                return sorted(SB_FIRST[u] + k for u in range(SB_NU) for k, c in enumerate(SB_CHUNKS[u]) if c[0] == item)[-1:]

            def products(j, item):
                h, q, first = SB_ITEMS[item]
                starts = q % 4 == 0 and first == 4
                if starts:
                    pe.wait_ge(drained, 4 * j + 2 * h + q // 4 + 1)
                for c in item_chunks(item):
                    wait_kept(j, c)
                tiles = [t for t in range(first, first + 4) if t >= QT - 2 - q]
                tiles.sort(key=lambda t: t < QT - 1 - q)
                col = (q % 4) * P
                for t in tiles:
                    lo = P if t < QT - 1 - q else 0
                    last = nc.tensor.matmul(m.PS[0:HD, 6 + q // 4, col + lo:col + 2 * P], vtok[:, t, own(h)],
                                            pt[:, item % 2, t % 4, lo:2 * P], start=starts and t == tiles[0],
                                            stop=q % 4 == 2 and (item + 1 == SB_NI or SB_ITEMS[item + 1][1] != q)
                                            and t == tiles[-1])
                last.then_inc(pv, 1)

            def pair(j, last):
                pe.wait_ge(qkv, 2 * j + 1)
                strip(j, 2, KT // 2, lambda: scores(j, 0))
                scores(j, 1)
                for c in range(2):
                    turn(j, c, [vfeat[:, t * P:(t + 1) * P] for t in range(4 * c, 4 * c + 4)])
                waiting = []
                for v in range(2, SB_NU + SB_AHEAD):
                    if v < SB_NU:
                        scores(j, v)
                    if v >= SB_AHEAD:
                        u = v - SB_AHEAD
                        pe.wait_ge(a_r, SB_NU * j + u + 1)
                        start = SB_CHUNKS[u][0][1] if len(SB_CHUNKS[u]) == 1 else SB_CHUNKS[u][1][1]
                        for k, (item, t0, t1) in enumerate(SB_CHUNKS[u]):
                            c = SB_FIRST[u] + k
                            turn(j, c, [beta[:, u % SB_SLOTS, (t - start) * P:(t - start + 1) * P] for t in range(t0, t1)])
                            while waiting:
                                products(j, waiting.pop(0))
                            if c == SB_LAST[item]:
                                waiting.append(item)
                    if v == SB_NU and not last:
                        pe.wait_ge(z_free, SB_NU * j + SB_NU)
                        strip(j + 1, 0)
                if last:
                    products(j, waiting.pop())
                else:
                    strip(j + 1, 1, 2, lambda: products(j, waiting.pop()))
                assert not waiting

            pe.sem_inc(st.multiplied, 2)
            pe.sem_inc(pv, 2)
            first_pair(nc, m, st, pe, norm.yl)
            with pe.Fori(0, PAIRS - 1) as j:
                pair(j, False)
            pair(PAIRS - 1, True)


def strips(w):
    r, c = w.shape
    return np.ascontiguousarray(w.reshape(r // P, P, c // P, P).transpose(2, 1, 0, 3))


def features_first(a):
    return np.ascontiguousarray(a.T.reshape(KT, P, SEQ).transpose(1, 0, 2))


def build_trunk(nc, x, gains, nsa_in, nsa_gate, gate_b, cmp_w1, cmp_w2, cmp_pe, nsa_out, sb_in, sb_out,
                w1, w3, w2, out):
    m = Memory(nc)
    nsa_memory(m)
    norms = [Norm(nc, m, 0, scratch=10, slots=2)] + [Norm(nc, m, n) for n in range(1, 5)]
    load_input(nc, m, x, gains, norms[0])
    nsa_projection(nc, m, norms[0], nsa_in, nsa_gate, gate_b)
    used = nsa_compress(nc, m, cmp_w1, cmp_w2, cmp_pe)
    nc.clear_and_free_semaphores(used)
    nc.all_engine_barrier()
    nsa_attention(nc, m)
    residual_projection(nc, m, "no", nsa_out, norms[1])
    ffn(nc, m, 0, w1[0], w3[0], w2[0], norms[1], norms[2])
    h_store = nc.dram_tensor("h_store", (P, KT, SEQ), F32, kind="Internal").ap()
    stick_breaking(nc, m, norms[2], sb_in, h_store)
    residual_projection(nc, m, "so", sb_out, norms[3], h_store)
    ffn(nc, m, 1, w1[1], w3[1], w2[1], norms[3], norms[4])
    store_normalised(nc, m, norms[4], out)


def kernel(x, mix_norm_g, ffn_norm_g, final_norm_g, nsa_w_in, nsa_gate_b, nsa_cmp_pe, nsa_cmp_w1, nsa_cmp_w2,
           nsa_w_out, sb_w_in, sb_w_out, ffn_w1, ffn_w3, ffn_w2):
    import concourse.bacc as bacc
    from concourse.bass_utils import run_bass_kernel_spmd

    mix, ffn, final, w_in = (np.asarray(a) for a in (mix_norm_g, ffn_norm_g, final_norm_g, nsa_w_in))
    qkv = NSA_TILES * P
    cuts = np.cumsum([0, D] + 6 * [KVW])
    order = np.concatenate([np.arange(cuts[n], cuts[n + 1]) for n in (0, 1, 2, 3, 5, 4, 6)])
    gains = np.stack([mix[0], ffn[0], mix[1], ffn[1], final])
    arrays = {
        "x": features_first(np.asarray(x)[0]),
        "gains": np.ascontiguousarray(gains.reshape(5, KT, P).transpose(2, 0, 1)),
        "nsa_in": strips(w_in[0][:, order]),
        "nsa_gate": np.ascontiguousarray(w_in[0][:, qkv:].reshape(KT, P, -1).transpose(1, 0, 2)),
        "gate_b": np.ascontiguousarray(np.asarray(nsa_gate_b)[0]),
        "cmp_w1": np.ascontiguousarray(np.asarray(nsa_cmp_w1)[0].reshape(2, 2 * KT, P, HID).transpose(2, 0, 1, 3)),
        "cmp_w2": np.ascontiguousarray(np.asarray(nsa_cmp_w2)[0].reshape(2, 2, P, HD).transpose(2, 0, 1, 3)),
        "cmp_pe": np.ascontiguousarray(np.asarray(nsa_cmp_pe)[0].reshape(2, 2 * KT, P).transpose(2, 0, 1)),
        "nsa_out": strips(np.asarray(nsa_w_out)[0]),
        "sb_in": strips(np.asarray(sb_w_in)[0]),
        "sb_out": strips(np.asarray(sb_w_out)[0]),
        "w1": np.stack([strips(w) for w in np.asarray(ffn_w1)]),
        "w3": np.stack([strips(w) for w in np.asarray(ffn_w3)]),
        "w2": np.stack([strips(w) for w in np.asarray(ffn_w2)]),
    }
    nc = bacc.Bacc("TRN2", target_bir_lowering=False, num_devices=1)
    args = {n: nc.dram_tensor(n, a.shape, mybir.dt.from_np(a.dtype), kind="ExternalInput").ap()
            for n, a in arrays.items()}
    out = nc.dram_tensor("out", (P, KT, SEQ), F32, kind="ExternalOutput").ap()
    build_trunk(nc, out=out, **args)
    r = run_bass_kernel_spmd(nc, [arrays], core_ids=[0])
    got = r.results[0]["out"]
    return np.ascontiguousarray(got.transpose(2, 1, 0)).reshape(1, SEQ, D)
```
